# Optimizing a Trainium2 kernel written in Bass

```python
import math
import jax, jax.numpy as jnp
from jax import lax
import numpy as np

D_MODEL = 1024
BATCH = 1
SEQ = 1024
DEPTH = 1

MEM_LEN = 256
C_CONV = D_MODEL
CONV_WIDTH = 31
SB_HEADS = 16
SB_HEAD_DIM = D_MODEL // SB_HEADS
D_ATT = SB_HEADS * SB_HEAD_DIM
N_BRANCHES = 2
D_IN = 2 * C_CONV + 3 * D_ATT + N_BRANCHES * D_MODEL
Q_BLOCK = 128
XA_HEADS = 4
XA_HEAD_DIM = D_MODEL // XA_HEADS
PEER_HEADS = 8
PEER_KEYS = 128
PEER_EXPERTS = PEER_KEYS * PEER_KEYS
PEER_QDIM = 256
PEER_HALF = PEER_QDIM // 2
PEER_TOPK = 16
TOK_BLOCK = 128
EPS = 1e-6

kernel_name = "hybrid_conv_stickbreak_peer_block"

def rms_norm(x, g):
    xf = x.astype(jnp.float32)
    xf = xf * lax.rsqrt(jnp.mean(xf * xf, axis=-1, keepdims=True) + EPS)
    return (xf * g.astype(jnp.float32)).astype(x.dtype)

def layer_norm(x, g, b):
    xf = x.astype(jnp.float32)
    mu = jnp.mean(xf, axis=-1, keepdims=True)
    var = jnp.mean(jnp.square(xf - mu), axis=-1, keepdims=True)
    y = (xf - mu) * lax.rsqrt(var + EPS)
    return (y * g.astype(jnp.float32) + b.astype(jnp.float32)).astype(x.dtype)

def conformer_conv(glu_in, dw_w, dw_b, ln_g, ln_b, w_proj):
    a, gt = jnp.split(glu_in, 2, axis=-1)
    u = a * jax.nn.sigmoid(gt)
    y = lax.conv_general_dilated(
        u, dw_w[:, None, :], window_strides=(1,),
        padding=[(CONV_WIDTH - 1, 0)],
        dimension_numbers=('NWC', 'WIO', 'NWC'),
        feature_group_count=C_CONV) + dw_b
    y = jax.nn.silu(layer_norm(y, ln_g, ln_b))
    return y @ w_proj

def stick_breaking_attention(q, k, v):
    b, s, h, dh = q.shape
    n_blk = s // Q_BLOCK
    kt = k.transpose(0, 2, 1, 3)
    vt = v.transpose(0, 2, 1, 3)
    qb = q.reshape(b, n_blk, Q_BLOCK, h, dh).transpose(1, 0, 3, 2, 4)
    starts = jnp.arange(n_blk, dtype=jnp.int32) * Q_BLOCK
    key_pos = jnp.arange(s, dtype=jnp.int32)
    scale = 1.0 / math.sqrt(dh)

    def block(args):
        q_blk, t0 = args
        z = jnp.einsum('bhqd,bhkd->bhqk', q_blk, kt).astype(jnp.float32) * scale
        q_pos = t0 + jnp.arange(Q_BLOCK, dtype=jnp.int32)
        causal = key_pos[None, :] < q_pos[:, None]
        log_1m = jnp.where(causal, -jax.nn.softplus(z), 0.0)
        after = lax.cumsum(log_1m, axis=3, reverse=True) - log_1m
        w = jnp.where(causal, jnp.exp(jax.nn.log_sigmoid(z) + after), 0.0)
        return jnp.einsum('bhqk,bhkd->bhqd', w.astype(vt.dtype), vt)

    o = lax.map(block, (qb, starts))
    return o.transpose(1, 0, 3, 2, 4).reshape(b, s, h * dh)

def memory_cross_attention(h, m, w_xq, w_xkv, w_xo):
    b, s, _ = h.shape
    m_len = m.shape[1]
    q = (h @ w_xq).reshape(b, s, XA_HEADS, XA_HEAD_DIM)
    kv = (m @ w_xkv).reshape(b, m_len, 2, XA_HEADS, XA_HEAD_DIM)
    k, v = kv[:, :, 0], kv[:, :, 1]
    sc = jnp.einsum('bshd,bmhd->bhsm', q, k).astype(jnp.float32) / math.sqrt(XA_HEAD_DIM)
    p = jax.nn.softmax(sc, axis=-1).astype(v.dtype)
    o = jnp.einsum('bhsm,bmhd->bshd', p, v).reshape(b, s, D_MODEL)
    return o @ w_xo

def peer_ffn(h, w_pq, sub_keys, u_emb, v_emb):
    b, s, d = h.shape
    q = (h @ w_pq).reshape(b, s, PEER_HEADS, 2, PEER_HALF)
    sc = jnp.einsum('bshpc,pnc->bshpn', q, sub_keys).astype(jnp.float32)
    top_v, top_i = lax.top_k(sc, PEER_TOPK)
    cand = (top_v[..., 0, :, None] + top_v[..., 1, None, :]).reshape(
        b, s, PEER_HEADS, PEER_TOPK * PEER_TOPK)
    best_v, best_i = lax.top_k(cand, PEER_TOPK)
    i1 = jnp.take_along_axis(top_i[..., 0, :], best_i // PEER_TOPK, axis=-1)
    i2 = jnp.take_along_axis(top_i[..., 1, :], best_i % PEER_TOPK, axis=-1)
    expert = i1 * PEER_KEYS + i2
    gate = jax.nn.softmax(best_v, axis=-1)
    n_blk = s // TOK_BLOCK

    def to_blocks(a):
        return a.reshape(b, n_blk, TOK_BLOCK, *a.shape[2:]).swapaxes(0, 1)

    def block(args):
        h_blk, e_blk, g_blk = args
        u = u_emb[e_blk]
        a = jnp.einsum('bthkd,btd->bthk', u, h_blk).astype(jnp.float32)
        act = (jax.nn.gelu(a) * g_blk).astype(h_blk.dtype)
        return jnp.einsum('bthk,bthkd->btd', act, v_emb[e_blk])

    out = lax.map(block, (to_blocks(h), to_blocks(expert), to_blocks(gate)))
    return out.swapaxes(0, 1).reshape(b, s, d)

def setup_inputs(seed: int = 0) -> dict:
    key = jax.random.key(seed)
    ks = jax.random.split(key, 26)

    def nrm(k, shape, scale):
        return jax.random.normal(k, shape, jnp.float32) * scale

    def gain(k, shape):
        return 1.0 + 0.01 * jax.random.normal(k, shape, jnp.float32)

    L = DEPTH
    return {
        "x": nrm(ks[0], (BATCH, SEQ, D_MODEL), 1.0),
        "mem": nrm(ks[1], (BATCH, MEM_LEN, D_MODEL), 1.0),
        "norm_mix_g": gain(ks[2], (L, D_MODEL)),
        "w_in": nrm(ks[3], (L, D_MODEL, D_IN), D_MODEL ** -0.5),
        "b_gate": nrm(ks[4], (L, N_BRANCHES * D_MODEL), 0.1),
        "conv_dw_w": nrm(ks[5], (L, CONV_WIDTH, C_CONV), CONV_WIDTH ** -0.5),
        "conv_dw_b": nrm(ks[6], (L, C_CONV), 0.02),
        "conv_ln_g": gain(ks[7], (L, C_CONV)),
        "conv_ln_b": nrm(ks[8], (L, C_CONV), 0.02),
        "w_conv_out": nrm(ks[9], (L, C_CONV, D_MODEL), C_CONV ** -0.5),
        "w_attn_out": nrm(ks[10], (L, D_ATT, D_MODEL), D_ATT ** -0.5),
        "w_out": nrm(ks[11], (L, D_MODEL, D_MODEL), D_MODEL ** -0.5),
        "norm_xattn_g": gain(ks[12], (L, D_MODEL)),
        "norm_mem_g": gain(ks[13], (L, D_MODEL)),
        "w_xq": nrm(ks[14], (L, D_MODEL, D_MODEL), D_MODEL ** -0.5),
        "w_xkv": nrm(ks[15], (L, D_MODEL, 2 * D_MODEL), D_MODEL ** -0.5),
        "w_xo": nrm(ks[16], (L, D_MODEL, D_MODEL), D_MODEL ** -0.5),
        "norm_ffn_g": gain(ks[17], (L, D_MODEL)),
        "w_peer_q": nrm(ks[18], (L, D_MODEL, PEER_HEADS * PEER_QDIM), D_MODEL ** -0.5),
        "peer_sub_keys": nrm(ks[19], (L, 2, PEER_KEYS, PEER_HALF), PEER_HALF ** -0.5),
        "peer_u": nrm(ks[20], (L, PEER_EXPERTS, D_MODEL), D_MODEL ** -0.5),
        "peer_v": nrm(ks[21], (L, PEER_EXPERTS, D_MODEL), PEER_HEADS ** -0.5),
        "norm_final_g": gain(ks[22], (D_MODEL,)),
    }

def reference(x, mem, norm_mix_g, w_in, b_gate, conv_dw_w, conv_dw_b, conv_ln_g, conv_ln_b,
              w_conv_out, w_attn_out, w_out, norm_xattn_g, norm_mem_g, w_xq, w_xkv, w_xo,
              norm_ffn_g, w_peer_q, peer_sub_keys, peer_u, peer_v, norm_final_g):
    b, s, _ = x.shape
    splits = [2 * C_CONV, 2 * C_CONV + D_ATT, 2 * C_CONV + 2 * D_ATT, 2 * C_CONV + 3 * D_ATT]
    for l in range(DEPTH):
        h = rms_norm(x, norm_mix_g[l])
        proj = h @ w_in[l]
        conv_in, q, k, v, gate_logits = jnp.split(proj, splits, axis=-1)
        gates = jax.nn.sigmoid(gate_logits + b_gate[l])
        g_conv, g_attn = jnp.split(gates, 2, axis=-1)
        conv_out = conformer_conv(conv_in, conv_dw_w[l], conv_dw_b[l],
                                  conv_ln_g[l], conv_ln_b[l], w_conv_out[l])
        attn = stick_breaking_attention(q.reshape(b, s, SB_HEADS, SB_HEAD_DIM),
                                        k.reshape(b, s, SB_HEADS, SB_HEAD_DIM),
                                        v.reshape(b, s, SB_HEADS, SB_HEAD_DIM))
        attn_out = attn @ w_attn_out[l]
        x = x + (g_conv * conv_out + g_attn * attn_out) @ w_out[l]
        h = rms_norm(x, norm_xattn_g[l])
        m = rms_norm(mem, norm_mem_g[l])
        x = x + memory_cross_attention(h, m, w_xq[l], w_xkv[l], w_xo[l])
        h = rms_norm(x, norm_ffn_g[l])
        x = x + peer_ffn(h, w_peer_q[l], peer_sub_keys[l], peer_u[l], peer_v[l])
    return rms_norm(x, norm_final_g)


_drawn_inputs = setup_inputs


def setup_inputs(seed=0):
    import zlib

    import numpy as np

    out = dict(_drawn_inputs(seed))
    spreads = {}
    factors = {'norm_mix_g': 4.025,
     'conv_ln_g': 5.307,
     'conv_ln_b': 3.843,
     'norm_xattn_g': 8.0,
     'norm_mem_g': 8.0,
     'norm_ffn_g': 26.352,
     'norm_final_g': 31.792}
    for name, (base, spread) in spreads.items():
        noise = np.random.default_rng([zlib.crc32(name.encode()), seed]).standard_normal(out[name].shape)
        drawn = base * np.exp(spread * noise) if base else spread * noise
        out[name] = __import__('jax').numpy.asarray(drawn.astype(out[name].dtype))
    for name, factor in factors.items():
        out[name] = (out[name] * factor).astype(out[name].dtype)
    return out
```

```python
from contextlib import ExitStack

import numpy as np
import concourse.bass as bass
from concourse import mybir

P = 128
D = 1024
T = 1024
M = 256
NC = D // P
NT = T // P
H = 512
TAPS = 31
PAD = TAPS - 1
SB_HD = 64
XH = 4
PH = 8
KEYS = 128
TOPK = 16
EPS = 1e-6
LOWEST = -3.4028235e38

F32 = mybir.dt.float32
F32R = mybir.dt.float32r
U32 = mybir.dt.uint32
ALU = mybir.AluOpType
ACT = mybir.ActivationFunctionType
AX = mybir.AxisListType
ds = bass.ds


class Phase:

    def __init__(self, nc, tag):
        self.nc, self.tag, self.tensors, self.sems = nc, tag, ExitStack(), []

    def __enter__(self):
        return self

    def sb(self, name, shape, dt=F32):
        return self.tensors.enter_context(self.nc.sbuf_tensor(f"{self.tag}_{name}", shape, dt))

    def ps(self, name, shape):
        return self.tensors.enter_context(self.nc.psum_tensor(f"{self.tag}_{name}", shape, F32))

    def sem(self, name, start=0):
        self.sems.append(self.nc.alloc_semaphore(name=f"{self.tag}_{name}"))
        if start:
            self.nc.gpsimd.sem_inc(self.sems[-1], start)
        return self.sems[-1]

    def block(self):
        self.nc.all_engine_barrier()
        return self.tensors.enter_context(self.nc.Block())

    def __exit__(self, *error):
        self.tensors.close()
        if not any(error):
            self.nc.clear_and_free_semaphores(self.sems)
            self.nc.all_engine_barrier()


class Rsqrt:

    def __init__(self, m, name, n):
        self.mean, self.inv = m.sb(f"{name}_mean", [P, n]), m.sb(f"{name}_inv", [P, n])
        self.rstd = m.sb(f"{name}_rstd", [P, n])
        self.step = m.sem(f"{name}_step")
        self.rooted = m.sem(f"{name}_rooted")
        self.made = m.sem(f"{name}_made")

    def start(self, nc, dve, sums, psum_free):
        for i, (cols, src) in enumerate(sums):
            nc.vector.tensor_scalar(self.mean[:, cols], src, 1.0 / D, EPS, ALU.mult, ALU.add).then_inc(psum_free(i), 1)
        for i in range(len(sums)):
            dve.wait_ge(psum_free(i), 1)
        nc.vector.reciprocal(self.inv[:], self.mean[:]).then_inc(self.step, 1)

    def root(self, nc, act):
        act.wait_ge(self.step, 1)
        nc.scalar.activation(self.rstd[:], self.inv[:], ACT.Sqrt).then_inc(self.rooted, 1)

    def finish(self, nc, dve):
        dve.wait_ge(self.rooted, 1)
        nc.vector.tensor_tensor(self.inv[:], self.mean[:], self.rstd[:], ALU.mult).then_inc(self.step, 1)
        dve.wait_ge(self.step, 2)
        nc.vector.tensor_tensor(self.inv[:], self.inv[:], self.rstd[:], ALU.mult).then_inc(self.step, 1)
        dve.wait_ge(self.step, 3)
        nc.vector.tensor_scalar(self.inv[:], self.inv[:], -0.5, 1.5, ALU.mult, ALU.add).then_inc(self.step, 1)
        dve.wait_ge(self.step, 4)
        nc.vector.tensor_tensor(self.rstd[:], self.rstd[:], self.inv[:], ALU.mult).then_inc(self.made, 1)


def mixer_phase(nc, xT, gain, wstream, conv_w, h_out, y_out, attn_out):
    with Phase(nc, "mix") as m:
        NW = 5
        NG = 2 * NW
        hT = m.sb("hT", [P, NC, T])
        xbuf = m.sb("xbuf", [P, NC, T])
        sq = m.sb("sq", [P, 2, T])
        norm = Rsqrt(m, "norm", T)
        g_sb = m.sb("gain", [P, NC])
        ones = m.sb("ones", [P, P])
        tri = m.sb("tri", [P, P])
        rest = m.sb("rest", [P, P])
        causal = m.sb("causal", [P, P])
        w_sb = m.sb("w", [P, NW, NC, P])
        egate = m.sb("egate", [P, T])
        den = m.sb("den", [P, T])
        u = m.sb("u", [P, 2, PAD + T])
        ybuf = m.sb("ybuf", [P, 2, T])
        cw = m.sb("cw", [P, NC, TAPS + 1])
        cwj = m.sb("cwj", [P, TAPS + 1])
        qT = m.sb("qT", [P, 2, T])
        kT = m.sb("kT", [P, 2, T])
        v = m.sb("v", [P, 2, NT, P])
        absz = m.sb("absz", [P, 2, H])
        ex = m.sb("exp", [P, 2, H])
        ln = m.sb("ln", [P, 2, H])
        sp = m.sb("softplus", [P, 2, H])
        ls = m.sb("logsig", [P, 2, H])
        lw = m.sb("logw", [P, 2, H])
        wt = m.sb("weight", [P, 2, H])
        oT = m.sb("oT", [P, 2, T])

        gemm = m.ps("gemm", [P, 2, H])
        zps = m.ps("z", [P, 2, H])
        cps = m.ps("c", [P, 2, H])
        ops = m.ps("o", [P, 2, H])

        x_loaded = [m.sem(f"x_loaded{i}") for i in range(2)]
        c_loaded = m.sem("c_loaded")
        const_made = m.sem("const_made")
        sq_made = m.sem("sq_made")
        sum_done = m.sem("sum_done")
        h_made = m.sem("h_made")
        w_loaded = [m.sem(f"w_loaded{c}") for c in range(NW)]
        w_used = m.sem("w_used")
        group_done = m.sem("group_done")
        evicted = [m.sem(f"evicted{b}") for b in range(2)]
        u_step = m.sem("u_step")
        u_made = m.sem("u_made", start=1)
        cwj_made = m.sem("cwj_made")
        conv_step = m.sem("conv_step")
        h_stored = m.sem("h_stored")
        y_stored = [m.sem(f"y_stored{b}", start=1) for b in range(2)]
        o_copied = m.sem("o_copied", start=1)
        o_stored = [m.sem(f"o_stored{b}", start=1) for b in range(2)]
        z_done = [m.sem(f"z_done{s}") for s in range(2)]
        act_step = [m.sem(f"act_step{s}") for s in range(2)]
        ln_done = [m.sem(f"ln_done{s}") for s in range(2)]
        sp_raw = [m.sem(f"sp_raw{s}") for s in range(2)]
        sp_done = [m.sem(f"sp_done{s}") for s in range(2)]
        c_done = [m.sem(f"c_done{s}") for s in range(2)]
        ls_done = [m.sem(f"ls_done{s}", start=1) for s in range(2)]
        lw_done = [m.sem(f"lw_done{s}", start=1) for s in range(2)]
        wt_raw = [m.sem(f"wt_raw{s}") for s in range(2)]
        wt_done = [m.sem(f"wt_done{s}", start=1) for s in range(2)]
        sp_used = [m.sem(f"sp_used{s}", start=1) for s in range(2)]
        pv_done = [m.sem(f"pv_done{s}", start=1) for s in range(2)]

        cells = [(qh, kb) for qh in range(2) for kb in range(4 * qh + 3, -1, -1)]
        NCELL = len(cells)
        col0 = [max(0, kb - 4 * qh) * P for qh, kb in cells]
        masked = [kb >= 4 * qh for qh, kb in cells]
        NMASK = sum(masked)
        opens = [kb == 4 * qh + 3 for qh, kb in cells]
        closes = [kb == 0 for qh, kb in cells]

        def pairs(eng, body):
            with eng.Fori(0, NC // 2 - 1) as jj:
                for par in range(2):
                    body(jj * 2 + par, par, jj, False)
            for par in range(2):
                body(NC - 2 + par, par, NC // 2 - 1, par == 1)

        def mask_count(j, i):
            return NMASK * j + sum(masked[:i])

        def bank_evicted(eng, j, g):
            eng.wait_ge(evicted[g % 2], NW * j + g // 2 + 2)

        block = m.block()

        @block.sync
        def _(sync):
            for i in range(2):
                sync.dma_start(xbuf[:, 4 * i:4 * i + 4, :], xT[:, 4 * i:4 * i + 4, :]).then_inc(x_loaded[i], 16)
            sync.dma_start(g_sb[:], gain).then_inc(c_loaded, 16)
            sync.dma_start(cw[:], conv_w).then_inc(c_loaded, 16)
            for c in range(NW):
                sync.dma_start(w_sb[:, c], wstream[c]).then_inc(w_loaded[c], 16)
            sync.wait_ge(h_made, NC)
            sync.dma_start(h_out, hT[:]).then_inc(h_stored, 16)

            def body(j, par, jj, last):
                if not last:
                    for c in range(NW):
                        sync.wait_ge(w_used, NW * j + c + 1)
                        sync.dma_start(w_sb[:, c], wstream[ds(j * NW + (NW + c), 1)].rearrange("a p c n -> (a p) c n")
                                       ).then_inc(w_loaded[c], 16)
                sync.wait_ge(conv_step, TAPS * j + TAPS)
                sync.dma_start(y_out[:, ds(j, 1), :], ybuf[:, par:par + 1, :]).then_inc(y_stored[par], 16)
                sync.wait_ge(o_copied, 4 * j + 4 + 1)
                sync.dma_start(attn_out[:, ds(j, 1), :], oT[:, par:par + 1, :]).then_inc(o_stored[par], 16)

            pairs(sync, body)
            sync.wait_ge(h_stored, 16)
            for b in range(2):
                sync.wait_ge(y_stored[b], 16 * (NC // 2) + 1)
                sync.wait_ge(o_stored[b], 16 * (NC // 2) + 1)

        @block.gpsimd
        def _(pool):
            nc.gpsimd.memset(ones[:], 1.0).then_inc(const_made, 1)
            nc.gpsimd.memset(u[:, :, 0:PAD], 0.0).then_inc(const_made, 1)
            pool.wait_ge(const_made, 2)
            nc.gpsimd.affine_select(out=tri[:], in_=ones[:], pattern=[[-1, P]], compare_op=ALU.is_gt, fill=0.0,
                                    base=0, channel_multiplier=1).then_inc(const_made, 1)
            nc.gpsimd.affine_select(out=rest[:], in_=ones[:], pattern=[[1, P]], compare_op=ALU.is_ge, fill=0.0,
                                    base=0, channel_multiplier=-1).then_inc(const_made, 1)
            nc.gpsimd.affine_select(out=causal[:], in_=ones[:], pattern=[[1, P]], compare_op=ALU.is_gt, fill=0.0,
                                    base=0, channel_multiplier=-1).then_inc(const_made, 1)
            pool.wait_ge(const_made, 5)

            with pool.Fori(0, NC) as j:
                for i in range(NCELL):
                    if not masked[i]:
                        continue
                    a = col0[i]
                    for s in range(2):
                        pool.wait_ge(sp_raw[s], mask_count(j, i) + 1)
                        nc.gpsimd.tensor_tensor(sp[:, s, a:a + P], sp[:, s, a:a + P], causal[:], ALU.mult
                                                ).then_inc(sp_done[s], 1)
                    for s in range(2):
                        pool.wait_ge(wt_raw[s], mask_count(j, i) + 1)
                        nc.gpsimd.tensor_tensor(wt[:, s, a:a + P], wt[:, s, a:a + P], causal[:], ALU.mult
                                                ).then_inc(wt_done[s], 1)

        @block.scalar
        def _(act):
            for i in range(NC):
                act.wait_ge(x_loaded[i // 4], 16)
                if i >= 2:
                    act.wait_ge(sum_done, i - 1)
                nc.scalar.activation(sq[:, i % 2], xbuf[:, i], ACT.Square).then_inc(sq_made, 1)

            norm.root(nc, act)
            nc.scalar.preload_act_table_set("natural_log_exp_and_others")

            def evict(j, par, g):
                c, h = g // 2, g % 2
                if c == 1:
                    return
                act.wait_ge(group_done, NG * j + g + 1)
                hs = slice(h * H, h * H + H)
                if c == 0:
                    act.wait_ge(u_made, 2 * j + 1)
                    nc.scalar.activation(egate[:, hs], gemm[:, h], ACT.Exp, scale=-1.0).then_inc(evicted[h], 1)
                elif c == 2:
                    nc.scalar.activation(qT[:, par, hs], gemm[:, h], ACT.Copy,
                                         scale=float(SB_HD) ** -0.5).then_inc(evicted[h], 1)
                elif c == 3:
                    nc.scalar.activation(kT[:, par, hs], gemm[:, h], ACT.Copy).then_inc(evicted[h], 1)
                else:
                    nc.scalar.activation(v[:, par, 4 * h:4 * h + 4, :],
                                         gemm[:, h].rearrange("p (t n) -> p t n", n=P), ACT.Copy).then_inc(evicted[h], 1)

            for g in range(NG):
                evict(0, 0, g)

            def body(j, par, jj, last):
                for i in range(NCELL):
                    a, n = col0[i], NCELL * j + i
                    for s in range(2):
                        act.wait_ge(z_done[s], n + 1)
                        nc.scalar.activation(absz[:, s, a:H], zps[:, s, a:H], ACT.Abs).then_inc(act_step[s], 1)
                    for s in range(2):
                        act.wait_ge(act_step[s], n * 2 + 1)
                        act.wait_ge(ls_done[s], n + 1)
                        nc.scalar.activation(ex[:, s, a:H], absz[:, s, a:H], ACT.Exp, scale=-1.0).then_inc(act_step[s], 1)
                    for s in range(2):
                        act.wait_ge(act_step[s], n * 2 + 2)
                        nc.scalar.activation(ln[:, s, a:H], ex[:, s, a:H], ACT.Ln, bias=1.0).then_inc(ln_done[s], 1)
                    if not last and 1 <= i <= NG:
                        evict(j + 1, 1 - par, i - 1)
                    for s in range(2):
                        act.wait_ge(lw_done[s], n + 1 + 1)
                        act.wait_ge(pv_done[s], n + 1)
                        ins = nc.scalar.activation(wt[:, s, a:H], lw[:, s, a:H], ACT.Exp)
                        ins.then_inc(wt_raw[s] if masked[i] else wt_done[s], 1)
                    if i and closes[i - 1]:
                        outputs(j, par, jj, cells[i - 1][0], NCELL * j + i)
                outputs(j, par, jj, 1, NCELL * j + NCELL)

            def outputs(j, par, jj, qh, n):
                act.wait_ge(o_stored[par], 16 * jj + 1)
                for s in range(2):
                    act.wait_ge(pv_done[s], n + 1)
                    rows = slice(64 * s, 64 * s + 64)
                    nc.scalar.activation(oT[rows, par, qh * H:qh * H + H], ops[rows, s, :], ACT.Copy
                                         ).then_inc(o_copied, 1)

            pairs(act, body)

        @block.vector
        def _(dve):
            dve.wait_ge(sum_done, NC)
            norm.start(nc, dve, [(slice(h * H, h * H + H), gemm[:, h]) for h in range(2)], lambda h: evicted[h])
            norm.finish(nc, dve)
            dve.wait_ge(c_loaded, 32)
            dve.wait_ge(norm.made, 1)
            for c in range(NC):
                nc.vector.scalar_tensor_tensor(out=hT[:, c], in0=xbuf[:, c], scalar=g_sb[:, c:c + 1], in1=norm.rstd[:],
                                               op0=ALU.mult, op1=ALU.mult).then_inc(h_made, 1)

            def value(j, par, h):
                dve.wait_ge(group_done, NG * j + 2 + h + 1)
                bank_evicted(dve, j, h)
                hs = slice(h * H, h * H + H)
                nc.vector.tensor_scalar(den[:, hs], egate[:, hs], 1.0, None, ALU.add).then_inc(u_step, 1)
                dve.wait_ge(u_step, 4 * j + 2 * h + 1)
                nc.vector.reciprocal(den[:, hs], den[:, hs]).then_inc(u_step, 1)
                dve.wait_ge(u_step, 4 * j + 2 * h + 2)
                nc.vector.tensor_tensor(u[:, par, PAD + h * H:PAD + h * H + H], gemm[:, h], den[:, hs],
                                        ALU.mult).then_inc(evicted[h], 1)
                bank_evicted(dve, j, 2 + h)
                dve.sem_inc(u_made, 1)

            def conv(j, par, jj, t):
                if t == 0:
                    nc.vector.tensor_copy(cwj[:], cw[:, ds(j, 1), :].rearrange("p a t -> p (a t)")).then_inc(cwj_made, 1)
                    dve.wait_ge(cwj_made, j + 1)
                    dve.wait_ge(y_stored[par], 16 * jj + 1)
                    dve.wait_ge(u_made, 2 * j + 2 + 1)
                    nc.vector.tensor_scalar(ybuf[:, par], u[:, par, 0:T], cwj[:, 0:1], cwj[:, TAPS:TAPS + 1],
                                            ALU.mult, ALU.add).then_inc(conv_step, 1)
                else:
                    dve.wait_ge(conv_step, TAPS * j + t)
                    nc.vector.scalar_tensor_tensor(out=ybuf[:, par], in0=u[:, par, t:t + T], scalar=cwj[:, t:t + 1],
                                                   in1=ybuf[:, par], op0=ALU.mult, op1=ALU.add).then_inc(conv_step, 1)

            for h in range(2):
                value(0, 0, h)

            def body(j, par, jj, last):
                for i in range(NCELL):
                    a, n = col0[i], NCELL * j + i
                    for s in range(2):
                        dve.wait_ge(ln_done[s], n + 1)
                        dve.wait_ge(sp_used[s], n + 1)
                        ins = nc.vector.scalar_tensor_tensor(out=sp[:, s, a:H], in0=zps[:, s, a:H], scalar=0.0,
                                                             in1=ln[:, s, a:H], op0=ALU.max, op1=ALU.add)
                        ins.then_inc(sp_raw[s] if masked[i] else sp_done[s], 1)
                    for s in range(2):
                        nc.vector.scalar_tensor_tensor(out=ls[:, s, a:H], in0=zps[:, s, a:H], scalar=0.0,
                                                       in1=ln[:, s, a:H], op0=ALU.min, op1=ALU.subtract
                                                       ).then_inc(ls_done[s], 1)
                    if not last and i in (3, 4):
                        value(j + 1, 1 - par, i - 3)
                    for s in range(2):
                        dve.wait_ge(c_done[s], n + 1)
                        dve.wait_ge(wt_raw[s], mask_count(j, i)) if i and masked[i - 1] else dve.wait_ge(wt_done[s], n + 1)
                        dve.wait_ge(ls_done[s], n + 1 + 1)
                        nc.vector.tensor_tensor(lw[:, s, a:H], ls[:, s, a:H], cps[:, s, a:H], ALU.subtract
                                                ).then_inc(lw_done[s], 1)
                    for t in range(3 * i, min(3 * i + 3, TAPS)):
                        conv(j, par, jj, t)

            pairs(dve, body)

        @block.tensor
        def _(pe):
            pe.wait_ge(const_made, 4)
            for c in range(NC):
                pe.wait_ge(sq_made, c + 1)
                for h in range(2):
                    mm = nc.tensor.matmul(gemm[:, h], ones[:], sq[:, c % 2, h * H:h * H + H],
                                          start=(c == 0), stop=(c == NC - 1))
                mm.then_inc(sum_done, 1)
            pe.wait_ge(h_made, NC)

            def project(j, g, k0, k1):
                c, h = g // 2, g % 2
                if k0 == 0:
                    if h == 0:
                        pe.wait_ge(w_loaded[c], j * 16 + 16)
                    pe.wait_ge(evicted[h], NW * j + c + 1)
                if c == 4:
                    for x in range(k0 // 2, k1 // 2):
                        t = 4 * h + x
                        for k in range(NC):
                            mm = nc.tensor.matmul(gemm[:, h, x * P:x * P + P], hT[:, k, t * P:t * P + P], w_sb[:, c, k],
                                                  start=(k == 0), stop=(k == NC - 1))
                else:
                    for k in range(k0, k1):
                        mm = nc.tensor.matmul(gemm[:, h], w_sb[:, c, k], hT[:, k, h * H:h * H + H],
                                              start=(k == 0), stop=(k == NC - 1))
                if k1 == NC:
                    mm.then_inc(group_done, 1)
                    if h == 1:
                        pe.wait_ge(group_done, NG * j + g + 1)
                        pe.sem_inc(w_used, 1)

            def z_cell(j, par, s, i):
                (qh, kb), a = cells[i], col0[i]
                if i == 0:
                    bank_evicted(pe, j, 6)
                    bank_evicted(pe, j, 7)
                pe.wait_ge(ls_done[s], NCELL * j + i + 1)
                rows = slice(64 * s, 64 * s + 64)
                nc.tensor.matmul(zps[:, s, a:H], kT[rows, par, kb * P:kb * P + P], qT[rows, par, qh * H + a:qh * H + H],
                                 start=True, stop=True).then_inc(z_done[s], 1)

            def add_own(j, s, i):
                a = col0[i]
                pe.wait_ge(sp_done[s], NCELL * j + i + 1)
                if opens[i]:
                    pe.wait_ge(lw_done[s], NCELL * j + i + 1)
                mm = nc.tensor.matmul(cps[:, s, a:H], tri[:], sp[:, s, a:H], start=opens[i], stop=True,
                                      skip_group_check=True)
                mm.then_inc(c_done[s], 1)
                if closes[i]:
                    pe.wait_ge(c_done[s], NCELL * j + i + 1)
                    pe.sem_inc(sp_used[s], 1)

            def add_rest(j, s, i):
                a = col0[i]
                if not closes[i]:
                    pe.wait_ge(lw_done[s], NCELL * j + i + 1 + 1)
                    nc.tensor.matmul(cps[:, s, a:H], rest[:], sp[:, s, a:H], start=False, stop=True,
                                     skip_group_check=True).then_inc(sp_used[s], 1)

            def weigh(j, par, s, i):
                (qh, kb), a = cells[i], col0[i]
                if i == 0:
                    bank_evicted(pe, j, 8)
                    bank_evicted(pe, j, 9)
                if opens[i]:
                    pe.wait_ge(o_copied, 4 * j + 2 * qh + 1)
                pe.wait_ge(wt_done[s], NCELL * j + i + 1 + 1)
                nc.tensor.matmul(ops[64 * s:64 * s + 64, s, a:H], v[:, par, kb, 64 * s:64 * s + 64], wt[:, s, a:H],
                                 start=opens[i], stop=closes[i], skip_group_check=True).then_inc(pv_done[s], 1)

            for g in range(NG):
                project(0, g, 0, NC)
            for s in range(2):
                z_cell(0, 0, s, 0)

            def body(j, par, jj, last):
                for i in range(NCELL):
                    for s in range(2):
                        add_own(j, s, i)
                    if not last and i < NG:
                        project(j + 1, i, 0, NC // 2)
                    for s in range(2):
                        add_rest(j, s, i)
                        if i < NCELL - 1:
                            z_cell(j, par, s, i + 1)
                        elif not last:
                            z_cell(j + 1, 1 - par, s, 0)
                    if not last and i < NG:
                        project(j + 1, i, NC // 2, NC)
                    for s in range(2):
                        weigh(j, par, s, i)

            pairs(pe, body)


def merge_phase(nc, xT, h_in, y_in, attn_in, wstream, ln_g, ln_b, gate_b, x_out):
    with Phase(nc, "merge") as m:
        NW = 4
        hT = m.sb("hT", [P, NC, T])
        zT = m.sb("zT", [P, NC, T])
        aT = m.sb("aT", [P, NC, T])
        mT = m.sb("mT", [P, NC, T])
        sq = m.sb("sq", [P, 2, T])
        mean = m.sb("mean", [P, T])
        norm = Rsqrt(m, "norm", T)
        ones = m.sb("ones", [P, P])
        lng, lnb = m.sb("lng", [P, NC]), m.sb("lnb", [P, NC])
        gb = m.sb("gb", [P, 2, NC])
        gbj = m.sb("gbj", [P, 2])
        w_sb = m.sb("w", [P, NW, NC, P])
        sg = m.sb("sg", [P, 2, T])
        xres = m.sb("xres", [P, 2, T])
        banks = m.ps("banks", [P, 8, H])

        y_loaded = [m.sem(f"y_loaded{i}") for i in range(2)]
        h_loaded = m.sem("h_loaded")
        a_loaded = m.sem("a_loaded")
        c_loaded = m.sem("c_loaded")
        ones_made = m.sem("ones_made")
        mean_sum = m.sem("mean_sum")
        mean_made = m.sem("mean_made")
        centred = m.sem("centred")
        sq_made = m.sem("sq_made")
        sq_used = m.sem("sq_used")
        sums_read = [m.sem(f"sums_read{h}") for h in range(2)]
        scaled = m.sem("scaled")
        z_made = m.sem("z_made")
        w_loaded = [m.sem(f"w_loaded{c}") for c in range(NW)]
        w_used = m.sem("w_used")
        group_done = m.sem("group_done")
        gbj_made = m.sem("gbj_made")
        gated = m.sem("gated", start=1)
        product = m.sem("product", start=1)
        m_made = m.sem("m_made", start=1)
        x_loaded = [m.sem(f"x_loaded{b}") for b in range(2)]
        x_made = m.sem("x_made", start=1)
        x_stored = [m.sem(f"x_stored{b}", start=1) for b in range(2)]
        block = m.block()

        @block.sync
        def _(sync):
            for i in range(2):
                sync.dma_start(zT[:, 4 * i:4 * i + 4], y_in[:, 4 * i:4 * i + 4]).then_inc(y_loaded[i], 16)
            sync.dma_start(lng[:], ln_g).then_inc(c_loaded, 16)
            sync.dma_start(lnb[:], ln_b).then_inc(c_loaded, 16)
            sync.dma_start(gb[:], gate_b).then_inc(c_loaded, 16)
            sync.dma_start(hT[:], h_in).then_inc(h_loaded, 16)
            for c in range(NW):
                sync.dma_start(w_sb[:, c], wstream[c]).then_inc(w_loaded[c], 16)
            sync.dma_start(aT[:], attn_in).then_inc(a_loaded, 16)
            with sync.Fori(0, NC + 1) as j:
                for c in range(NW):
                    sync.wait_ge(w_used, j * NW + (c + 1))
                    sync.dma_start(w_sb[:, c], wstream[ds(j * NW + (NW + c), 1)].rearrange("a p c n -> (a p) c n")
                                   ).then_inc(w_loaded[c], 16)
            with sync.Fori(0, NC // 2) as jj:
                for b in range(2):
                    n = jj * 2 + b
                    sync.wait_ge(x_stored[b], jj * 16 + 1)
                    sync.dma_start(xres[:, b], xT[:, ds(n, 1), :].rearrange("p a t -> p (a t)")).then_inc(x_loaded[b], 16)
                for b in range(2):
                    n = jj * 2 + b
                    sync.wait_ge(x_made, n * 2 + 2 + 1)
                    sync.dma_start(x_out[:, ds(n, 1), :].rearrange("p a t -> p (a t)"), xres[:, b]).then_inc(x_stored[b], 16)
            for b in range(2):
                sync.wait_ge(x_stored[b], 16 * (NC // 2) + 1)

        @block.gpsimd
        def _(pool):
            nc.gpsimd.memset(ones[:], 1.0).then_inc(ones_made, 1)

        @block.tensor
        def _(pe):
            pe.wait_ge(ones_made, 1)
            for k in range(NC):
                if k % 4 == 0:
                    pe.wait_ge(y_loaded[k // 4], 16)
                for h in range(2):
                    mm = nc.tensor.matmul(banks[:, h], ones[:], zT[:, k, h * H:h * H + H], start=(k == 0), stop=(k == NC - 1))
            mm.then_inc(mean_sum, 1)
            for k in range(NC):
                pe.wait_ge(sq_made, k + 1)
                for h in range(2):
                    mm = nc.tensor.matmul(banks[:, 2 + h], ones[:], sq[:, k % 2, h * H:h * H + H],
                                          start=(k == 0), stop=(k == NC - 1))
                mm.then_inc(sq_used, 1)
            pe.wait_ge(h_loaded, 16)
            pe.wait_ge(z_made, NC)
            pe.wait_ge(a_loaded, 16)
            with pe.Fori(0, NC) as j:
                for c, src in enumerate((hT, zT, hT, aT)):
                    pe.wait_ge(w_loaded[c], j * 16 + 16)
                    if c % 2 == 0:
                        pe.wait_ge(gated, j * 4 + 1)
                    else:
                        pe.wait_ge(product, j * 4 + 1)
                    for h in range(2):
                        for k in range(NC):
                            mm = nc.tensor.matmul(banks[:, 2 * c + h], w_sb[:, c, k], src[:, k, h * H:h * H + H],
                                                  start=(k == 0), stop=(k == NC - 1))
                        if h == 0:
                            mm.then_inc(group_done, 1)
                    mm.then_inc(group_done, 1)
                    pe.wait_ge(group_done, j * 8 + (2 * c + 2))
                    pe.sem_inc(w_used, 1)
            pe.wait_ge(m_made, 2 * NC + 1)
            with pe.Fori(0, NC // NW) as r:
                for c in range(NW):
                    pe.wait_ge(w_loaded[c], r * 16 + 16 * (NC + 1))
                    pe.wait_ge(x_made, r * 8 + 1)
                    for h in range(2):
                        for k in range(NC):
                            mm = nc.tensor.matmul(banks[:, 2 * c + h], w_sb[:, c, k], mT[:, k, h * H:h * H + H],
                                                  start=(k == 0), stop=(k == NC - 1))
                        if h == 0:
                            mm.then_inc(group_done, 1)
                    mm.then_inc(group_done, 1)
                    pe.wait_ge(group_done, r * 8 + (8 * NC + 2 * c + 2))
                    pe.sem_inc(w_used, 1)

        @block.scalar
        def _(act):
            for k in range(NC):
                act.wait_ge(centred, k + 1)
                if k >= 2:
                    act.wait_ge(sq_used, k - 1)
                nc.scalar.activation(sq[:, k % 2], zT[:, k], ACT.Square).then_inc(sq_made, 1)
            norm.root(nc, act)
            act.wait_ge(c_loaded, 48)
            for k in range(NC):
                act.wait_ge(scaled, k + 1)
                nc.scalar.activation(zT[:, k], zT[:, k], ACT.Silu, bias=lnb[:, k:k + 1]).then_inc(z_made, 1)
            nc.scalar.preload_act_table(ACT.Sigmoid)
            with act.Fori(0, NC) as j:
                act.wait_ge(m_made, j * 2 + 1)
                nc.scalar.activation(gbj[:], gb[:, :, ds(j, 1)].rearrange("p b a -> p (b a)"), ACT.Copy).then_inc(gbj_made, 1)
                act.wait_ge(gbj_made, j + 1)
                for b in range(2):
                    for h in range(2):
                        act.wait_ge(group_done, j * 8 + (4 * b + h + 1))
                        nc.scalar.activation(sg[:, b, h * H:h * H + H], banks[:, 4 * b + h], ACT.Sigmoid, bias=gbj[:, b:b + 1]
                                             ).then_inc(gated, 1)

        @block.vector
        def _(dve):
            dve.wait_ge(mean_sum, 1)
            for h in range(2):
                nc.vector.tensor_scalar(mean[:, h * H:h * H + H], banks[:, h], 1.0 / D, None, ALU.mult).then_inc(mean_made, 1)
            dve.wait_ge(mean_made, 2)
            for k in range(NC):
                nc.vector.tensor_tensor(zT[:, k], zT[:, k], mean[:], ALU.subtract).then_inc(centred, 1)
            dve.wait_ge(sq_used, NC)
            norm.start(nc, dve, [(slice(h * H, h * H + H), banks[:, 2 + h]) for h in range(2)], lambda h: sums_read[h])
            norm.finish(nc, dve)
            dve.wait_ge(norm.made, 1)
            dve.wait_ge(c_loaded, 48)
            for k in range(NC):
                nc.vector.scalar_tensor_tensor(out=zT[:, k], in0=zT[:, k], scalar=lng[:, k:k + 1], in1=norm.rstd[:],
                                               op0=ALU.mult, op1=ALU.mult).then_inc(scaled, 1)
            with dve.Fori(0, NC) as j:
                for b in range(2):
                    for h in range(2):
                        hs = slice(h * H, h * H + H)
                        dve.wait_ge(group_done, j * 8 + (4 * b + 2 + h + 1))
                        dve.wait_ge(gated, j * 4 + (2 * b + h + 1) + 1)
                        nc.vector.tensor_tensor(sg[:, b, hs], sg[:, b, hs], banks[:, 4 * b + 2 + h], ALU.mult
                                                ).then_inc(product, 1)
                for h in range(2):
                    hs = slice(h * H, h * H + H)
                    dve.wait_ge(product, j * 4 + (3 + h) + 1)
                    nc.vector.tensor_tensor(mT[:, ds(j, 1), hs].rearrange("p a t -> p (a t)"), sg[:, 0, hs], sg[:, 1, hs],
                                            ALU.add).then_inc(m_made, 1)
            with dve.Fori(0, NC // NW) as r:
                for c in range(NW):
                    b = c % 2
                    dve.wait_ge(x_loaded[b], r * 32 + 16 * (c // 2 + 1))
                    for h in range(2):
                        hs = slice(h * H, h * H + H)
                        dve.wait_ge(group_done, r * 8 + (8 * NC + 2 * c + h + 1))
                        nc.vector.tensor_tensor(xres[:, b, hs], xres[:, b, hs], banks[:, 2 * c + h], ALU.add
                                                ).then_inc(x_made, 1)


def cross_attention_phase(nc, x_in, gain, memT, mem_gain, wstream, x_out):
    with Phase(nc, "xattn") as m:
        NW = 6
        HC = 2
        MT = M // P
        xT = m.sb("xT", [P, NC, T])
        hT = m.sb("hT", [P, NC, T])
        mT = m.sb("mT", [P, NC, M])
        oT = m.sb("oT", [P, NC, T])
        sq = m.sb("sq", [P, 2, T])
        msq = m.sb("msq", [P, NC, M])
        norm = Rsqrt(m, "norm", T)
        mnorm = Rsqrt(m, "mnorm", M)
        g_sb, mg_sb = m.sb("gain", [P, NC]), m.sb("mgain", [P, NC])
        ones = m.sb("ones", [P, P])
        ident = m.sb("ident", [P, P])
        w_sb = m.sb("w", [P, NW, NC, P])
        qT = m.sb("qT", [P, HC, T])
        kT = m.sb("kT", [P, HC, M])
        v = m.sb("v", [P, MT, HC * P])
        top = m.sb("top", [P, NT])
        total = m.sb("total", [P, NT])
        inv = m.sb("inv", [P, NT])
        prob = m.sb("prob", [P, 2, 2, M])
        pT = m.sb("pT", [P, MT, T])

        gemm = m.ps("gemm", [P, 2, H])
        score = m.ps("score", [P, 2, 2, M])
        turned = m.ps("turned", [P, 2, MT, 2 * P])
        out = m.ps("out", [P, 2, H])

        x_loaded = [m.sem(f"x_loaded{i}") for i in range(2)]
        m_loaded = m.sem("m_loaded")
        c_loaded = m.sem("c_loaded")
        made = m.sem("made")
        sq_made = m.sem("sq_made")
        sq_used = m.sem("sq_used")
        msq_made = m.sem("msq_made")
        msum_done = m.sem("msum_done")
        msum_read = m.sem("msum_read")
        mh_made = m.sem("mh_made")
        h_made = m.sem("h_made")
        w_loaded = [m.sem(f"w_loaded{c}") for c in range(NW)]
        w_used = m.sem("w_used")
        group_done = m.sem("group_done")
        evicted = [m.sem(f"evicted{b}") for b in range(2)]
        score_done = m.sem("score_done")
        top_made = m.sem("top_made")
        exp_made = m.sem("exp_made", start=1)
        inv_made = m.sem("inv_made")
        prob_made = m.sem("prob_made")
        turned_done = m.sem("turned_done", start=1)
        pT_made = m.sem("pT_made", start=1)
        out_done = m.sem("out_done", start=1)
        o_made = m.sem("o_made", start=1)
        x_made = m.sem("x_made")
        x_stored = m.sem("x_stored")
        block = m.block()
        GH = 2 * NW
        GROUPS = [("q", 0, 0), ("q", 0, 1), ("q", 1, 0), ("q", 1, 1), ("k", 0, 0), ("k", 1, 0), ("v", 0, 0), ("v", 1, 0)]
        NGR = len(GROUPS)

        @block.sync
        def _(sync):
            for i in range(2):
                sync.dma_start(xT[:, 4 * i:4 * i + 4], x_in[:, 4 * i:4 * i + 4]).then_inc(x_loaded[i], 16)
            sync.dma_start(mT[:], memT).then_inc(m_loaded, 16)
            sync.dma_start(g_sb[:], gain).then_inc(c_loaded, 16)
            sync.dma_start(mg_sb[:], mem_gain).then_inc(c_loaded, 16)
            for c in range(NW):
                sync.dma_start(w_sb[:, c], wstream[c]).then_inc(w_loaded[c], 16)
            with sync.Fori(0, XH - 1) as hd:
                for c in range(NW):
                    sync.wait_ge(w_used, hd * NW + (c + 1))
                    sync.dma_start(w_sb[:, c], wstream[ds(hd * NW + (NW + c), 1)].rearrange("a p c n -> (a p) c n")
                                   ).then_inc(w_loaded[c], 16)
            for n in range(NC):
                c = n % 4
                sync.wait_ge(w_used, NW * (XH - 1) + c + 1 if n < 4 else NW * XH + n - 3)
                sync.dma_start(w_sb[:, c], wstream[NW * XH + n]).then_inc(w_loaded[c], 16)
            for n in range(NC):
                sync.wait_ge(x_made, 2 * n + 2)
                sync.dma_start(x_out[:, n], xT[:, n]).then_inc(x_stored, 16)
            sync.wait_ge(x_stored, 16 * NC)

        @block.gpsimd
        def _(pool):
            nc.gpsimd.memset(ones[:], 1.0).then_inc(made, 1)
            pool.wait_ge(made, 1)
            nc.gpsimd.affine_select(out=ident[:], in_=ones[:], pattern=[[-1, P]], compare_op=ALU.is_equal, fill=0.0,
                                    base=0, channel_multiplier=1).then_inc(made, 1)

        @block.tensor
        def _(pe):
            pe.wait_ge(made, 2)
            pe.wait_ge(msq_made, 1)
            for k in range(NC):
                mm = nc.tensor.matmul(out[:, 0, 0:M], ones[:], msq[:, k], start=(k == 0), stop=(k == NC - 1))
            mm.then_inc(msum_done, 1)
            for k in range(NC):
                pe.wait_ge(sq_made, k + 1)
                for h in range(2):
                    mm = nc.tensor.matmul(gemm[:, h], ones[:], sq[:, k % 2, h * H:h * H + H], start=(k == 0), stop=(k == NC - 1))
                mm.then_inc(sq_used, 1)
            pe.wait_ge(mh_made, NC)
            pe.wait_ge(h_made, NC)

            def turn(hd, s):
                pe.wait_ge(prob_made, hd * 8 + (2 * s + 2))
                pe.wait_ge(pT_made, hd * 4 + s - 1 + 1) if s else pe.wait_ge(pT_made, hd * 4 + 1)
                for x in range(2):
                    for t in range(MT):
                        mm = nc.tensor.transpose(turned[:, s % 2, t, x * P:x * P + P], prob[:, s % 2, x, t * P:t * P + P],
                                                 ident[:])
                mm.then_inc(turned_done, 1)

            with pe.Fori(0, XH) as hd:
                for g, (what, i, h) in enumerate(GROUPS):
                    b = g % 2
                    if what == "q":
                        c, n = i, H
                    else:
                        c, n = (2 + i if what == "k" else 4), M
                    pe.wait_ge(w_loaded[c], hd * 16 + 16)
                    if what == "v":
                        pe.wait_ge(w_loaded[5], hd * 16 + 16)
                    pe.wait_ge(evicted[b], hd * (NGR // 2) + (g // 2 + 1))
                    if what == "q":
                        for k in range(NC):
                            mm = nc.tensor.matmul(gemm[:, b], w_sb[:, c, k], hT[:, k, h * H:h * H + H],
                                                  start=(k == 0), stop=(k == NC - 1))
                    elif what == "k":
                        for k in range(NC):
                            mm = nc.tensor.matmul(gemm[:, b, 0:M], w_sb[:, c, k], mT[:, k], start=(k == 0), stop=(k == NC - 1))
                    else:
                        for half in range(HC):
                            for k in range(NC):
                                mm = nc.tensor.matmul(gemm[:, b, half * P:half * P + P], mT[:, k, i * P:i * P + P],
                                                      w_sb[:, 4 + half, k], start=(k == 0), stop=(k == NC - 1))
                    mm.then_inc(group_done, 1)
                    done = {1: 1, 3: 1, 4: 1, 5: 1, 7: 2}.get(g, 0)
                    if done:
                        pe.wait_ge(group_done, hd * NGR + (g + 1))
                        pe.sem_inc(w_used, done)
                for b in range(2):
                    pe.wait_ge(evicted[b], hd * (NGR // 2) + (NGR // 2 + 1))
                for s in range(4):
                    if s >= 2:
                        pe.wait_ge(exp_made, hd * 8 + 2 * (s - 1) + 1)
                    else:
                        pe.wait_ge(exp_made, hd * 8 + 1)
                    for x in range(2):
                        t = 2 * s + x
                        for c in range(HC):
                            mm = nc.tensor.matmul(score[:, s % 2, x], qT[:, c, t * P:t * P + P], kT[:, c],
                                                  start=(c == 0), stop=(c == HC - 1))
                    mm.then_inc(score_done, 1)
                    if s >= 1:
                        turn(hd, s - 1)
                turn(hd, 3)
                pe.wait_ge(pT_made, hd * 4 + 4 + 1)
                for c in range(HC):
                    for h in range(2):
                        pe.wait_ge(o_made, hd * 4 + (2 * c + h - 1) + 1) if 2 * c + h >= 2 else pe.wait_ge(o_made, hd * 4 + 1)
                        for t in range(MT):
                            mm = nc.tensor.matmul(out[:, h], v[:, t, c * P:c * P + P], pT[:, t, h * H:h * H + H],
                                                  start=(t == 0), stop=(t == MT - 1))
                        mm.then_inc(out_done, 1)
            pe.wait_ge(o_made, 4 * XH + 1)
            for n in range(NC):
                c = n % 4
                pe.wait_ge(w_loaded[c], 16 * (XH + 1 + n // 4))
                for h in range(2):
                    if n:
                        pe.wait_ge(x_made, 2 * n - 1 + h)
                    for k in range(NC):
                        mm = nc.tensor.matmul(gemm[:, h], w_sb[:, c, k], oT[:, k, h * H:h * H + H],
                                              start=(k == 0), stop=(k == NC - 1))
                    mm.then_inc(group_done, 1)
                pe.wait_ge(group_done, NGR * XH + 2 * n + 2)
                pe.sem_inc(w_used, 1)

        def copy_turned(act, hd, s):
            act.wait_ge(turned_done, hd * 4 + (s + 1) + 1)
            if s == 0:
                act.wait_ge(out_done, hd * 4 + 1)
            nc.scalar.activation(pT[:, :, 2 * s * P:2 * s * P + 2 * P], turned[:, s % 2], ACT.Copy).then_inc(pT_made, 1)

        @block.scalar
        def _(act):
            act.wait_ge(m_loaded, 16)
            nc.scalar.activation(msq[:], mT[:], ACT.Square).then_inc(msq_made, 1)
            for k in range(NC):
                act.wait_ge(x_loaded[k // 4], 16)
                if k >= 2:
                    act.wait_ge(sq_used, k - 1)
                nc.scalar.activation(sq[:, k % 2], xT[:, k], ACT.Square).then_inc(sq_made, 1)
            mnorm.root(nc, act)
            norm.root(nc, act)
            nc.scalar.preload_act_table(ACT.Exp)
            with act.Fori(0, XH) as hd:
                for g, (what, i, h) in enumerate(GROUPS):
                    b = g % 2
                    act.wait_ge(group_done, hd * NGR + (g + 1))
                    if what == "q":
                        nc.scalar.activation(qT[:, i, h * H:h * H + H], gemm[:, b], ACT.Copy, scale=1.0 / 16
                                             ).then_inc(evicted[b], 1)
                    elif what == "k":
                        nc.scalar.activation(kT[:, i], gemm[:, b, 0:M], ACT.Copy).then_inc(evicted[b], 1)
                    else:
                        nc.scalar.activation(v[:, i], gemm[:, b, 0:M], ACT.Copy).then_inc(evicted[b], 1)
                for t in range(NT):
                    s, x = t // 2, t % 2
                    act.wait_ge(top_made, hd * 4 + (s + 1))
                    act.wait_ge(turned_done, 1 + (hd * 4 + (s - 1) if s >= 2 else hd * 4))
                    nc.scalar.activation(prob[:, s % 2, x], score[:, s % 2, x], ACT.Exp, bias=top[:, t:t + 1],
                                         accum_out=total[:, t:t + 1]).then_inc(exp_made, 1)
                    if x == 1 and s >= 1:
                        copy_turned(act, hd, s - 1)
                copy_turned(act, hd, 3)
                for c in range(HC):
                    for h in range(2):
                        act.wait_ge(out_done, hd * 4 + (2 * c + h + 1) + 1)
                        nc.scalar.activation(oT[:, ds(hd * HC + c, 1), h * H:h * H + H].rearrange("p a t -> p (a t)"),
                                             out[:, h], ACT.Copy).then_inc(o_made, 1)

        def normalise(dve, hd, s):
            dve.wait_ge(exp_made, hd * 8 + (2 * s + 2) + 1)
            nc.vector.reciprocal(inv[:, 2 * s:2 * s + 2], total[:, 2 * s:2 * s + 2]).then_inc(inv_made, 1)
            dve.wait_ge(inv_made, hd * 4 + (s + 1))
            for x in range(2):
                nc.vector.tensor_scalar(prob[:, s % 2, x], prob[:, s % 2, x], inv[:, 2 * s + x:2 * s + x + 1], None, ALU.mult
                                        ).then_inc(prob_made, 1)

        @block.vector
        def _(dve):
            dve.wait_ge(c_loaded, 32)
            dve.wait_ge(msum_done, 1)
            mnorm.start(nc, dve, [(slice(0, M), out[:, 0, 0:M])], lambda h: msum_read)
            mnorm.finish(nc, dve)
            dve.wait_ge(mnorm.made, 1)
            for k in range(NC):
                nc.vector.scalar_tensor_tensor(out=mT[:, k], in0=mT[:, k], scalar=mg_sb[:, k:k + 1], in1=mnorm.rstd[:],
                                               op0=ALU.mult, op1=ALU.mult).then_inc(mh_made, 1)
            dve.wait_ge(sq_used, NC)
            norm.start(nc, dve, [(slice(h * H, h * H + H), gemm[:, h]) for h in range(2)], lambda h: evicted[h])
            norm.finish(nc, dve)
            dve.wait_ge(norm.made, 1)
            for k in range(NC):
                nc.vector.scalar_tensor_tensor(out=hT[:, k], in0=xT[:, k], scalar=g_sb[:, k:k + 1], in1=norm.rstd[:],
                                               op0=ALU.mult, op1=ALU.mult).then_inc(h_made, 1)
            with dve.Fori(0, XH) as hd:
                for s in range(4):
                    dve.wait_ge(score_done, hd * 4 + (s + 1))
                    nc.vector.tensor_reduce(top[:, 2 * s:2 * s + 2], score[:, s % 2], AX.X, ALU.max, negate=True
                                            ).then_inc(top_made, 1)
                    if s:
                        normalise(dve, hd, s - 1)
                normalise(dve, hd, 3)
            for n in range(NC):
                for h in range(2):
                    hs = slice(h * H, h * H + H)
                    dve.wait_ge(group_done, NGR * XH + 2 * n + h + 1)
                    nc.vector.tensor_tensor(xT[:, n, hs], xT[:, n, hs], gemm[:, h], ALU.add).then_inc(x_made, 1)



def select_phase(nc, x_in, gain, keysT, wstream, h_out, sel_out):
    with Phase(nc, "select") as m:
        K = TOPK
        xT = m.sb("xT", [P, NC, T])
        hT = m.sb("hT", [P, NC, T])
        sq = m.sb("sq", [P, 2, T])
        norm = Rsqrt(m, "norm", T)
        g_sb = m.sb("gain", [P, NC])
        ones, ident = m.sb("ones", [P, P]), m.sb("ident", [P, P])
        keys = m.sb("keys", [P, 2, KEYS])
        w_sb = m.sb("w", [P, 2, NC, P])
        qT = m.sb("qT", [P, 2, T])
        sc = m.sb("sc", [P, 2, NT, KEYS])
        sc2 = m.sb("sc2", [P, 2, NT, KEYS])
        top = m.sb("top", [P, 2, NT, K])
        idx = m.sb("idx", [P, 2, NT, K], U32)
        idxf = m.sb("idxf", [P, 2, NT, K])
        cand = m.sb("cand", [P, NT, K * K])
        cand2 = m.sb("cand2", [P, NT, K * K])
        best = m.sb("best", [P, NT, K])
        bidx = m.sb("bidx", [P, NT, K], U32)
        part = m.sb("part", [P, 2, NT, K], U32)
        partf = m.sb("partf", [P, 2, NT, K])
        iota16 = m.sb("iota16", [P, K])
        hit = m.sb("hit", [P, NT, K, K])
        shifted = m.sb("shifted", [P, NT, K])
        expv = m.sb("expv", [P, NT, K])
        total, inv = m.sb("total", [P, NT]), m.sb("inv", [P, NT])
        res = m.sb("res", [P, 3, NT, PH, K])
        resT = m.sb("resT", [P, 3, T])

        gemm = m.ps("gemm", [P, 2, H])
        scps = m.ps("scps", [P, 2, NT, KEYS])
        turned = m.ps("turned", [P, 2, H])

        x_loaded = [m.sem(f"x_loaded{i}") for i in range(2)]
        c_loaded = m.sem("c_loaded")
        made = m.sem("made")
        sq_made, sq_used, h_made = m.sem("sq_made"), m.sem("sq_used"), m.sem("h_made")
        w_loaded = [m.sem(f"w_loaded{c}") for c in range(2)]
        w_used = m.sem("w_used")
        group_done = m.sem("group_done")
        evicted = [m.sem(f"evicted{b}") for b in range(2)]
        scored = m.sem("scored", start=1)
        sc_made = m.sem("sc_made", start=1)
        first8, index8, cut8, last8 = [m.sem(n) for n in ("first8", "index8", "cut8", "last8")]
        index16 = m.sem("index16", start=1)
        idxf_made = m.sem("idxf_made")
        cand_made = m.sem("cand_made")
        cfirst8, cindex8, ccut8, clast8, cindex16 = [m.sem(n) for n in ("cfirst8", "cindex8", "ccut8", "clast8", "cindex16")]
        part_made, partf_made = m.sem("part_made"), m.sem("partf_made")
        hit_step = m.sem("hit_step")
        shift_made, exp_made, gate_step = m.sem("shift_made"), m.sem("exp_made"), m.sem("gate_step")
        res_made = m.sem("res_made", start=1)
        turn_done, turn_read = m.sem("turn_done"), m.sem("turn_read")
        held = m.sem("held")
        h_stored, stored = m.sem("h_stored"), m.sem("stored")
        block = m.block()

        @block.sync
        def _(sync):
            for i in range(2):
                sync.dma_start(xT[:, 4 * i:4 * i + 4], x_in[:, 4 * i:4 * i + 4]).then_inc(x_loaded[i], 16)
            sync.dma_start(g_sb[:], gain).then_inc(c_loaded, 16)
            sync.dma_start(keys[:], keysT).then_inc(c_loaded, 16)
            for c in range(2):
                sync.dma_start(w_sb[:, c], wstream[c]).then_inc(w_loaded[c], 16)
            sync.wait_ge(h_made, NC)
            sync.dma_start(h_out, hT[:]).then_inc(h_stored, 16)
            with sync.Fori(0, PH - 1) as hd:
                for c in range(2):
                    sync.wait_ge(w_used, hd * 2 + (c + 1))
                    sync.dma_start(w_sb[:, c], wstream[ds(hd * 2 + (2 + c), 1)].rearrange("a p c n -> (a p) c n")
                                   ).then_inc(w_loaded[c], 16)
            sync.wait_ge(turn_read, 6)
            sync.dma_start(sel_out, resT[:]).then_inc(stored, 16)
            sync.wait_ge(h_stored, 16)
            sync.wait_ge(stored, 16)

        @block.gpsimd
        def _(pool):
            nc.gpsimd.memset(ones[:], 1.0).then_inc(made, 1)
            nc.gpsimd.iota(iota16[:], pattern=[[1, K]], base=0, channel_multiplier=0,
                           allow_small_or_imprecise_dtypes=True).then_inc(made, 1)
            pool.wait_ge(made, 2)
            nc.gpsimd.affine_select(out=ident[:], in_=ones[:], pattern=[[-1, P]], compare_op=ALU.is_equal, fill=0.0,
                                    base=0, channel_multiplier=1).then_inc(made, 1)

        @block.tensor
        def _(pe):
            pe.wait_ge(made, 3)
            for k in range(NC):
                pe.wait_ge(sq_made, k + 1)
                for h in range(2):
                    mm = nc.tensor.matmul(gemm[:, h], ones[:], sq[:, k % 2, h * H:h * H + H], start=(k == 0), stop=(k == NC - 1))
                mm.then_inc(sq_used, 1)
            pe.wait_ge(h_made, NC)
            pe.wait_ge(c_loaded, 32)
            with pe.Fori(0, PH) as hd:
                for c in range(2):
                    pe.wait_ge(w_loaded[c], hd * 16 + 16)
                    for h in range(2):
                        pe.wait_ge(evicted[h], hd * 2 + (c + 1))
                        for k in range(NC):
                            mm = nc.tensor.matmul(gemm[:, h], w_sb[:, c, k], hT[:, k, h * H:h * H + H],
                                                  start=(k == 0), stop=(k == NC - 1))
                        mm.then_inc(group_done, 1)
                    pe.wait_ge(group_done, hd * 4 + (2 * c + 2))
                    pe.sem_inc(w_used, 1)
                for c in range(2):
                    pe.wait_ge(evicted[1], hd * 2 + (c + 2))
                    pe.wait_ge(evicted[0], hd * 2 + (c + 2))
                    pe.wait_ge(sc_made, hd * 2 + 1)
                    for t in range(NT):
                        mm = nc.tensor.matmul(scps[:, c, t], qT[:, c, t * P:t * P + P], keys[:, c], start=True, stop=True)
                    mm.then_inc(scored, 1)
            pe.wait_ge(res_made, 3 * PH + 1)
            for g in range(6):
                r, b = g // 2, g % 2
                if g >= 2:
                    pe.wait_ge(turn_read, g - 1)
                for x in range(4):
                    mm = nc.tensor.transpose(turned[:, b, x * P:x * P + P],
                                             res[:, r, 4 * (g % 2) + x].rearrange("p h k -> p (h k)"), ident[:])
                mm.then_inc(turn_done, 1)

        @block.scalar
        def _(act):
            for k in range(NC):
                act.wait_ge(x_loaded[k // 4], 16)
                if k >= 2:
                    act.wait_ge(sq_used, k - 1)
                nc.scalar.activation(sq[:, k % 2], xT[:, k], ACT.Square).then_inc(sq_made, 1)
            norm.root(nc, act)
            nc.scalar.preload_act_table(ACT.Exp)
            with act.Fori(0, PH) as hd:
                for c in range(2):
                    for h in range(2):
                        act.wait_ge(group_done, hd * 4 + (2 * c + h + 1))
                        act.wait_ge(scored, hd * 2 + 1)
                        nc.scalar.activation(qT[:, c, h * H:h * H + H], gemm[:, h], ACT.Copy).then_inc(evicted[h], 1)
                for c in range(2):
                    act.wait_ge(scored, hd * 2 + (c + 1) + 1)
                    act.wait_ge(index16, hd * 16 + 1)
                    nc.scalar.activation(sc[:, c], scps[:, c], ACT.Copy).then_inc(sc_made, 1)
                act.wait_ge(shift_made, hd + 1)
                nc.scalar.activation(expv[:], shifted[:], ACT.Exp).then_inc(exp_made, 1)
            for g in range(6):
                act.wait_ge(turn_done, g + 1)
                nc.scalar.activation(resT[:, g // 2, (g % 2) * H:(g % 2) * H + H], turned[:, g % 2], ACT.Copy).then_inc(turn_read, 1)

        def alone(dve, sem, value):
            dve.wait_ge(sem, value)
            dve.sem_inc(held, 1)

        @block.vector
        def _(dve):
            dve.wait_ge(sq_used, NC)
            norm.start(nc, dve, [(slice(h * H, h * H + H), gemm[:, h]) for h in range(2)], lambda h: evicted[h])
            norm.finish(nc, dve)
            dve.wait_ge(norm.made, 1)
            dve.wait_ge(c_loaded, 32)
            for k in range(NC):
                nc.vector.scalar_tensor_tensor(out=hT[:, k], in0=xT[:, k], scalar=g_sb[:, k:k + 1], in1=norm.rstd[:],
                                               op0=ALU.mult, op1=ALU.mult).then_inc(h_made, 1)
            units = [(c, t) for c in range(2) for t in range(NT)]
            NU = len(units)
            with dve.Fori(0, PH) as hd:
                alone(dve, sc_made, hd * 2 + 2 + 1)
                for c, t in units:
                    nc.vector.max(top[:, c, t, 0:8], sc[:, c, t]).then_inc(first8, 1)
                alone(dve, first8, hd * NU + NU)
                for c, t in units:
                    nc.vector.max_index(idx[:, c, t, 0:8], top[:, c, t, 0:8], sc[:, c, t]).then_inc(index8, 1)
                    nc.vector.match_replace(sc2[:, c, t], top[:, c, t, 0:8], sc[:, c, t], LOWEST).then_inc(cut8, 1)
                alone(dve, cut8, hd * NU + NU)
                for c, t in units:
                    nc.vector.max(top[:, c, t, 8:16], sc2[:, c, t]).then_inc(last8, 1)
                alone(dve, last8, hd * NU + NU)
                for c, t in units:
                    nc.vector.max_index(idx[:, c, t, 8:16], top[:, c, t, 8:16], sc2[:, c, t]).then_inc(index16, 1)
                for t in range(NT):
                    nc.vector.tensor_tensor(cand[:, t].rearrange("p (a b) -> p a b", b=K),
                                            top[:, 0, t].unsqueeze(2).to_broadcast([P, K, K]),
                                            top[:, 1, t].unsqueeze(1).to_broadcast([P, K, K]), ALU.add).then_inc(cand_made, 1)
                dve.wait_ge(index8, hd * NU + NU)
                dve.wait_ge(index16, hd * NU + NU + 1)
                nc.vector.tensor_copy(idxf[:], idx[:]).then_inc(idxf_made, 1)
                alone(dve, cand_made, hd * NT + NT)
                for t in range(NT):
                    nc.vector.max(best[:, t, 0:8], cand[:, t]).then_inc(cfirst8, 1)
                alone(dve, cfirst8, hd * NT + NT)
                for t in range(NT):
                    nc.vector.max_index(bidx[:, t, 0:8], best[:, t, 0:8], cand[:, t]).then_inc(cindex8, 1)
                    nc.vector.match_replace(cand2[:, t], best[:, t, 0:8], cand[:, t], LOWEST).then_inc(ccut8, 1)
                alone(dve, ccut8, hd * NT + NT)
                for t in range(NT):
                    nc.vector.max(best[:, t, 8:16], cand2[:, t]).then_inc(clast8, 1)
                alone(dve, clast8, hd * NT + NT)
                for t in range(NT):
                    nc.vector.max_index(bidx[:, t, 8:16], best[:, t, 8:16], cand2[:, t]).then_inc(cindex16, 1)
                nc.vector.tensor_tensor(shifted[:], best[:], best[:, :, 0:1].to_broadcast([P, NT, K]), ALU.subtract
                                        ).then_inc(shift_made, 1)
                dve.wait_ge(cindex8, hd * NT + NT)
                dve.wait_ge(cindex16, hd * NT + NT)
                nc.vector.tensor_single_scalar(part[:, 0], bidx[:], 4, ALU.logical_shift_right).then_inc(part_made, 1)
                nc.vector.tensor_single_scalar(part[:, 1], bidx[:], K - 1, ALU.bitwise_and).then_inc(part_made, 1)
                dve.wait_ge(part_made, hd * 2 + 2)
                nc.vector.tensor_copy(partf[:], part[:]).then_inc(partf_made, 1)
                dve.wait_ge(partf_made, hd + 1)
                dve.wait_ge(idxf_made, hd + 1)
                for c in range(2):
                    if c == 0:
                        dve.wait_ge(made, 3)
                    dve.wait_ge(res_made, hd * 3 + c + 1)
                    nc.vector.tensor_tensor(hit[:], partf[:, c].unsqueeze(3).to_broadcast([P, NT, K, K]),
                                            iota16[:].unsqueeze(1).unsqueeze(1).to_broadcast([P, NT, K, K]), ALU.is_equal
                                            ).then_inc(hit_step, 1)
                    dve.wait_ge(hit_step, hd * 4 + (2 * c + 1))
                    nc.vector.tensor_tensor(hit[:], hit[:], idxf[:, c].unsqueeze(2).to_broadcast([P, NT, K, K]), ALU.mult
                                            ).then_inc(hit_step, 1)
                    dve.wait_ge(hit_step, hd * 4 + (2 * c + 2))
                    nc.vector.tensor_reduce(res[:, c, :, ds(hd, 1), :].rearrange("p t a k -> p t (a k)"), hit[:], AX.X, ALU.add
                                            ).then_inc(res_made, 1)
                dve.wait_ge(exp_made, hd + 1)
                nc.vector.tensor_reduce(total[:], expv[:], AX.X, ALU.add).then_inc(gate_step, 1)
                dve.wait_ge(gate_step, hd * 2 + 1)
                nc.vector.reciprocal(inv[:], total[:]).then_inc(gate_step, 1)
                dve.wait_ge(gate_step, hd * 2 + 2)
                nc.vector.tensor_tensor(res[:, 2, :, ds(hd, 1), :].rearrange("p t a k -> p t (a k)"), expv[:],
                                        inv[:].unsqueeze(2).to_broadcast([P, NT, K]), ALU.mult).then_inc(res_made, 1)


def spread_phase(nc, sel_in, g_out):
    with Phase(nc, "spread") as m:
        B = 16
        S = 8
        NS = B // S
        sel = m.sb("sel", [P, 3, T])
        now = m.sb("now", [P, 3, B])
        iota = m.sb("iota", [P, KEYS])
        one1 = m.sb("one1", [P, NS, S, KEYS])
        one2 = m.sb("one2", [P, NS, S, KEYS])
        stage = m.sb("stage", [P, 2, KEYS, P])
        ps = m.ps("g", [P, NS, 2, 4, KEYS])

        loaded = m.sem("loaded")
        iota_made = m.sem("iota_made")
        now_made = m.sem("now_made")
        ones_made = m.sem("ones_made", start=1)
        g_done = m.sem("g_done", start=1)
        staged = m.sem("staged", start=1)
        stored = [m.sem(f"stored{b}", start=1) for b in range(2)]
        block = m.block()
        STEPS = P // B

        def tiles(eng, body):
            with eng.Fori(0, NT // 2) as tt:
                for par in range(2):
                    with eng.Fori(0, STEPS) as st:
                        body(tt, par, st)

        def steps(tt, par, st):
            return tt * (2 * STEPS) + (st + par * STEPS)

        @block.sync
        def _(sync):
            sync.dma_start(sel[:], sel_in).then_inc(loaded, 16)
            with sync.Fori(0, NT // 2) as tt:
                for par in range(2):
                    sync.wait_ge(staged, tt * (2 * STEPS * 4) + (par + 1) * STEPS * 4 + 1)
                    sync.dma_start(g_out.rearrange("a p t -> p a t")[:, :, ds(tt * (2 * P) + par * P, P)],
                                   stage[:, par]).then_inc(stored[par], 16)
            for b in range(2):
                sync.wait_ge(stored[b], 16 * (NT // 2) + 1)

        @block.gpsimd
        def _(pool):
            nc.gpsimd.iota(iota[:], pattern=[[1, KEYS]], base=0, channel_multiplier=0,
                           allow_small_or_imprecise_dtypes=True).then_inc(iota_made, 1)

        @block.vector
        def _(dve):
            dve.wait_ge(loaded, 16)
            dve.wait_ge(iota_made, 1)

            def body(tt, par, st):
                n = steps(tt, par, st)
                dve.wait_ge(ones_made, n * NS + 1)
                nc.vector.tensor_copy(now[:], sel[:, :, ds(n * B, B)]).then_inc(now_made, 1)
                dve.wait_ge(now_made, n + 1)
                for s in range(NS):
                    dve.wait_ge(g_done, n * (2 * NS) + 1)
                    for x in range(S):
                        t = s * S + x
                        nc.vector.tensor_scalar(one1[:, s, x], iota[:], now[:, 0, t:t + 1], None, ALU.is_equal)
                        last = nc.vector.tensor_scalar(one2[:, s, x], iota[:], now[:, 1, t:t + 1], now[:, 2, t:t + 1],
                                                       ALU.is_equal, ALU.mult)
                    last.then_inc(ones_made, 1)

            tiles(dve, body)

        @block.tensor
        def _(pe):
            def body(tt, par, st):
                n = steps(tt, par, st)
                for s in range(NS):
                    pe.wait_ge(ones_made, n * NS + (s + 1) + 1)
                    for b in range(2):
                        pe.wait_ge(staged, n * (2 * NS) + 1)
                        for x in range(4):
                            mm = nc.tensor.matmul(ps[:, s, b, x], one1[:, s, 4 * b + x], one2[:, s, 4 * b + x],
                                                  start=True, stop=True)
                        mm.then_inc(g_done, 1)

            tiles(pe, body)

        @block.scalar
        def _(act):
            def body(tt, par, st):
                n = steps(tt, par, st)
                act.wait_ge(stored[par], tt * 16 + 1)
                for s in range(NS):
                    for b in range(2):
                        act.wait_ge(g_done, n * (2 * NS) + (2 * s + b + 1) + 1)
                        nc.scalar.activation(stage[:, par, :, ds(st * B + (s * S + 4 * b), 4)],
                                             ps[:, s, b].rearrange("p t i -> p i t"), ACT.Copy).then_inc(staged, 1)

            tiles(act, body)


def expert_phase(nc, h_in, x_in, g_in, u_stream, v_stream, final_gain, out):
    with Phase(nc, "expert") as m:
        E = 2
        NG = KEYS // E
        NQ = 4
        QC = NC // NQ
        QG = 2 * QC
        SG = NQ * QG
        hhi = m.sb("hhi", [P, NC, T], F32R)
        hlo = m.sb("hlo", [P, NC, T], F32R)
        acc = m.sb("acc", [P, NC, T])
        g_sb = m.sb("gain", [P, NC])
        ones = m.sb("ones", [P, P])
        uraw = m.sb("uraw", [P, E, NC, P])
        uhi = m.sb("uhi", [P, E, NC, P], F32R)
        ulo = m.sb("ulo", [P, E, NC, P], F32R)
        vraw = m.sb("vraw", [P, NQ, E, QC * P])
        vhi = m.sb("vhi", [P, NQ, E, QC * P], F32R)
        vlo = m.sb("vlo", [P, NQ, E, QC * P], F32R)
        graw = m.sb("graw", [P, E, T])
        act = m.sb("act", [P, E, T])
        ahi = m.sb("ahi", [P, 2, E, T], F32R)
        alo = m.sb("alo", [P, 2, E, T], F32R)

        aps = m.ps("a", [P, E, 2, H])
        ops = m.ps("o", [P, QC, 2, H])

        h_loaded = [m.sem(f"h_loaded{b}") for b in range(2)]
        x_loaded, c_loaded = m.sem("x_loaded"), m.sem("c_loaded")
        ones_made = m.sem("ones_made")
        hhi_made, hlo_made = m.sem("hhi_made"), m.sem("hlo_made")
        u_loaded = [m.sem(f"u_loaded{e}") for e in range(E)]
        g_loaded = [m.sem(f"g_loaded{e}") for e in range(E)]
        v_loaded = [m.sem(f"v_loaded{q}") for q in range(NQ)]
        uhi_made, ulo_made = m.sem("uhi_made"), m.sem("ulo_made")
        vhi_made, vlo_made = m.sem("vhi_made"), m.sem("vlo_made")
        a_done = m.sem("a_done")
        gelu_made = m.sem("gelu_made")
        gated = m.sem("gated")
        ahi_made, alo_made = m.sem("ahi_made"), m.sem("alo_made", start=1)
        o_done = m.sem("o_done", start=1)
        added = m.sem("added")
        sq_made, sq_used, sum_read = m.sem("sq_made"), m.sem("sq_used"), [m.sem(f"sum_read{h}") for h in range(2)]
        step, rooted = m.sem("step"), m.sem("rooted")
        y_made, stored = m.sem("y_made"), m.sem("stored")
        block = m.block()

        def groups(eng, body):
            with eng.Fori(0, NG // 2 - 1) as gg:
                for par in range(2):
                    body(gg * 2 + par, par, False)
            for par in range(2):
                body(NG - 2 + par, par, par == 1)

        @block.sync
        def _(sync):
            for k in range(NC):
                if k >= 2:
                    sync.wait_ge(hhi_made, k - 1)
                    sync.wait_ge(hlo_made, k - 1)
                sync.dma_start(act[:, k % 2], h_in[:, k]).then_inc(h_loaded[k % 2], 16)
                if k == 1:
                    for e in range(E):
                        sync.dma_start(uraw[:, e], u_stream[e]).then_inc(u_loaded[e], 16)
            for e in range(E):
                sync.dma_start(graw[:, e], g_in[e]).then_inc(g_loaded[e], 16)
            for q in range(NQ):
                sync.dma_start(vraw[:, q], v_stream[0, q]).then_inc(v_loaded[q], 16)
            sync.dma_start(acc[:], x_in).then_inc(x_loaded, 16)
            sync.dma_start(g_sb[:], final_gain).then_inc(c_loaded, 16)
            with sync.Fori(0, NG - 1) as g:
                for e in range(E):
                    sync.wait_ge(uhi_made, g * E + (e + 1))
                    sync.wait_ge(ulo_made, g * E + (e + 1))
                    sync.dma_start(uraw[:, e], u_stream[ds(g * E + (E + e), 1)].rearrange("a p c n -> (a p) c n")
                                   ).then_inc(u_loaded[e], 16)
                for e in range(E):
                    sync.wait_ge(gated, g * E + (e + 1))
                    sync.dma_start(graw[:, e], g_in[ds(g * E + (E + e), 1)].rearrange("a p t -> (a p) t")
                                   ).then_inc(g_loaded[e], 16)
                for q in range(NQ):
                    sync.wait_ge(vhi_made, g * NQ + (q + 1))
                    sync.wait_ge(vlo_made, g * NQ + (q + 1))
                    sync.dma_start(vraw[:, q], v_stream[ds(g + 1, 1), q].rearrange("a p e n -> (a p) e n")
                                   ).then_inc(v_loaded[q], 16)
            for k in range(NC):
                sync.wait_ge(y_made, k + 1)
                sync.dma_start(out[:, k], acc[:, k]).then_inc(stored, 16)
            sync.wait_ge(stored, 16 * NC)

        def split_low(eng, low, raw, high):
            return eng.tensor_tensor(low, raw, high.bitcast(F32), ALU.subtract)

        @block.gpsimd
        def _(pool):
            nc.gpsimd.memset(ones[:], 1.0).then_inc(ones_made, 1)
            for e in range(E):
                pool.wait_ge(uhi_made, e + 1)
                split_low(nc.gpsimd, ulo[:, e], uraw[:, e], uhi[:, e]).then_inc(ulo_made, 1)

            def body(g, par, last):
                if not last:
                    for e in range(E):
                        pool.wait_ge(uhi_made, g * E + (E + e + 1))
                        split_low(nc.gpsimd, ulo[:, e], uraw[:, e], uhi[:, e]).then_inc(ulo_made, 1)
                for q in range(NQ):
                    pool.wait_ge(vhi_made, g * NQ + (q + 1))
                    split_low(nc.gpsimd, vlo[:, q], vraw[:, q], vhi[:, q]).then_inc(vlo_made, 1)

            groups(pool, body)

        @block.scalar
        def _(act_eng):
            for e in range(E):
                act_eng.wait_ge(u_loaded[e], 16)
                nc.scalar.activation(uhi[:, e], uraw[:, e], ACT.Copy).then_inc(uhi_made, 1)
            for k in range(NC):
                act_eng.wait_ge(h_loaded[k % 2], 16 * (k // 2 + 1))
                nc.scalar.activation(hhi[:, k], act[:, k % 2], ACT.Copy).then_inc(hhi_made, 1)
            act_eng.wait_ge(hlo_made, NC)
            nc.scalar.preload_act_table(ACT.Gelu_apprx_tanh)

            def body(g, par, last):
                for e in range(E):
                    for h in range(2):
                        act_eng.wait_ge(a_done, g * (2 * E) + (2 * e + h + 1))
                        act_eng.wait_ge(alo_made, g * E + 1)
                        nc.scalar.activation(act[:, e, h * H:h * H + H], aps[:, e, h], ACT.Gelu_apprx_tanh
                                             ).then_inc(gelu_made, 1)
                    if not last:
                        act_eng.wait_ge(u_loaded[e], g * 16 + 32)
                        act_eng.wait_ge(ulo_made, g * E + (e + 1))
                        nc.scalar.activation(uhi[:, e], uraw[:, e], ACT.Copy).then_inc(uhi_made, 1)
                    act_eng.wait_ge(gated, g * E + (e + 1))
                    act_eng.wait_ge(o_done, g * SG + 1)
                    nc.scalar.activation(ahi[:, par, e], act[:, e], ACT.Copy).then_inc(ahi_made, 1)
                for q in range(NQ):
                    act_eng.wait_ge(v_loaded[q], g * 16 + 16)
                    act_eng.wait_ge(o_done, g * SG + (q + 1) * QG + 1)
                    nc.scalar.activation(vhi[:, q], vraw[:, q], ACT.Copy).then_inc(vhi_made, 1)

            groups(act_eng, body)
            for k in range(NC):
                act_eng.wait_ge(added, QG + NG * SG)
                if k >= 2:
                    act_eng.wait_ge(sq_used, k - 1)
                nc.scalar.activation(act[:, k % 2], acc[:, k], ACT.Square).then_inc(sq_made, 1)
            act_eng.wait_ge(step, 1)
            nc.scalar.activation(graw[:, 1], act[:, 1], ACT.Sqrt).then_inc(rooted, 1)

        @block.vector
        def _(dve):
            for k in range(NC):
                dve.wait_ge(hhi_made, k + 1)
                split_low(nc.vector, hlo[:, k], act[:, k % 2], hhi[:, k]).then_inc(hlo_made, 1)
            dve.wait_ge(x_loaded, 16)

            def body(g, par, last):
                for e in range(E):
                    dve.wait_ge(gelu_made, g * (2 * E) + (2 * e + 2))
                    dve.wait_ge(g_loaded[e], g * 16 + 16)
                    nc.vector.tensor_tensor(act[:, e], act[:, e], graw[:, e], ALU.mult).then_inc(gated, 1)
                    dve.wait_ge(ahi_made, g * E + (e + 1))
                    split_low(nc.vector, alo[:, par, e], act[:, e], ahi[:, par, e]).then_inc(alo_made, 1)
                for w in range(SG):
                    q, d, h = w // QG, w // 2 % QC, w % 2
                    k = q * QC + d
                    dve.wait_ge(o_done, g * SG + (SG + w + 1) + 1)
                    nc.vector.tensor_tensor(acc[:, k, h * H:h * H + H], acc[:, k, h * H:h * H + H], ops[:, d, h], ALU.add
                                            ).then_inc(added, 1)

            groups(dve, body)
            dve.wait_ge(sq_used, NC)
            mean, inv, rstd = graw[:, 0], act[:, 1], graw[:, 1]
            for h in range(2):
                nc.vector.tensor_scalar(mean[:, h * H:h * H + H], aps[:, 0, h], 1.0 / D, EPS, ALU.mult, ALU.add
                                        ).then_inc(sum_read[h], 1)
                dve.wait_ge(sum_read[h], 1)
            nc.vector.reciprocal(inv, mean).then_inc(step, 1)
            dve.wait_ge(rooted, 1)
            nc.vector.tensor_tensor(inv, mean, rstd, ALU.mult).then_inc(step, 1)
            dve.wait_ge(step, 2)
            nc.vector.tensor_tensor(inv, inv, rstd, ALU.mult).then_inc(step, 1)
            dve.wait_ge(step, 3)
            nc.vector.tensor_scalar(inv, inv, -0.5, 1.5, ALU.mult, ALU.add).then_inc(step, 1)
            dve.wait_ge(step, 4)
            nc.vector.tensor_tensor(rstd, rstd, inv, ALU.mult).then_inc(step, 1)
            dve.wait_ge(step, 5)
            dve.wait_ge(c_loaded, 16)
            for k in range(NC):
                nc.vector.scalar_tensor_tensor(out=acc[:, k], in0=acc[:, k], scalar=g_sb[:, k:k + 1], in1=rstd,
                                               op0=ALU.mult, op1=ALU.mult).then_inc(y_made, 1)

        @block.tensor
        def _(pe):
            pe.sem_inc(o_done, SG)
            pe.sem_inc(added, QG)
            pe.wait_ge(hlo_made, NC)

            def stage1(g):
                for e in range(E):
                    pe.wait_ge(uhi_made, g * E + (e + 1))
                    pe.wait_ge(ulo_made, g * E + (e + 1))
                    for h in range(2):
                        if not (isinstance(g, int) and g == 0):
                            pe.wait_ge(gelu_made, g * (2 * E) + (2 * e + h + 1 - 2 * E))
                        hs = slice(h * H, h * H + H)
                        for k in range(NC):
                            nc.tensor.matmul(aps[:, e, h], uhi[:, e, k], hhi[:, k, hs], start=(k == 0), stop=False)
                            nc.tensor.matmul(aps[:, e, h], uhi[:, e, k], hlo[:, k, hs], start=False, stop=False)
                            mm = nc.tensor.matmul(aps[:, e, h], ulo[:, e, k], hhi[:, k, hs], start=False, stop=(k == NC - 1))
                        mm.then_inc(a_done, 1)

            def stage2(g, par):
                pe.wait_ge(ahi_made, g * E + E)
                pe.wait_ge(alo_made, g * E + E + 1)
                for w in range(SG):
                    q, d, h = w // QG, w // 2 % QC, w % 2
                    if w % QG == 0:
                        pe.wait_ge(vlo_made, g * NQ + (q + 1))
                    pe.wait_ge(added, g * SG + (w + 1))
                    hs, dp = slice(h * H, h * H + H), slice(d * P, d * P + P)
                    for e in range(E):
                        nc.tensor.matmul(ops[:, d, h], vhi[:, q, e, dp], ahi[:, par, e, hs], start=(e == 0), stop=False)
                        nc.tensor.matmul(ops[:, d, h], vhi[:, q, e, dp], alo[:, par, e, hs], start=False, stop=False)
                        mm = nc.tensor.matmul(ops[:, d, h], vlo[:, q, e, dp], ahi[:, par, e, hs], start=False, stop=(e == E - 1))
                    mm.then_inc(o_done, 1)

            stage1(0)

            def body(g, par, last):
                if not last:
                    stage1(g + 1)
                stage2(g, par)

            groups(pe, body)
            pe.wait_ge(ones_made, 1)
            for k in range(NC):
                pe.wait_ge(sq_made, k + 1)
                for h in range(2):
                    mm = nc.tensor.matmul(aps[:, 0, h], ones[:], act[:, k % 2, h * H:h * H + H], start=(k == 0), stop=(k == NC - 1))
                mm.then_inc(sq_used, 1)


def build(nc, a, out):
    def scratch(name, shape):
        return nc.dram_tensor(name, shape, F32).ap()

    full = [P, NC, T]
    h1, conv, attn = scratch("h1", full), scratch("conv", full), scratch("attn", full)
    x1, x2, h3 = scratch("x1", full), scratch("x2", full), scratch("h3", full)
    sel, gates = scratch("sel", [P, 3, T]), scratch("gates", [KEYS, P, T])
    mixer_phase(nc, a["x"], a["mix_gain"], a["w_mix"], a["conv_w"], h1, conv, attn)
    merge_phase(nc, a["x"], h1, conv, attn, a["w_merge"], a["ln_g"], a["ln_b"], a["gate_b"], x1)
    cross_attention_phase(nc, x1, a["x_gain"], a["mem"], a["mem_gain"], a["w_cross"], x2)
    select_phase(nc, x2, a["ffn_gain"], a["keys"], a["w_query"], h3, sel)
    spread_phase(nc, sel, gates)
    expert_phase(nc, h3, x2, gates, a["peer_u"], a["peer_v"], a["final_gain"], out)


def kernel(x, mem, norm_mix_g, w_in, b_gate, conv_dw_w, conv_dw_b, conv_ln_g, conv_ln_b,
           w_conv_out, w_attn_out, w_out, norm_xattn_g, norm_mem_g, w_xq, w_xkv, w_xo,
           norm_ffn_g, w_peer_q, peer_sub_keys, peer_u, peer_v, norm_final_g):
    import concourse.bacc as bacc
    from concourse.bass_utils import run_bass_kernel_spmd

    def channels(t):
        return t.T.reshape(NC, P, -1).transpose(1, 0, 2)

    def vector(t):
        return t.reshape(-1, P).T

    def chunks(w):
        return w.reshape(NC, P, -1, P).transpose(2, 1, 0, 3)

    w = np.asarray(w_in)[0]
    val, gate, q, k, v, g_conv, g_attn = [chunks(w[:, i * D:(i + 1) * D]) for i in range(7)]
    xq, xo = chunks(np.asarray(w_xq)[0]), chunks(np.asarray(w_xo)[0])
    xk, xv = [chunks(np.asarray(w_xkv)[0][:, i * D:(i + 1) * D]) for i in range(2)]
    per_head = [t.reshape(XH, 2, P, NC, P) for t in (xq, xk, xv)]
    flat = (-1, P, NC, P)
    arrays = {
        "x": channels(np.asarray(x)[0]),
        "mem": channels(np.asarray(mem)[0]),
        "mix_gain": vector(np.asarray(norm_mix_g)[0]),
        "w_mix": np.stack([gate, val, q, k, v], 1).reshape(flat),
        "conv_w": np.concatenate([np.asarray(conv_dw_w)[0], np.asarray(conv_dw_b)]).T.reshape(NC, P, TAPS + 1).transpose(1, 0, 2),
        "w_merge": np.concatenate([np.stack([g_conv, chunks(np.asarray(w_conv_out)[0]), g_attn,
                                             chunks(np.asarray(w_attn_out)[0])], 1).reshape(flat),
                                   chunks(np.asarray(w_out)[0])]),
        "ln_g": vector(np.asarray(conv_ln_g)[0]),
        "ln_b": vector(np.asarray(conv_ln_b)[0]),
        "gate_b": np.asarray(b_gate)[0].reshape(2, NC, P).transpose(2, 0, 1),
        "x_gain": vector(np.asarray(norm_xattn_g)[0]),
        "mem_gain": vector(np.asarray(norm_mem_g)[0]),
        "w_cross": np.concatenate([np.stack(per_head, 1).reshape(flat), xo]),
        "ffn_gain": vector(np.asarray(norm_ffn_g)[0]),
        "w_query": chunks(np.asarray(w_peer_q)[0]),
        "keys": np.asarray(peer_sub_keys)[0].transpose(2, 0, 1),
        "peer_u": np.asarray(peer_u)[0].reshape(P, KEYS, NC, P).transpose(1, 3, 2, 0),
        "peer_v": np.asarray(peer_v)[0].reshape(P, KEYS // 2, 2, 4, D // 4).transpose(1, 3, 0, 2, 4),
        "final_gain": vector(np.asarray(norm_final_g)),
    }
    arrays = {f"in_{n}": np.ascontiguousarray(t) for n, t in arrays.items()}
    nc = bacc.Bacc("TRN2", target_bir_lowering=False, num_devices=1)
    aps = {n: nc.dram_tensor(n, list(t.shape), F32, kind="ExternalInput").ap() for n, t in arrays.items()}
    out = nc.dram_tensor("out", [P, NC, T], F32, kind="ExternalOutput").ap()
    build(nc, {n[3:]: ap for n, ap in aps.items()}, out)
    r = run_bass_kernel_spmd(nc, [arrays], core_ids=[0])
    got = r.results[0]["out"]
    return np.ascontiguousarray(got.transpose(1, 0, 2).reshape(D, T).T)[None]
```

```python
from contextlib import ExitStack

import numpy as np
import concourse.bass as bass
from concourse import mybir

P = 128
D = 1024
T = 1024
M = 256
NC = D // P
NT = T // P
H = 512
TAPS = 31
PAD = TAPS - 1
SELECT_TILES = 32
SB_HD = 64
XH = 4
PH = 8
KEYS = 128
TOPK = 16
EPS = 1e-6
LOWEST = -3.4028235e38

F32 = mybir.dt.float32
F32R = mybir.dt.float32r
BF16 = mybir.dt.bfloat16
U32 = mybir.dt.uint32
ALU = mybir.AluOpType
ACT = mybir.ActivationFunctionType
AX = mybir.AxisListType
ds = bass.ds


class Phase:

    def __init__(self, nc, tag):
        self.nc, self.tag, self.tensors, self.sems = nc, tag, ExitStack(), []

    def __enter__(self):
        return self

    def sb(self, name, shape, dt=F32):
        return self.tensors.enter_context(self.nc.sbuf_tensor(f"{self.tag}_{name}", shape, dt))

    def ps(self, name, shape):
        return self.tensors.enter_context(self.nc.psum_tensor(f"{self.tag}_{name}", shape, F32))

    def sem(self, name, start=0):
        self.sems.append(self.nc.alloc_semaphore(name=f"{self.tag}_{name}"))
        if start:
            self.nc.gpsimd.sem_inc(self.sems[-1], start)
        return self.sems[-1]

    def block(self):
        self.nc.all_engine_barrier()
        return self.tensors.enter_context(self.nc.Block())

    def __exit__(self, *error):
        self.tensors.close()
        if not any(error):
            self.nc.clear_and_free_semaphores(self.sems)
            self.nc.all_engine_barrier()


class Rsqrt:

    def __init__(self, m, name, n):
        self.mean, self.inv = m.sb(f"{name}_mean", [P, n]), m.sb(f"{name}_inv", [P, n])
        self.rstd = m.sb(f"{name}_rstd", [P, n])
        self.step = m.sem(f"{name}_step")
        self.rooted = m.sem(f"{name}_rooted")
        self.made = m.sem(f"{name}_made")

    def start(self, nc, dve, sums, psum_free):
        for i, (cols, src) in enumerate(sums):
            nc.vector.tensor_scalar(self.mean[:, cols], src, 1.0 / D, EPS, ALU.mult, ALU.add).then_inc(psum_free(i), 1)
        for i in range(len(sums)):
            dve.wait_ge(psum_free(i), 1)
        nc.vector.reciprocal(self.inv[:], self.mean[:]).then_inc(self.step, 1)

    def root(self, nc, act):
        act.wait_ge(self.step, 1)
        nc.scalar.activation(self.rstd[:], self.inv[:], ACT.Sqrt).then_inc(self.rooted, 1)

    def finish(self, nc, dve):
        dve.wait_ge(self.rooted, 1)
        nc.vector.tensor_tensor(self.inv[:], self.mean[:], self.rstd[:], ALU.mult).then_inc(self.step, 1)
        dve.wait_ge(self.step, 2)
        nc.vector.tensor_tensor(self.inv[:], self.inv[:], self.rstd[:], ALU.mult).then_inc(self.step, 1)
        dve.wait_ge(self.step, 3)
        nc.vector.tensor_scalar(self.inv[:], self.inv[:], -0.5, 1.5, ALU.mult, ALU.add).then_inc(self.step, 1)
        dve.wait_ge(self.step, 4)
        nc.vector.tensor_tensor(self.rstd[:], self.rstd[:], self.inv[:], ALU.mult).then_inc(self.made, 1)


def three_pass(nc, out, terms):
    for i, (whi, wlo, xhi, xlo) in enumerate(terms):
        nc.tensor.matmul(out, whi, xhi, start=(i == 0), stop=False)
        nc.tensor.matmul(out, whi, xlo, start=False, stop=False)
        mm = nc.tensor.matmul(out, wlo, xhi, start=False, stop=(i == len(terms) - 1))
    return mm


def mixer_phase(nc, xT, gain, wstream, conv_w, h_out, y_out, attn_out):
    with Phase(nc, "mix") as m:
        NW = 5
        NG = 2 * NW
        hT = m.sb("hT", [P, NC, T])
        xbuf = m.sb("xbuf", [P, NC, T])
        sq = m.sb("sq", [P, 2, T])
        norm = Rsqrt(m, "norm", T)
        g_sb = m.sb("gain", [P, NC])
        ones = m.sb("ones", [P, P])
        tri = m.sb("tri", [P, P])
        rest = m.sb("rest", [P, P])
        causal = m.sb("causal", [P, P])
        w_sb = m.sb("w", [P, NW, NC, P])
        egate = m.sb("egate", [P, T])
        den = m.sb("den", [P, T])
        u = m.sb("u", [P, 2, PAD + T])
        ybuf = m.sb("ybuf", [P, 2, T])
        cw = m.sb("cw", [P, NC, TAPS + 1])
        cwj = m.sb("cwj", [P, TAPS + 1])
        qT = m.sb("qT", [P, 2, T])
        kT = m.sb("kT", [P, 2, T])
        v = m.sb("v", [P, 2, NT, P])
        absz = m.sb("absz", [P, 2, H])
        ex = m.sb("exp", [P, 2, H])
        ln = m.sb("ln", [P, 2, H])
        sp = m.sb("softplus", [P, 2, H])
        ls = m.sb("logsig", [P, 2, H])
        lw = m.sb("logw", [P, 2, H])
        wt = m.sb("weight", [P, 2, H])
        oT = m.sb("oT", [P, 2, T])

        gemm = m.ps("gemm", [P, 2, H])
        zps = m.ps("z", [P, 2, H])
        cps = m.ps("c", [P, 2, H])
        ops = m.ps("o", [P, 2, H])

        x_loaded = [m.sem(f"x_loaded{i}") for i in range(2)]
        c_loaded = m.sem("c_loaded")
        const_made = m.sem("const_made")
        sq_made = m.sem("sq_made")
        sum_done = m.sem("sum_done")
        h_made = m.sem("h_made")
        w_loaded = [m.sem(f"w_loaded{c}") for c in range(NW)]
        w_used = m.sem("w_used")
        group_done = m.sem("group_done")
        evicted = [m.sem(f"evicted{b}") for b in range(2)]
        u_step = m.sem("u_step")
        u_made = m.sem("u_made", start=1)
        cwj_made = m.sem("cwj_made")
        conv_step = m.sem("conv_step")
        h_stored = m.sem("h_stored")
        y_stored = [m.sem(f"y_stored{b}", start=1) for b in range(2)]
        o_copied = m.sem("o_copied", start=1)
        o_stored = [m.sem(f"o_stored{b}", start=1) for b in range(2)]
        z_done = [m.sem(f"z_done{s}") for s in range(2)]
        act_step = [m.sem(f"act_step{s}") for s in range(2)]
        ln_done = [m.sem(f"ln_done{s}") for s in range(2)]
        sp_raw = [m.sem(f"sp_raw{s}") for s in range(2)]
        sp_done = [m.sem(f"sp_done{s}") for s in range(2)]
        c_done = [m.sem(f"c_done{s}") for s in range(2)]
        ls_done = [m.sem(f"ls_done{s}", start=1) for s in range(2)]
        lw_done = [m.sem(f"lw_done{s}", start=1) for s in range(2)]
        wt_raw = [m.sem(f"wt_raw{s}") for s in range(2)]
        wt_done = [m.sem(f"wt_done{s}", start=1) for s in range(2)]
        sp_used = [m.sem(f"sp_used{s}", start=1) for s in range(2)]
        pv_done = [m.sem(f"pv_done{s}", start=1) for s in range(2)]

        cells = [(qh, kb) for qh in range(2) for kb in range(4 * qh + 3, -1, -1)]
        NCELL = len(cells)
        col0 = [max(0, kb - 4 * qh) * P for qh, kb in cells]
        masked = [kb >= 4 * qh for qh, kb in cells]
        NMASK = sum(masked)
        opens = [kb == 4 * qh + 3 for qh, kb in cells]
        closes = [kb == 0 for qh, kb in cells]

        def pairs(eng, body):
            with eng.Fori(0, NC // 2 - 1) as jj:
                for par in range(2):
                    body(jj * 2 + par, par, jj, False)
            for par in range(2):
                body(NC - 2 + par, par, NC // 2 - 1, par == 1)

        def mask_count(j, i):
            return NMASK * j + sum(masked[:i])

        def bank_evicted(eng, j, g):
            eng.wait_ge(evicted[g % 2], NW * j + g // 2 + 2)

        block = m.block()

        @block.sync
        def _(sync):
            for i in range(2):
                sync.dma_start(xbuf[:, 4 * i:4 * i + 4, :], xT[:, 4 * i:4 * i + 4, :]).then_inc(x_loaded[i], 16)
            sync.dma_start(g_sb[:], gain).then_inc(c_loaded, 16)
            sync.dma_start(cw[:], conv_w).then_inc(c_loaded, 16)
            for c in range(NW):
                sync.dma_start(w_sb[:, c], wstream[c]).then_inc(w_loaded[c], 16)
            sync.wait_ge(h_made, NC)
            sync.dma_start(h_out, hT[:]).then_inc(h_stored, 16)

            def body(j, par, jj, last):
                if not last:
                    for c in range(NW):
                        sync.wait_ge(w_used, NW * j + c + 1)
                        sync.dma_start(w_sb[:, c], wstream[ds(j * NW + (NW + c), 1)].rearrange("a p c n -> (a p) c n")
                                       ).then_inc(w_loaded[c], 16)
                sync.wait_ge(conv_step, TAPS * j + TAPS)
                sync.dma_start(y_out[:, ds(j, 1), :], ybuf[:, par:par + 1, :]).then_inc(y_stored[par], 16)
                sync.wait_ge(o_copied, 4 * j + 4 + 1)
                sync.dma_start(attn_out[:, ds(j, 1), :], oT[:, par:par + 1, :]).then_inc(o_stored[par], 16)

            pairs(sync, body)
            sync.wait_ge(h_stored, 16)
            for b in range(2):
                sync.wait_ge(y_stored[b], 16 * (NC // 2) + 1)
                sync.wait_ge(o_stored[b], 16 * (NC // 2) + 1)

        @block.gpsimd
        def _(pool):
            nc.gpsimd.memset(ones[:], 1.0).then_inc(const_made, 1)
            nc.gpsimd.memset(u[:, :, 0:PAD], 0.0).then_inc(const_made, 1)
            pool.wait_ge(const_made, 2)
            nc.gpsimd.affine_select(out=tri[:], in_=ones[:], pattern=[[-1, P]], compare_op=ALU.is_gt, fill=0.0,
                                    base=0, channel_multiplier=1).then_inc(const_made, 1)
            nc.gpsimd.affine_select(out=rest[:], in_=ones[:], pattern=[[1, P]], compare_op=ALU.is_ge, fill=0.0,
                                    base=0, channel_multiplier=-1).then_inc(const_made, 1)
            nc.gpsimd.affine_select(out=causal[:], in_=ones[:], pattern=[[1, P]], compare_op=ALU.is_gt, fill=0.0,
                                    base=0, channel_multiplier=-1).then_inc(const_made, 1)
            pool.wait_ge(const_made, 5)

            with pool.Fori(0, NC) as j:
                for i in range(NCELL):
                    if not masked[i]:
                        continue
                    a = col0[i]
                    for s in range(2):
                        pool.wait_ge(sp_raw[s], mask_count(j, i) + 1)
                        nc.gpsimd.tensor_tensor(sp[:, s, a:a + P], sp[:, s, a:a + P], causal[:], ALU.mult
                                                ).then_inc(sp_done[s], 1)
                    for s in range(2):
                        pool.wait_ge(wt_raw[s], mask_count(j, i) + 1)
                        nc.gpsimd.tensor_tensor(wt[:, s, a:a + P], wt[:, s, a:a + P], causal[:], ALU.mult
                                                ).then_inc(wt_done[s], 1)

        @block.scalar
        def _(act):
            for i in range(NC):
                act.wait_ge(x_loaded[i // 4], 16)
                if i >= 2:
                    act.wait_ge(sum_done, i - 1)
                nc.scalar.activation(sq[:, i % 2], xbuf[:, i], ACT.Square).then_inc(sq_made, 1)

            norm.root(nc, act)
            nc.scalar.preload_act_table_set("natural_log_exp_and_others")

            def evict(j, par, g):
                c, h = g // 2, g % 2
                if c == 1:
                    return
                act.wait_ge(group_done, NG * j + g + 1)
                hs = slice(h * H, h * H + H)
                if c == 0:
                    act.wait_ge(u_made, 2 * j + 1)
                    nc.scalar.activation(egate[:, hs], gemm[:, h], ACT.Exp, scale=-1.0).then_inc(evicted[h], 1)
                elif c == 2:
                    nc.scalar.activation(qT[:, par, hs], gemm[:, h], ACT.Copy,
                                         scale=float(SB_HD) ** -0.5).then_inc(evicted[h], 1)
                elif c == 3:
                    nc.scalar.activation(kT[:, par, hs], gemm[:, h], ACT.Copy).then_inc(evicted[h], 1)
                else:
                    nc.scalar.activation(v[:, par, 4 * h:4 * h + 4, :],
                                         gemm[:, h].rearrange("p (t n) -> p t n", n=P), ACT.Copy).then_inc(evicted[h], 1)

            for g in range(NG):
                evict(0, 0, g)

            def body(j, par, jj, last):
                for i in range(NCELL):
                    a, n = col0[i], NCELL * j + i
                    for s in range(2):
                        act.wait_ge(z_done[s], n + 1)
                        nc.scalar.activation(absz[:, s, a:H], zps[:, s, a:H], ACT.Abs).then_inc(act_step[s], 1)
                    for s in range(2):
                        act.wait_ge(act_step[s], n * 2 + 1)
                        act.wait_ge(ls_done[s], n + 1)
                        nc.scalar.activation(ex[:, s, a:H], absz[:, s, a:H], ACT.Exp, scale=-1.0).then_inc(act_step[s], 1)
                    for s in range(2):
                        act.wait_ge(act_step[s], n * 2 + 2)
                        nc.scalar.activation(ln[:, s, a:H], ex[:, s, a:H], ACT.Ln, bias=1.0).then_inc(ln_done[s], 1)
                    if not last and 1 <= i <= NG:
                        evict(j + 1, 1 - par, i - 1)
                    for s in range(2):
                        act.wait_ge(lw_done[s], n + 1 + 1)
                        act.wait_ge(pv_done[s], n + 1)
                        ins = nc.scalar.activation(wt[:, s, a:H], lw[:, s, a:H], ACT.Exp)
                        ins.then_inc(wt_raw[s] if masked[i] else wt_done[s], 1)
                    if i and closes[i - 1]:
                        outputs(j, par, jj, cells[i - 1][0], NCELL * j + i)
                outputs(j, par, jj, 1, NCELL * j + NCELL)

            def outputs(j, par, jj, qh, n):
                act.wait_ge(o_stored[par], 16 * jj + 1)
                for s in range(2):
                    act.wait_ge(pv_done[s], n + 1)
                    rows = slice(64 * s, 64 * s + 64)
                    nc.scalar.activation(oT[rows, par, qh * H:qh * H + H], ops[rows, s, :], ACT.Copy
                                         ).then_inc(o_copied, 1)

            pairs(act, body)

        @block.vector
        def _(dve):
            dve.wait_ge(sum_done, NC)
            norm.start(nc, dve, [(slice(h * H, h * H + H), gemm[:, h]) for h in range(2)], lambda h: evicted[h])
            norm.finish(nc, dve)
            dve.wait_ge(c_loaded, 32)
            dve.wait_ge(norm.made, 1)
            for c in range(NC):
                nc.vector.scalar_tensor_tensor(out=hT[:, c], in0=xbuf[:, c], scalar=g_sb[:, c:c + 1], in1=norm.rstd[:],
                                               op0=ALU.mult, op1=ALU.mult).then_inc(h_made, 1)

            def value(j, par, h):
                dve.wait_ge(group_done, NG * j + 2 + h + 1)
                bank_evicted(dve, j, h)
                hs = slice(h * H, h * H + H)
                nc.vector.tensor_scalar(den[:, hs], egate[:, hs], 1.0, None, ALU.add).then_inc(u_step, 1)
                dve.wait_ge(u_step, 4 * j + 2 * h + 1)
                nc.vector.reciprocal(den[:, hs], den[:, hs]).then_inc(u_step, 1)
                dve.wait_ge(u_step, 4 * j + 2 * h + 2)
                nc.vector.tensor_tensor(u[:, par, PAD + h * H:PAD + h * H + H], gemm[:, h], den[:, hs],
                                        ALU.mult).then_inc(evicted[h], 1)
                bank_evicted(dve, j, 2 + h)
                dve.sem_inc(u_made, 1)

            def conv(j, par, jj, t):
                if t == 0:
                    nc.vector.tensor_copy(cwj[:], cw[:, ds(j, 1), :].rearrange("p a t -> p (a t)")).then_inc(cwj_made, 1)
                    dve.wait_ge(cwj_made, j + 1)
                    dve.wait_ge(y_stored[par], 16 * jj + 1)
                    dve.wait_ge(u_made, 2 * j + 2 + 1)
                    nc.vector.tensor_scalar(ybuf[:, par], u[:, par, 0:T], cwj[:, 0:1], cwj[:, TAPS:TAPS + 1],
                                            ALU.mult, ALU.add).then_inc(conv_step, 1)
                else:
                    dve.wait_ge(conv_step, TAPS * j + t)
                    nc.vector.scalar_tensor_tensor(out=ybuf[:, par], in0=u[:, par, t:t + T], scalar=cwj[:, t:t + 1],
                                                   in1=ybuf[:, par], op0=ALU.mult, op1=ALU.add).then_inc(conv_step, 1)

            for h in range(2):
                value(0, 0, h)

            def body(j, par, jj, last):
                for i in range(NCELL):
                    a, n = col0[i], NCELL * j + i
                    for s in range(2):
                        dve.wait_ge(ln_done[s], n + 1)
                        dve.wait_ge(sp_used[s], n + 1)
                        ins = nc.vector.scalar_tensor_tensor(out=sp[:, s, a:H], in0=zps[:, s, a:H], scalar=0.0,
                                                             in1=ln[:, s, a:H], op0=ALU.max, op1=ALU.add)
                        ins.then_inc(sp_raw[s] if masked[i] else sp_done[s], 1)
                    for s in range(2):
                        nc.vector.scalar_tensor_tensor(out=ls[:, s, a:H], in0=zps[:, s, a:H], scalar=0.0,
                                                       in1=ln[:, s, a:H], op0=ALU.min, op1=ALU.subtract
                                                       ).then_inc(ls_done[s], 1)
                    if not last and i in (3, 4):
                        value(j + 1, 1 - par, i - 3)
                    for s in range(2):
                        dve.wait_ge(c_done[s], n + 1)
                        dve.wait_ge(wt_raw[s], mask_count(j, i)) if i and masked[i - 1] else dve.wait_ge(wt_done[s], n + 1)
                        dve.wait_ge(ls_done[s], n + 1 + 1)
                        nc.vector.tensor_tensor(lw[:, s, a:H], ls[:, s, a:H], cps[:, s, a:H], ALU.subtract
                                                ).then_inc(lw_done[s], 1)
                    for t in range(3 * i, min(3 * i + 3, TAPS)):
                        conv(j, par, jj, t)

            pairs(dve, body)

        @block.tensor
        def _(pe):
            pe.wait_ge(const_made, 4)
            for c in range(NC):
                pe.wait_ge(sq_made, c + 1)
                for h in range(2):
                    mm = nc.tensor.matmul(gemm[:, h], ones[:], sq[:, c % 2, h * H:h * H + H],
                                          start=(c == 0), stop=(c == NC - 1))
                mm.then_inc(sum_done, 1)
            pe.wait_ge(h_made, NC)

            def project(j, g, k0, k1):
                c, h = g // 2, g % 2
                if k0 == 0:
                    if h == 0:
                        pe.wait_ge(w_loaded[c], j * 16 + 16)
                    pe.wait_ge(evicted[h], NW * j + c + 1)
                if c == 4:
                    for x in range(k0 // 2, k1 // 2):
                        t = 4 * h + x
                        for k in range(NC):
                            mm = nc.tensor.matmul(gemm[:, h, x * P:x * P + P], hT[:, k, t * P:t * P + P], w_sb[:, c, k],
                                                  start=(k == 0), stop=(k == NC - 1))
                else:
                    for k in range(k0, k1):
                        mm = nc.tensor.matmul(gemm[:, h], w_sb[:, c, k], hT[:, k, h * H:h * H + H],
                                              start=(k == 0), stop=(k == NC - 1))
                if k1 == NC:
                    mm.then_inc(group_done, 1)
                    if h == 1:
                        pe.wait_ge(group_done, NG * j + g + 1)
                        pe.sem_inc(w_used, 1)

            def z_cell(j, par, s, i):
                (qh, kb), a = cells[i], col0[i]
                if i == 0:
                    bank_evicted(pe, j, 6)
                    bank_evicted(pe, j, 7)
                pe.wait_ge(ls_done[s], NCELL * j + i + 1)
                rows = slice(64 * s, 64 * s + 64)
                nc.tensor.matmul(zps[:, s, a:H], kT[rows, par, kb * P:kb * P + P], qT[rows, par, qh * H + a:qh * H + H],
                                 start=True, stop=True).then_inc(z_done[s], 1)

            def add_own(j, s, i):
                a = col0[i]
                pe.wait_ge(sp_done[s], NCELL * j + i + 1)
                if opens[i]:
                    pe.wait_ge(lw_done[s], NCELL * j + i + 1)
                mm = nc.tensor.matmul(cps[:, s, a:H], tri[:], sp[:, s, a:H], start=opens[i], stop=True,
                                      skip_group_check=True)
                mm.then_inc(c_done[s], 1)
                if closes[i]:
                    pe.wait_ge(c_done[s], NCELL * j + i + 1)
                    pe.sem_inc(sp_used[s], 1)

            def add_rest(j, s, i):
                a = col0[i]
                if not closes[i]:
                    pe.wait_ge(lw_done[s], NCELL * j + i + 1 + 1)
                    nc.tensor.matmul(cps[:, s, a:H], rest[:], sp[:, s, a:H], start=False, stop=True,
                                     skip_group_check=True).then_inc(sp_used[s], 1)

            def weigh(j, par, s, i):
                (qh, kb), a = cells[i], col0[i]
                if i == 0:
                    bank_evicted(pe, j, 8)
                    bank_evicted(pe, j, 9)
                if opens[i]:
                    pe.wait_ge(o_copied, 4 * j + 2 * qh + 1)
                pe.wait_ge(wt_done[s], NCELL * j + i + 1 + 1)
                nc.tensor.matmul(ops[64 * s:64 * s + 64, s, a:H], v[:, par, kb, 64 * s:64 * s + 64], wt[:, s, a:H],
                                 start=opens[i], stop=closes[i], skip_group_check=True).then_inc(pv_done[s], 1)

            for g in range(NG):
                project(0, g, 0, NC)
            for s in range(2):
                z_cell(0, 0, s, 0)

            def body(j, par, jj, last):
                for i in range(NCELL):
                    for s in range(2):
                        add_own(j, s, i)
                    if not last and i < NG:
                        project(j + 1, i, 0, NC // 2)
                    for s in range(2):
                        add_rest(j, s, i)
                        if i < NCELL - 1:
                            z_cell(j, par, s, i + 1)
                        elif not last:
                            z_cell(j + 1, 1 - par, s, 0)
                    if not last and i < NG:
                        project(j + 1, i, NC // 2, NC)
                    for s in range(2):
                        weigh(j, par, s, i)

            pairs(pe, body)


def merge_phase(nc, xT, h_in, y_in, attn_in, wstream, ln_g, ln_b, gate_b, x_out):
    with Phase(nc, "merge") as m:
        NW = 4
        hT = m.sb("hT", [P, NC, T])
        zT = m.sb("zT", [P, NC, T])
        aT = m.sb("aT", [P, NC, T])
        mT = m.sb("mT", [P, NC, T])
        sq = m.sb("sq", [P, 2, T])
        mean = m.sb("mean", [P, T])
        norm = Rsqrt(m, "norm", T)
        ones = m.sb("ones", [P, P])
        lng, lnb = m.sb("lng", [P, NC]), m.sb("lnb", [P, NC])
        gb = m.sb("gb", [P, 2, NC])
        gbj = m.sb("gbj", [P, 2])
        w_sb = m.sb("w", [P, NW, NC, P])
        sg = m.sb("sg", [P, 2, T])
        xres = m.sb("xres", [P, 2, T])
        banks = m.ps("banks", [P, 8, H])

        y_loaded = [m.sem(f"y_loaded{i}") for i in range(2)]
        h_loaded = m.sem("h_loaded")
        a_loaded = m.sem("a_loaded")
        c_loaded = m.sem("c_loaded")
        ones_made = m.sem("ones_made")
        mean_sum = m.sem("mean_sum")
        mean_made = m.sem("mean_made")
        centred = m.sem("centred")
        sq_made = m.sem("sq_made")
        sq_used = m.sem("sq_used")
        sums_read = [m.sem(f"sums_read{h}") for h in range(2)]
        scaled = m.sem("scaled")
        z_made = m.sem("z_made")
        w_loaded = [m.sem(f"w_loaded{c}") for c in range(NW)]
        w_used = m.sem("w_used")
        group_done = m.sem("group_done")
        gbj_made = m.sem("gbj_made")
        gated = m.sem("gated", start=1)
        product = m.sem("product", start=1)
        m_made = m.sem("m_made", start=1)
        x_loaded = [m.sem(f"x_loaded{b}") for b in range(2)]
        x_made = m.sem("x_made", start=1)
        x_stored = [m.sem(f"x_stored{b}", start=1) for b in range(2)]
        block = m.block()

        @block.sync
        def _(sync):
            for i in range(2):
                sync.dma_start(zT[:, 4 * i:4 * i + 4], y_in[:, 4 * i:4 * i + 4]).then_inc(y_loaded[i], 16)
            sync.dma_start(lng[:], ln_g).then_inc(c_loaded, 16)
            sync.dma_start(lnb[:], ln_b).then_inc(c_loaded, 16)
            sync.dma_start(gb[:], gate_b).then_inc(c_loaded, 16)
            sync.dma_start(hT[:], h_in).then_inc(h_loaded, 16)
            for c in range(NW):
                sync.dma_start(w_sb[:, c], wstream[c]).then_inc(w_loaded[c], 16)
            sync.dma_start(aT[:], attn_in).then_inc(a_loaded, 16)
            with sync.Fori(0, NC + 1) as j:
                for c in range(NW):
                    sync.wait_ge(w_used, j * NW + (c + 1))
                    sync.dma_start(w_sb[:, c], wstream[ds(j * NW + (NW + c), 1)].rearrange("a p c n -> (a p) c n")
                                   ).then_inc(w_loaded[c], 16)
            with sync.Fori(0, NC // 2) as jj:
                for b in range(2):
                    n = jj * 2 + b
                    sync.wait_ge(x_stored[b], jj * 16 + 1)
                    sync.dma_start(xres[:, b], xT[:, ds(n, 1), :].rearrange("p a t -> p (a t)")).then_inc(x_loaded[b], 16)
                for b in range(2):
                    n = jj * 2 + b
                    sync.wait_ge(x_made, n * 2 + 2 + 1)
                    sync.dma_start(x_out[:, ds(n, 1), :].rearrange("p a t -> p (a t)"), xres[:, b]).then_inc(x_stored[b], 16)
            for b in range(2):
                sync.wait_ge(x_stored[b], 16 * (NC // 2) + 1)

        @block.gpsimd
        def _(pool):
            nc.gpsimd.memset(ones[:], 1.0).then_inc(ones_made, 1)

        @block.tensor
        def _(pe):
            pe.wait_ge(ones_made, 1)
            for k in range(NC):
                if k % 4 == 0:
                    pe.wait_ge(y_loaded[k // 4], 16)
                for h in range(2):
                    mm = nc.tensor.matmul(banks[:, h], ones[:], zT[:, k, h * H:h * H + H], start=(k == 0), stop=(k == NC - 1))
            mm.then_inc(mean_sum, 1)
            for k in range(NC):
                pe.wait_ge(sq_made, k + 1)
                for h in range(2):
                    mm = nc.tensor.matmul(banks[:, 2 + h], ones[:], sq[:, k % 2, h * H:h * H + H],
                                          start=(k == 0), stop=(k == NC - 1))
                mm.then_inc(sq_used, 1)
            pe.wait_ge(h_loaded, 16)
            pe.wait_ge(z_made, NC)
            pe.wait_ge(a_loaded, 16)
            with pe.Fori(0, NC) as j:
                for c, src in enumerate((hT, zT, hT, aT)):
                    pe.wait_ge(w_loaded[c], j * 16 + 16)
                    if c % 2 == 0:
                        pe.wait_ge(gated, j * 4 + 1)
                    else:
                        pe.wait_ge(product, j * 4 + 1)
                    for h in range(2):
                        for k in range(NC):
                            mm = nc.tensor.matmul(banks[:, 2 * c + h], w_sb[:, c, k], src[:, k, h * H:h * H + H],
                                                  start=(k == 0), stop=(k == NC - 1))
                        if h == 0:
                            mm.then_inc(group_done, 1)
                    mm.then_inc(group_done, 1)
                    pe.wait_ge(group_done, j * 8 + (2 * c + 2))
                    pe.sem_inc(w_used, 1)
            pe.wait_ge(m_made, 2 * NC + 1)
            with pe.Fori(0, NC // NW) as r:
                for c in range(NW):
                    pe.wait_ge(w_loaded[c], r * 16 + 16 * (NC + 1))
                    pe.wait_ge(x_made, r * 8 + 1)
                    for h in range(2):
                        for k in range(NC):
                            mm = nc.tensor.matmul(banks[:, 2 * c + h], w_sb[:, c, k], mT[:, k, h * H:h * H + H],
                                                  start=(k == 0), stop=(k == NC - 1))
                        if h == 0:
                            mm.then_inc(group_done, 1)
                    mm.then_inc(group_done, 1)
                    pe.wait_ge(group_done, r * 8 + (8 * NC + 2 * c + 2))
                    pe.sem_inc(w_used, 1)

        @block.scalar
        def _(act):
            for k in range(NC):
                act.wait_ge(centred, k + 1)
                if k >= 2:
                    act.wait_ge(sq_used, k - 1)
                nc.scalar.activation(sq[:, k % 2], zT[:, k], ACT.Square).then_inc(sq_made, 1)
            norm.root(nc, act)
            act.wait_ge(c_loaded, 48)
            for k in range(NC):
                act.wait_ge(scaled, k + 1)
                nc.scalar.activation(zT[:, k], zT[:, k], ACT.Silu, bias=lnb[:, k:k + 1]).then_inc(z_made, 1)
            nc.scalar.preload_act_table(ACT.Sigmoid)
            with act.Fori(0, NC) as j:
                act.wait_ge(m_made, j * 2 + 1)
                nc.scalar.activation(gbj[:], gb[:, :, ds(j, 1)].rearrange("p b a -> p (b a)"), ACT.Copy).then_inc(gbj_made, 1)
                act.wait_ge(gbj_made, j + 1)
                for b in range(2):
                    for h in range(2):
                        act.wait_ge(group_done, j * 8 + (4 * b + h + 1))
                        nc.scalar.activation(sg[:, b, h * H:h * H + H], banks[:, 4 * b + h], ACT.Sigmoid, bias=gbj[:, b:b + 1]
                                             ).then_inc(gated, 1)

        @block.vector
        def _(dve):
            dve.wait_ge(mean_sum, 1)
            for h in range(2):
                nc.vector.tensor_scalar(mean[:, h * H:h * H + H], banks[:, h], 1.0 / D, None, ALU.mult).then_inc(mean_made, 1)
            dve.wait_ge(mean_made, 2)
            for k in range(NC):
                nc.vector.tensor_tensor(zT[:, k], zT[:, k], mean[:], ALU.subtract).then_inc(centred, 1)
            dve.wait_ge(sq_used, NC)
            norm.start(nc, dve, [(slice(h * H, h * H + H), banks[:, 2 + h]) for h in range(2)], lambda h: sums_read[h])
            norm.finish(nc, dve)
            dve.wait_ge(norm.made, 1)
            dve.wait_ge(c_loaded, 48)
            for k in range(NC):
                nc.vector.scalar_tensor_tensor(out=zT[:, k], in0=zT[:, k], scalar=lng[:, k:k + 1], in1=norm.rstd[:],
                                               op0=ALU.mult, op1=ALU.mult).then_inc(scaled, 1)
            with dve.Fori(0, NC) as j:
                for b in range(2):
                    for h in range(2):
                        hs = slice(h * H, h * H + H)
                        dve.wait_ge(group_done, j * 8 + (4 * b + 2 + h + 1))
                        dve.wait_ge(gated, j * 4 + (2 * b + h + 1) + 1)
                        nc.vector.tensor_tensor(sg[:, b, hs], sg[:, b, hs], banks[:, 4 * b + 2 + h], ALU.mult
                                                ).then_inc(product, 1)
                for h in range(2):
                    hs = slice(h * H, h * H + H)
                    dve.wait_ge(product, j * 4 + (3 + h) + 1)
                    nc.vector.tensor_tensor(mT[:, ds(j, 1), hs].rearrange("p a t -> p (a t)"), sg[:, 0, hs], sg[:, 1, hs],
                                            ALU.add).then_inc(m_made, 1)
            with dve.Fori(0, NC // NW) as r:
                for c in range(NW):
                    b = c % 2
                    dve.wait_ge(x_loaded[b], r * 32 + 16 * (c // 2 + 1))
                    for h in range(2):
                        hs = slice(h * H, h * H + H)
                        dve.wait_ge(group_done, r * 8 + (8 * NC + 2 * c + h + 1))
                        nc.vector.tensor_tensor(xres[:, b, hs], xres[:, b, hs], banks[:, 2 * c + h], ALU.add
                                                ).then_inc(x_made, 1)


def cross_attention_phase(nc, x_in, gain, memT, mem_gain, wstream, x_out):
    with Phase(nc, "xattn") as m:
        NW = 6
        HC = 2
        MT = M // P
        xT = m.sb("xT", [P, NC, T])
        hT = m.sb("hT", [P, NC, T])
        mT = m.sb("mT", [P, NC, M])
        oT = m.sb("oT", [P, NC, T])
        sq = m.sb("sq", [P, 2, T])
        msq = m.sb("msq", [P, NC, M])
        norm = Rsqrt(m, "norm", T)
        mnorm = Rsqrt(m, "mnorm", M)
        g_sb, mg_sb = m.sb("gain", [P, NC]), m.sb("mgain", [P, NC])
        ones = m.sb("ones", [P, P])
        ident = m.sb("ident", [P, P])
        w_sb = m.sb("w", [P, NW, NC, P])
        qT = m.sb("qT", [P, HC, T])
        kT = m.sb("kT", [P, HC, M])
        v = m.sb("v", [P, MT, HC * P])
        top = m.sb("top", [P, NT])
        total = m.sb("total", [P, NT])
        inv = m.sb("inv", [P, NT])
        prob = m.sb("prob", [P, 2, 2, M])
        pT = m.sb("pT", [P, MT, T])

        gemm = m.ps("gemm", [P, 2, H])
        score = m.ps("score", [P, 2, 2, M])
        turned = m.ps("turned", [P, 2, MT, 2 * P])
        out = m.ps("out", [P, 2, H])

        x_loaded = [m.sem(f"x_loaded{i}") for i in range(2)]
        m_loaded = m.sem("m_loaded")
        c_loaded = m.sem("c_loaded")
        made = m.sem("made")
        sq_made = m.sem("sq_made")
        sq_used = m.sem("sq_used")
        msq_made = m.sem("msq_made")
        msum_done = m.sem("msum_done")
        msum_read = m.sem("msum_read")
        mh_made = m.sem("mh_made")
        h_made = m.sem("h_made")
        w_loaded = [m.sem(f"w_loaded{c}") for c in range(NW)]
        w_used = m.sem("w_used")
        group_done = m.sem("group_done")
        evicted = [m.sem(f"evicted{b}") for b in range(2)]
        score_done = m.sem("score_done")
        top_made = m.sem("top_made")
        exp_made = m.sem("exp_made", start=1)
        inv_made = m.sem("inv_made")
        prob_made = m.sem("prob_made")
        turned_done = m.sem("turned_done", start=1)
        pT_made = m.sem("pT_made", start=1)
        out_done = m.sem("out_done", start=1)
        o_made = m.sem("o_made", start=1)
        x_made = m.sem("x_made")
        x_stored = m.sem("x_stored")
        block = m.block()
        GH = 2 * NW
        GROUPS = [("q", 0, 0), ("q", 0, 1), ("q", 1, 0), ("q", 1, 1), ("k", 0, 0), ("k", 1, 0), ("v", 0, 0), ("v", 1, 0)]
        NGR = len(GROUPS)

        @block.sync
        def _(sync):
            for i in range(2):
                sync.dma_start(xT[:, 4 * i:4 * i + 4], x_in[:, 4 * i:4 * i + 4]).then_inc(x_loaded[i], 16)
            sync.dma_start(mT[:], memT).then_inc(m_loaded, 16)
            sync.dma_start(g_sb[:], gain).then_inc(c_loaded, 16)
            sync.dma_start(mg_sb[:], mem_gain).then_inc(c_loaded, 16)
            for c in range(NW):
                sync.dma_start(w_sb[:, c], wstream[c]).then_inc(w_loaded[c], 16)
            with sync.Fori(0, XH - 1) as hd:
                for c in range(NW):
                    sync.wait_ge(w_used, hd * NW + (c + 1))
                    sync.dma_start(w_sb[:, c], wstream[ds(hd * NW + (NW + c), 1)].rearrange("a p c n -> (a p) c n")
                                   ).then_inc(w_loaded[c], 16)
            for n in range(NC):
                c = n % 4
                sync.wait_ge(w_used, NW * (XH - 1) + c + 1 if n < 4 else NW * XH + n - 3)
                sync.dma_start(w_sb[:, c], wstream[NW * XH + n]).then_inc(w_loaded[c], 16)
            for n in range(NC):
                sync.wait_ge(x_made, 2 * n + 2)
                sync.dma_start(x_out[:, n], xT[:, n]).then_inc(x_stored, 16)
            sync.wait_ge(x_stored, 16 * NC)

        @block.gpsimd
        def _(pool):
            nc.gpsimd.memset(ones[:], 1.0).then_inc(made, 1)
            pool.wait_ge(made, 1)
            nc.gpsimd.affine_select(out=ident[:], in_=ones[:], pattern=[[-1, P]], compare_op=ALU.is_equal, fill=0.0,
                                    base=0, channel_multiplier=1).then_inc(made, 1)

        @block.tensor
        def _(pe):
            pe.wait_ge(made, 2)
            pe.wait_ge(msq_made, 1)
            for k in range(NC):
                mm = nc.tensor.matmul(out[:, 0, 0:M], ones[:], msq[:, k], start=(k == 0), stop=(k == NC - 1))
            mm.then_inc(msum_done, 1)
            for k in range(NC):
                pe.wait_ge(sq_made, k + 1)
                for h in range(2):
                    mm = nc.tensor.matmul(gemm[:, h], ones[:], sq[:, k % 2, h * H:h * H + H], start=(k == 0), stop=(k == NC - 1))
                mm.then_inc(sq_used, 1)
            pe.wait_ge(mh_made, NC)
            pe.wait_ge(h_made, NC)

            def turn(hd, s):
                pe.wait_ge(prob_made, hd * 8 + (2 * s + 2))
                pe.wait_ge(pT_made, hd * 4 + s - 1 + 1) if s else pe.wait_ge(pT_made, hd * 4 + 1)
                for x in range(2):
                    for t in range(MT):
                        mm = nc.tensor.transpose(turned[:, s % 2, t, x * P:x * P + P], prob[:, s % 2, x, t * P:t * P + P],
                                                 ident[:])
                mm.then_inc(turned_done, 1)

            with pe.Fori(0, XH) as hd:
                for g, (what, i, h) in enumerate(GROUPS):
                    b = g % 2
                    if what == "q":
                        c, n = i, H
                    else:
                        c, n = (2 + i if what == "k" else 4), M
                    pe.wait_ge(w_loaded[c], hd * 16 + 16)
                    if what == "v":
                        pe.wait_ge(w_loaded[5], hd * 16 + 16)
                    pe.wait_ge(evicted[b], hd * (NGR // 2) + (g // 2 + 1))
                    if what == "q":
                        for k in range(NC):
                            mm = nc.tensor.matmul(gemm[:, b], w_sb[:, c, k], hT[:, k, h * H:h * H + H],
                                                  start=(k == 0), stop=(k == NC - 1))
                    elif what == "k":
                        for k in range(NC):
                            mm = nc.tensor.matmul(gemm[:, b, 0:M], w_sb[:, c, k], mT[:, k], start=(k == 0), stop=(k == NC - 1))
                    else:
                        for half in range(HC):
                            for k in range(NC):
                                mm = nc.tensor.matmul(gemm[:, b, half * P:half * P + P], mT[:, k, i * P:i * P + P],
                                                      w_sb[:, 4 + half, k], start=(k == 0), stop=(k == NC - 1))
                    mm.then_inc(group_done, 1)
                    done = {1: 1, 3: 1, 4: 1, 5: 1, 7: 2}.get(g, 0)
                    if done:
                        pe.wait_ge(group_done, hd * NGR + (g + 1))
                        pe.sem_inc(w_used, done)
                for b in range(2):
                    pe.wait_ge(evicted[b], hd * (NGR // 2) + (NGR // 2 + 1))
                for s in range(4):
                    if s >= 2:
                        pe.wait_ge(exp_made, hd * 8 + 2 * (s - 1) + 1)
                    else:
                        pe.wait_ge(exp_made, hd * 8 + 1)
                    for x in range(2):
                        t = 2 * s + x
                        for c in range(HC):
                            mm = nc.tensor.matmul(score[:, s % 2, x], qT[:, c, t * P:t * P + P], kT[:, c],
                                                  start=(c == 0), stop=(c == HC - 1))
                    mm.then_inc(score_done, 1)
                    if s >= 1:
                        turn(hd, s - 1)
                turn(hd, 3)
                pe.wait_ge(pT_made, hd * 4 + 4 + 1)
                for c in range(HC):
                    for h in range(2):
                        pe.wait_ge(o_made, hd * 4 + (2 * c + h - 1) + 1) if 2 * c + h >= 2 else pe.wait_ge(o_made, hd * 4 + 1)
                        for t in range(MT):
                            mm = nc.tensor.matmul(out[:, h], v[:, t, c * P:c * P + P], pT[:, t, h * H:h * H + H],
                                                  start=(t == 0), stop=(t == MT - 1))
                        mm.then_inc(out_done, 1)
            pe.wait_ge(o_made, 4 * XH + 1)
            for n in range(NC):
                c = n % 4
                pe.wait_ge(w_loaded[c], 16 * (XH + 1 + n // 4))
                for h in range(2):
                    if n:
                        pe.wait_ge(x_made, 2 * n - 1 + h)
                    for k in range(NC):
                        mm = nc.tensor.matmul(gemm[:, h], w_sb[:, c, k], oT[:, k, h * H:h * H + H],
                                              start=(k == 0), stop=(k == NC - 1))
                    mm.then_inc(group_done, 1)
                pe.wait_ge(group_done, NGR * XH + 2 * n + 2)
                pe.sem_inc(w_used, 1)

        def copy_turned(act, hd, s):
            act.wait_ge(turned_done, hd * 4 + (s + 1) + 1)
            if s == 0:
                act.wait_ge(out_done, hd * 4 + 1)
            nc.scalar.activation(pT[:, :, 2 * s * P:2 * s * P + 2 * P], turned[:, s % 2], ACT.Copy).then_inc(pT_made, 1)

        @block.scalar
        def _(act):
            act.wait_ge(m_loaded, 16)
            nc.scalar.activation(msq[:], mT[:], ACT.Square).then_inc(msq_made, 1)
            for k in range(NC):
                act.wait_ge(x_loaded[k // 4], 16)
                if k >= 2:
                    act.wait_ge(sq_used, k - 1)
                nc.scalar.activation(sq[:, k % 2], xT[:, k], ACT.Square).then_inc(sq_made, 1)
            mnorm.root(nc, act)
            norm.root(nc, act)
            nc.scalar.preload_act_table(ACT.Exp)
            with act.Fori(0, XH) as hd:
                for g, (what, i, h) in enumerate(GROUPS):
                    b = g % 2
                    act.wait_ge(group_done, hd * NGR + (g + 1))
                    if what == "q":
                        nc.scalar.activation(qT[:, i, h * H:h * H + H], gemm[:, b], ACT.Copy, scale=1.0 / 16
                                             ).then_inc(evicted[b], 1)
                    elif what == "k":
                        nc.scalar.activation(kT[:, i], gemm[:, b, 0:M], ACT.Copy).then_inc(evicted[b], 1)
                    else:
                        nc.scalar.activation(v[:, i], gemm[:, b, 0:M], ACT.Copy).then_inc(evicted[b], 1)
                for t in range(NT):
                    s, x = t // 2, t % 2
                    act.wait_ge(top_made, hd * 4 + (s + 1))
                    act.wait_ge(turned_done, 1 + (hd * 4 + (s - 1) if s >= 2 else hd * 4))
                    nc.scalar.activation(prob[:, s % 2, x], score[:, s % 2, x], ACT.Exp, bias=top[:, t:t + 1],
                                         accum_out=total[:, t:t + 1]).then_inc(exp_made, 1)
                    if x == 1 and s >= 1:
                        copy_turned(act, hd, s - 1)
                copy_turned(act, hd, 3)
                for c in range(HC):
                    for h in range(2):
                        act.wait_ge(out_done, hd * 4 + (2 * c + h + 1) + 1)
                        nc.scalar.activation(oT[:, ds(hd * HC + c, 1), h * H:h * H + H].rearrange("p a t -> p (a t)"),
                                             out[:, h], ACT.Copy).then_inc(o_made, 1)

        def normalise(dve, hd, s):
            dve.wait_ge(exp_made, hd * 8 + (2 * s + 2) + 1)
            nc.vector.reciprocal(inv[:, 2 * s:2 * s + 2], total[:, 2 * s:2 * s + 2]).then_inc(inv_made, 1)
            dve.wait_ge(inv_made, hd * 4 + (s + 1))
            for x in range(2):
                nc.vector.tensor_scalar(prob[:, s % 2, x], prob[:, s % 2, x], inv[:, 2 * s + x:2 * s + x + 1], None, ALU.mult
                                        ).then_inc(prob_made, 1)

        @block.vector
        def _(dve):
            dve.wait_ge(c_loaded, 32)
            dve.wait_ge(msum_done, 1)
            mnorm.start(nc, dve, [(slice(0, M), out[:, 0, 0:M])], lambda h: msum_read)
            mnorm.finish(nc, dve)
            dve.wait_ge(mnorm.made, 1)
            for k in range(NC):
                nc.vector.scalar_tensor_tensor(out=mT[:, k], in0=mT[:, k], scalar=mg_sb[:, k:k + 1], in1=mnorm.rstd[:],
                                               op0=ALU.mult, op1=ALU.mult).then_inc(mh_made, 1)
            dve.wait_ge(sq_used, NC)
            norm.start(nc, dve, [(slice(h * H, h * H + H), gemm[:, h]) for h in range(2)], lambda h: evicted[h])
            norm.finish(nc, dve)
            dve.wait_ge(norm.made, 1)
            for k in range(NC):
                nc.vector.scalar_tensor_tensor(out=hT[:, k], in0=xT[:, k], scalar=g_sb[:, k:k + 1], in1=norm.rstd[:],
                                               op0=ALU.mult, op1=ALU.mult).then_inc(h_made, 1)
            with dve.Fori(0, XH) as hd:
                for s in range(4):
                    dve.wait_ge(score_done, hd * 4 + (s + 1))
                    nc.vector.tensor_reduce(top[:, 2 * s:2 * s + 2], score[:, s % 2], AX.X, ALU.max, negate=True
                                            ).then_inc(top_made, 1)
                    if s:
                        normalise(dve, hd, s - 1)
                normalise(dve, hd, 3)
            for n in range(NC):
                for h in range(2):
                    hs = slice(h * H, h * H + H)
                    dve.wait_ge(group_done, NGR * XH + 2 * n + h + 1)
                    nc.vector.tensor_tensor(xT[:, n, hs], xT[:, n, hs], gemm[:, h], ALU.add).then_inc(x_made, 1)



class Experts1:

    def __init__(self, nc, tensors):
        sb = lambda name, shape, dt=F32: tensors.enter_context(nc.sbuf_tensor(name, shape, dt))
        self.nc = nc
        self.hhi, self.hlo = sb("hhi", [P, NC, T], F32R), sb("hlo", [P, NC, T], F32R)
        self.raw = sb("uraw", [P, 2, NC, P])
        self.hi, self.lo = sb("uhi", [P, 2, NC, P], F32R), sb("ulo", [P, 2, NC, P], F32R)
        self.out = sb("ugelu", [P, 2, T])

    def begin(self, m, u_stream, a_out):
        self.u_stream, self.a_out = u_stream, a_out
        self.ps = m.ps("a", [P, 2, H])
        self.loaded = [m.sem(f"u_loaded{s}") for s in range(2)]
        self.hi_made, self.lo_made = m.sem("uhi_made"), m.sem("ulo_made")
        self.done = m.sem("a_done")
        self.gelu = m.sem("a_gelu", start=2)
        self.stored = [m.sem(f"a_stored{s}", start=1) for s in range(2)]


    def load(self, sync, tile0, n, m, slot, first=False):
        if not first:
            sync.wait_ge(self.lo_made, n - 1)
        sync.dma_start(self.raw[:, slot], self.u_stream[ds(n + tile0, 1)].rearrange("a p c n -> (a p) c n")
                       ).then_inc(self.loaded[slot], 16)

    def store(self, sync, tile0, n, slot):
        sync.wait_ge(self.gelu, n * 2 + 4)
        sync.dma_start(self.a_out[ds(n + tile0, 1)].rearrange("a p t -> (a p) t"), self.out[:, slot]
                       ).then_inc(self.stored[slot], 16)

    def split_high(self, act, n, m, slot, first=False):
        act.wait_ge(self.loaded[slot], m * 16 + 16)
        if not first:
            act.wait_ge(self.done, n * 2 - 2)
        self.nc.scalar.activation(self.hi[:, slot], self.raw[:, slot], ACT.Copy).then_inc(self.hi_made, 1)

    def split_low(self, pool, n, slot):
        pool.wait_ge(self.hi_made, n + 1)
        self.nc.gpsimd.tensor_tensor(self.lo[:, slot], self.raw[:, slot], self.hi[:, slot].bitcast(F32), ALU.subtract
                                     ).then_inc(self.lo_made, 1)

    def product(self, pe, n, slot):
        pe.wait_ge(self.hi_made, n + 1)
        pe.wait_ge(self.lo_made, n + 1)
        for h in range(2):
            pe.wait_ge(self.gelu, n * 2 + (h + 1))
            mm = three_pass(self.nc, self.ps[:, h], [(self.hi[:, slot, k], self.lo[:, slot, k],
                                                      self.hhi[:, k, h * H:h * H + H], self.hlo[:, k, h * H:h * H + H])
                                                     for k in range(NC)])
            mm.then_inc(self.done, 1)

    def activate(self, act, n, m, slot):
        act.wait_ge(self.stored[slot], m * 16 + 1)
        for h in range(2):
            act.wait_ge(self.done, n * 2 + (h + 1))
            self.nc.scalar.activation(self.out[:, slot, h * H:h * H + H], self.ps[:, h], ACT.Gelu_apprx_tanh
                                      ).then_inc(self.gelu, 1)

    def finish(self, sync, n):
        for s in range(2):
            sync.wait_ge(self.stored[s], n // 2 * 16 + 1)


def select_phase(nc, ex, x_in, gain, keysT, wstream, u_stream, a_out, sel_out):
    with Phase(nc, "select") as m:
        K = TOPK
        xT = m.sb("xT", [P, NC, T])
        room = xT[:].rearrange("p c t -> p (c t)")
        sc = room[:, 0:2048].rearrange("p (c t n) -> p c t n", c=2, t=NT)
        sc2 = room[:, 2048:4096].rearrange("p (c t n) -> p c t n", c=2, t=NT)
        cand = room[:, 4096:6144].rearrange("p (t n) -> p t n", t=NT)
        cand2 = room[:, 6144:8192].rearrange("p (t n) -> p t n", t=NT)
        sq = ex.out
        norm = Rsqrt(m, "norm", T)
        g_sb = m.sb("gain", [P, NC])
        ones, ident = m.sb("ones", [P, P]), m.sb("ident", [P, P])
        keys = m.sb("keys", [P, 2, KEYS])
        w_raw = m.sb("wraw", [P, 2, NC, P])
        w_hi, w_lo = m.sb("whi", [P, 2, NC, P], F32R), m.sb("wlo", [P, 2, NC, P], F32R)
        qT = m.sb("qT", [P, 2, T])
        top = m.sb("top", [P, 2, NT, K])
        idx = m.sb("idx", [P, 2, NT, K], U32)
        idxf = m.sb("idxf", [P, 2, NT, K])
        best = m.sb("best", [P, NT, K])
        bidx = m.sb("bidx", [P, NT, K], U32)
        part = m.sb("part", [P, 2, NT, K], U32)
        partf = m.sb("partf", [P, 2, NT, K])
        iota16 = m.sb("iota16", [P, K])
        hit = m.sb("hit", [P, NT, K, K])
        shifted = m.sb("shifted", [P, NT, K])
        expv = m.sb("expv", [P, NT, K])
        total, inv = m.sb("total", [P, NT]), m.sb("inv", [P, NT])
        res = m.sb("res", [P, 3, NT, PH, K])
        resT = room[:, 0:3 * T].rearrange("p (r t) -> p r t", r=3)

        gemm = m.ps("gemm", [P, 2, H])
        scps = m.ps("scps", [P, 2, NT, KEYS])

        x_loaded = [m.sem(f"x_loaded{i}") for i in range(2)]
        c_loaded = m.sem("c_loaded")
        made = m.sem("made")
        sq_made, sq_used = m.sem("sq_made"), m.sem("sq_used")
        h_made, hhi_made, hlo_made = m.sem("h_made"), m.sem("hhi_made"), m.sem("hlo_made")
        w_loaded = [m.sem(f"w_loaded{c}") for c in range(2)]
        whi_made, wlo_made = m.sem("whi_made"), m.sem("wlo_made")
        group_done = m.sem("group_done")
        evicted = [m.sem(f"evicted{b}") for b in range(2)]
        scored = m.sem("scored", start=1)
        sc_made = m.sem("sc_made", start=1)
        first8, index8, cut8, last8 = [m.sem(n) for n in ("first8", "index8", "cut8", "last8")]
        index16 = m.sem("index16", start=1)
        idxf_made = m.sem("idxf_made")
        cand_made = m.sem("cand_made")
        cfirst8, cindex8, ccut8, clast8, cindex16 = [m.sem(n) for n in ("cfirst8", "cindex8", "ccut8", "clast8", "cindex16")]
        part_made, partf_made = m.sem("part_made"), m.sem("partf_made")
        hit_step = m.sem("hit_step")
        shift_made, exp_made, gate_step = m.sem("shift_made"), m.sem("exp_made"), m.sem("gate_step")
        hit_summed = m.sem("hit_summed", start=1)
        gate_made = m.sem("gate_made", start=1)
        turn_done, turn_read = m.sem("turn_done"), m.sem("turn_read")
        held = m.sem("held")
        stored = m.sem("stored")
        ex.begin(m, u_stream, a_out)
        NX = SELECT_TILES // PH
        block = m.block()

        def heads(eng, body):
            body(0, True, False)
            with eng.Fori(1, PH - 1) as hd:
                body(hd, False, False)
            body(PH - 1, False, True)

        @block.sync
        def _(sync):
            for i in range(2):
                sync.dma_start(xT[:, 4 * i:4 * i + 4, :], x_in[:, 4 * i:4 * i + 4, :]).then_inc(x_loaded[i], 16)
            sync.dma_start(g_sb[:], gain).then_inc(c_loaded, 16)
            sync.dma_start(keys[:], keysT).then_inc(c_loaded, 16)
            for c in range(2):
                sync.dma_start(w_raw[:, c], wstream[c]).then_inc(w_loaded[c], 16)
            for s in range(2):
                ex.load(sync, 0, s, 0, s, first=True)

            def body(hd, first, last):
                for i in range(NX):
                    if i in (0, 1) and not last:
                        sync.wait_ge(wlo_made, hd * 2 + (i + 1))
                        sync.dma_start(w_raw[:, i], wstream[ds(hd * 2 + (2 + i), 1)].rearrange("a p c n -> (a p) c n")
                                       ).then_inc(w_loaded[i], 16)
                    if not (last and i >= NX - 2):
                        ex.load(sync, 0, hd * NX + (i + 2), 0, i % 2)
                    ex.store(sync, 0, hd * NX + i, i % 2)

            heads(sync, body)
            sync.wait_ge(turn_read, 6)
            sync.dma_start(sel_out, resT).then_inc(stored, 16)
            ex.finish(sync, SELECT_TILES)
            sync.wait_ge(stored, 16)

        @block.gpsimd
        def _(pool):
            nc.gpsimd.memset(ones[:], 1.0).then_inc(made, 1)
            nc.gpsimd.iota(iota16[:], pattern=[[1, K]], base=0, channel_multiplier=0,
                           allow_small_or_imprecise_dtypes=True).then_inc(made, 1)
            pool.wait_ge(made, 2)
            nc.gpsimd.affine_select(out=ident[:], in_=ones[:], pattern=[[-1, P]], compare_op=ALU.is_equal, fill=0.0,
                                    base=0, channel_multiplier=1).then_inc(made, 1)

            def weights(n, c):
                pool.wait_ge(whi_made, n + 1)
                nc.gpsimd.tensor_tensor(w_lo[:, c], w_raw[:, c], w_hi[:, c].bitcast(F32), ALU.subtract).then_inc(wlo_made, 1)

            for c in range(2):
                weights(c, c)
            for s in range(2):
                ex.split_low(pool, s, s)

            def body(hd, first, last):
                for i in range(NX):
                    if i in (2, 3) and not last:
                        weights(hd * 2 + i, i - 2)
                    if not (last and i >= NX - 2):
                        ex.split_low(pool, hd * NX + (i + 2), i % 2)

            heads(pool, body)

        @block.tensor
        def _(pe):
            pe.wait_ge(made, 3)
            for k in range(NC):
                pe.wait_ge(sq_made, k + 1)
                for h in range(2):
                    mm = nc.tensor.matmul(gemm[:, h], ones[:], sq[:, k % 2, h * H:h * H + H], start=(k == 0), stop=(k == NC - 1))
                mm.then_inc(sq_used, 1)
            pe.wait_ge(hlo_made, NC)
            pe.wait_ge(c_loaded, 32)

            def queries(hd, c):
                pe.wait_ge(wlo_made, hd * 2 + (c + 1))
                for h in range(2):
                    pe.wait_ge(evicted[h], hd * 2 + (c + 1))
                    hs = slice(h * H, h * H + H)
                    three_pass(nc, gemm[:, h], [(w_hi[:, c, k], w_lo[:, c, k], ex.hhi[:, k, hs], ex.hlo[:, k, hs])
                                                for k in range(NC)]).then_inc(group_done, 1)

            def scores(hd, c):
                pe.wait_ge(evicted[1], hd * 2 + (c + 2))
                pe.wait_ge(evicted[0], hd * 2 + (c + 2))
                pe.wait_ge(sc_made, hd * 2 + 1)
                for t in range(NT):
                    mm = nc.tensor.matmul(scps[:, c, t], qT[:, c, t * P:t * P + P], keys[:, c], start=True, stop=True)
                mm.then_inc(scored, 1)

            def body(hd, first, last):
                for i in range(NX):
                    if i < 2:
                        queries(hd, i)
                    if i == 2:
                        scores(hd, 0)
                        scores(hd, 1)
                    ex.product(pe, hd * NX + i, i % 2)

            heads(pe, body)
            pe.wait_ge(gate_made, PH + 1)
            pe.wait_ge(hit_summed, 2 * PH + 1)
            for g in range(6):
                r, b = g // 2, g % 2
                if g >= 2:
                    pe.wait_ge(turn_read, g - 1)
                for x in range(4):
                    mm = nc.tensor.transpose(gemm[:, b, x * P:x * P + P],
                                             res[:, r, 4 * (g % 2) + x].rearrange("p h k -> p (h k)"), ident[:])
                mm.then_inc(turn_done, 1)

        @block.scalar
        def _(act):
            for k in range(NC):
                act.wait_ge(x_loaded[k // 4], 16)
                if k >= 2:
                    act.wait_ge(sq_used, k - 1)
                nc.scalar.activation(sq[:, k % 2], xT[:, k], ACT.Square).then_inc(sq_made, 1)

            for c in range(2):
                act.wait_ge(w_loaded[c], 16)
                nc.scalar.activation(w_hi[:, c], w_raw[:, c], ACT.Copy).then_inc(whi_made, 1)
            for s in range(2):
                ex.split_high(act, s, 0, s, first=True)
            norm.root(nc, act)
            for k in range(NC):
                act.wait_ge(h_made, k + 1)
                nc.scalar.activation(ex.hhi[:, k], xT[:, k], ACT.Copy).then_inc(hhi_made, 1)

            def body(hd, first, last):
                for i in range(NX):
                    if i < 2:
                        for h in range(2):
                            act.wait_ge(group_done, hd * 4 + (2 * i + h + 1))
                            act.wait_ge(scored, hd * 2 + 1)
                            nc.scalar.activation(qT[:, i, h * H:h * H + H], gemm[:, h], ACT.Copy).then_inc(evicted[h], 1)
                    if i == 2:
                        if not first:
                            act.wait_ge(shift_made, hd)
                            nc.scalar.activation(expv[:], shifted[:], ACT.Exp).then_inc(exp_made, 1)
                        for c in range(2):
                            act.wait_ge(scored, hd * 2 + (c + 2))
                            act.wait_ge(index16, hd * 16 + 1)
                            nc.scalar.activation(sc[:, c], scps[:, c], ACT.Copy).then_inc(sc_made, 1)
                        if not last:
                            for c in range(2):
                                act.wait_ge(w_loaded[c], hd * 16 + 32)
                                nc.scalar.activation(w_hi[:, c], w_raw[:, c], ACT.Copy).then_inc(whi_made, 1)
                    ex.activate(act, hd * NX + i, hd * (NX // 2) + i // 2, i % 2)
                    if not (last and i >= NX - 2):
                        ex.split_high(act, hd * NX + (i + 2), hd * (NX // 2) + (i // 2 + 1), i % 2)

            act.wait_ge(hlo_made, NC)
            heads(act, body)
            act.wait_ge(shift_made, PH)
            nc.scalar.activation(expv[:], shifted[:], ACT.Exp).then_inc(exp_made, 1)
            act.wait_ge(index16, PH * 16 + 1)
            for g in range(6):
                act.wait_ge(turn_done, g + 1)
                nc.scalar.activation(resT[:, g // 2, (g % 2) * H:(g % 2) * H + H], gemm[:, g % 2], ACT.Copy).then_inc(turn_read, 1)

        def alone(dve, sem, value):
            dve.wait_ge(sem, value)
            dve.sem_inc(held, 1)

        @block.vector
        def _(dve):
            dve.wait_ge(sq_used, NC)
            norm.start(nc, dve, [(slice(h * H, h * H + H), gemm[:, h]) for h in range(2)], lambda h: evicted[h])
            norm.finish(nc, dve)
            dve.wait_ge(norm.made, 1)
            dve.wait_ge(c_loaded, 32)
            for k in range(NC):
                nc.vector.scalar_tensor_tensor(out=xT[:, k], in0=xT[:, k], scalar=g_sb[:, k:k + 1], in1=norm.rstd[:],
                                               op0=ALU.mult, op1=ALU.mult).then_inc(h_made, 1)
            for k in range(NC):
                dve.wait_ge(hhi_made, k + 1)
                nc.vector.tensor_tensor(ex.hlo[:, k], xT[:, k], ex.hhi[:, k].bitcast(F32), ALU.subtract).then_inc(hlo_made, 1)
            units = [(c, t) for c in range(2) for t in range(NT)]
            NU = len(units)

            def gates(hd):
                dve.wait_ge(exp_made, hd + 1)
                nc.vector.tensor_reduce(total[:], expv[:], AX.X, ALU.add).then_inc(gate_step, 1)
                dve.wait_ge(gate_step, hd * 2 + 1)
                nc.vector.reciprocal(inv[:], total[:]).then_inc(gate_step, 1)
                dve.wait_ge(gate_step, hd * 2 + 2)
                nc.vector.tensor_tensor(res[:, 2, :, ds(hd, 1), :].rearrange("p t a k -> p t (a k)"), expv[:],
                                        inv[:].unsqueeze(2).to_broadcast([P, NT, K]), ALU.mult).then_inc(gate_made, 1)

            def body(hd, first, last):
                if not first:
                    gates(hd - 1)
                alone(dve, sc_made, hd * 2 + 3)
                for c, t in units:
                    nc.vector.max(top[:, c, t, 0:8], sc[:, c, t]).then_inc(first8, 1)
                alone(dve, first8, hd * NU + NU)
                for c, t in units:
                    nc.vector.max_index(idx[:, c, t, 0:8], top[:, c, t, 0:8], sc[:, c, t]).then_inc(index8, 1)
                    nc.vector.match_replace(sc2[:, c, t], top[:, c, t, 0:8], sc[:, c, t], LOWEST).then_inc(cut8, 1)
                alone(dve, cut8, hd * NU + NU)
                for c, t in units:
                    nc.vector.max(top[:, c, t, 8:16], sc2[:, c, t]).then_inc(last8, 1)
                alone(dve, last8, hd * NU + NU)
                for c, t in units:
                    nc.vector.max_index(idx[:, c, t, 8:16], top[:, c, t, 8:16], sc2[:, c, t]).then_inc(index16, 1)
                for t in range(NT):
                    nc.vector.tensor_tensor(cand[:, t].rearrange("p (a b) -> p a b", b=K),
                                            top[:, 0, t].unsqueeze(2).to_broadcast([P, K, K]),
                                            top[:, 1, t].unsqueeze(1).to_broadcast([P, K, K]), ALU.add).then_inc(cand_made, 1)
                dve.wait_ge(index8, hd * NU + NU)
                dve.wait_ge(index16, hd * NU + NU + 1)
                nc.vector.tensor_copy(idxf[:], idx[:]).then_inc(idxf_made, 1)
                alone(dve, cand_made, hd * NT + NT)
                for t in range(NT):
                    nc.vector.max(best[:, t, 0:8], cand[:, t]).then_inc(cfirst8, 1)
                alone(dve, cfirst8, hd * NT + NT)
                for t in range(NT):
                    nc.vector.max_index(bidx[:, t, 0:8], best[:, t, 0:8], cand[:, t]).then_inc(cindex8, 1)
                    nc.vector.match_replace(cand2[:, t], best[:, t, 0:8], cand[:, t], LOWEST).then_inc(ccut8, 1)
                alone(dve, ccut8, hd * NT + NT)
                for t in range(NT):
                    nc.vector.max(best[:, t, 8:16], cand2[:, t]).then_inc(clast8, 1)
                alone(dve, clast8, hd * NT + NT)
                for t in range(NT):
                    nc.vector.max_index(bidx[:, t, 8:16], best[:, t, 8:16], cand2[:, t]).then_inc(cindex16, 1)
                nc.vector.tensor_tensor(shifted[:], best[:], best[:, :, 0:1].to_broadcast([P, NT, K]), ALU.subtract
                                        ).then_inc(shift_made, 1)
                dve.wait_ge(cindex8, hd * NT + NT)
                dve.wait_ge(cindex16, hd * NT + NT)
                nc.vector.tensor_single_scalar(part[:, 0], bidx[:], 4, ALU.logical_shift_right).then_inc(part_made, 1)
                nc.vector.tensor_single_scalar(part[:, 1], bidx[:], K - 1, ALU.bitwise_and).then_inc(part_made, 1)
                dve.wait_ge(part_made, hd * 2 + 2)
                nc.vector.tensor_copy(partf[:], part[:]).then_inc(partf_made, 1)
                dve.wait_ge(partf_made, hd + 1)
                dve.wait_ge(idxf_made, hd + 1)
                for c in range(2):
                    dve.wait_ge(hit_summed, hd * 2 + c + 1)
                    nc.vector.tensor_tensor(hit[:], partf[:, c].unsqueeze(3).to_broadcast([P, NT, K, K]),
                                            iota16[:].unsqueeze(1).unsqueeze(1).to_broadcast([P, NT, K, K]), ALU.is_equal
                                            ).then_inc(hit_step, 1)
                    dve.wait_ge(hit_step, hd * 4 + (2 * c + 1))
                    nc.vector.tensor_tensor(hit[:], hit[:], idxf[:, c].unsqueeze(2).to_broadcast([P, NT, K, K]), ALU.mult
                                            ).then_inc(hit_step, 1)
                    dve.wait_ge(hit_step, hd * 4 + (2 * c + 2))
                    nc.vector.tensor_reduce(res[:, c, :, ds(hd, 1), :].rearrange("p t a k -> p t (a k)"), hit[:], AX.X, ALU.add
                                            ).then_inc(hit_summed, 1)

            dve.wait_ge(made, 3)
            heads(dve, body)
            gates(PH - 1)


def spread_phase(nc, ex, sel_in, u_stream, a_out, g_out):
    with Phase(nc, "spread") as m:
        B = 16
        NB = B // 4
        STEPS = P // B
        PER = (KEYS - SELECT_TILES) // NT
        EXTRA = PER - STEPS
        NS = EXTRA
        parts = m.sb("parts", [P, 5, T], BF16)
        iota = m.sb("iota", [P, KEYS], BF16)
        eq = m.sb("eq", [P, B, KEYS], BF16)
        one1 = m.sb("one1", [P, 2, B, KEYS], BF16)
        gate = m.sb("gate", [P, 3, 2, B, KEYS], BF16)
        stage = m.sb("stage", [P, KEYS, P])
        sel = stage[:, 0:3 * NT, :].rearrange("p (r t) n -> p r (t n)", r=3)
        ps = m.ps("g", [P, NB, 4, KEYS])

        loaded = m.sem("loaded")
        iota_made = m.sem("iota_made")
        part_made, rest_made = m.sem("part_made"), m.sem("rest_made")
        eq_made = m.sem("eq_made")
        one1_made = m.sem("one1_made")
        dve_gated, pool_gated = m.sem("dve_gated", start=4), m.sem("pool_gated", start=2)
        g_done = m.sem("g_done", start=2 * NB)
        staged = m.sem("staged", start=NB)
        stored = m.sem("stored", start=1)
        ex.begin(m, u_stream, a_out)
        block = m.block()

        def tiles(eng, step, extra):
            def tile(tt, last):
                with eng.Fori(0, STEPS // 2) as ss:
                    for b in range(2):
                        step(tt * STEPS + (ss * 2 + b), tt * PER + (ss * 2 + b), tt * (PER // 2) + ss, b, tt, ss * 2 + b)
                for i in range(EXTRA):
                    extra(i, tt, tt * PER + (STEPS + i), tt * (PER // 2) + (STEPS + i) // 2, i % 2,
                          EXTRA - 1 - i if last else EXTRA)

            with eng.Fori(0, NT - 1) as tt:
                tile(tt, False)
            tile(NT - 1, True)

        @block.sync
        def _(sync):
            sync.dma_start(sel, sel_in).then_inc(loaded, 16)
            for s in range(2):
                ex.load(sync, SELECT_TILES, s, 0, s, first=True)

            def step(n, tile, half, b, tt, st):
                ex.load(sync, SELECT_TILES, tile + 2, half + 1, b)
                ex.store(sync, SELECT_TILES, tile, b)

            def extra(i, tt, tile, half, b, left):
                if left >= 2:
                    ex.load(sync, SELECT_TILES, tile + 2, half + 1, b)
                sync.wait_ge(staged, tt * (STEPS * NB) + (STEPS * NB + NB))
                part = slice(i * KEYS // NS, (i + 1) * KEYS // NS)
                sync.dma_start(g_out[part].rearrange("a p t -> p a t")[:, :, ds(tt * P, P)], stage[:, part, :]
                               ).then_inc(stored, 16)
                ex.store(sync, SELECT_TILES, tile, b)

            tiles(sync, step, extra)
            ex.finish(sync, KEYS - SELECT_TILES)
            sync.wait_ge(stored, 16 * NS * NT + 1)

        @block.gpsimd
        def _(pool):
            nc.gpsimd.iota(iota[:], pattern=[[1, KEYS]], base=0, channel_multiplier=0,
                           allow_small_or_imprecise_dtypes=True).then_inc(iota_made, 1)
            ex.split_low(pool, 0, 0)
            pool.wait_ge(part_made, 5)

            def step(n, tile, half, b, tt, st):
                pool.wait_ge(eq_made, n + 1)
                pool.wait_ge(g_done, n * NB + NB)
                nc.gpsimd.tensor_tensor(gate[:, 2, b], eq[:], parts[:, 4, ds(n * B, B)].unsqueeze(2).to_broadcast([P, B, KEYS]),
                                        ALU.mult).then_inc(pool_gated, 1)
                ex.split_low(pool, tile + 1, 1 - b)

            def extra(i, tt, tile, half, b, left):
                if left >= 1:
                    ex.split_low(pool, tile + 1, 1 - b)

            tiles(pool, step, extra)

        @block.vector
        def _(dve):
            for i in range(2):
                dve.wait_ge(part_made, 3 + i)
                nc.vector.tensor_tensor(sel[:, 2], sel[:, 2], parts[:, 2 + i], ALU.subtract).then_inc(rest_made, 1)
            dve.wait_ge(part_made, 5)
            dve.wait_ge(iota_made, 1)

            def one_hot(dst, row, n):
                return nc.vector.tensor_tensor(dst, iota[:].unsqueeze(1).to_broadcast([P, B, KEYS]),
                                               parts[:, row, ds(n * B, B)].unsqueeze(2).to_broadcast([P, B, KEYS]),
                                               ALU.is_equal)

            def step(n, tile, half, b, tt, st):
                dve.wait_ge(g_done, n * NB + NB)
                one_hot(one1[:, b], 0, n).then_inc(one1_made, 1)
                dve.wait_ge(pool_gated, n + 2)
                dve.wait_ge(dve_gated, n * 2 + 4)
                one_hot(eq[:], 1, n).then_inc(eq_made, 1)
                dve.wait_ge(eq_made, n + 1)
                for i in range(2):
                    nc.vector.tensor_tensor(gate[:, i, b], eq[:],
                                            parts[:, 2 + i, ds(n * B, B)].unsqueeze(2).to_broadcast([P, B, KEYS]),
                                            ALU.mult).then_inc(dve_gated, 1)

            tiles(dve, step, lambda *a: None)

        @block.tensor
        def _(pe):
            def step(n, tile, half, b, tt, st):
                pe.wait_ge(one1_made, n + 1)
                pe.wait_ge(dve_gated, n * 2 + 6)
                pe.wait_ge(pool_gated, n + 3)
                for bank in range(NB):
                    pe.wait_ge(staged, n * NB + (bank + 1))
                    for x in range(4):
                        t = 4 * bank + x
                        for i in range(3):
                            mm = nc.tensor.matmul(ps[:, bank, x], one1[:, b, t], gate[:, i, b, t], start=(i == 0), stop=(i == 2))
                    mm.then_inc(g_done, 1)
                ex.product(pe, tile, b)

            tiles(pe, step, lambda i, tt, tile, half, b, left: ex.product(pe, tile, b))

        @block.scalar
        def _(act):
            act.wait_ge(loaded, 16)
            for i in range(5):
                if i >= 3:
                    act.wait_ge(rest_made, i - 2)
                nc.scalar.activation(parts[:, i], sel[:, min(i, 2)], ACT.Copy).then_inc(part_made, 1)
            for s in range(2):
                ex.split_high(act, s, 0, s, first=True)

            def step(n, tile, half, b, tt, st):
                act.wait_ge(stored, tt * (16 * NS) + 1)
                for bank in range(NB):
                    act.wait_ge(g_done, n * NB + (2 * NB + bank + 1))
                    nc.scalar.activation(stage[:, :, ds(st * B + 4 * bank, 4)], ps[:, bank].rearrange("p t i -> p i t"), ACT.Copy
                                         ).then_inc(staged, 1)
                ex.activate(act, tile, half, b)
                ex.split_high(act, tile + 2, half + 1, b)

            def extra(i, tt, tile, half, b, left):
                ex.activate(act, tile, half, b)
                if left >= 2:
                    ex.split_high(act, tile + 2, half + 1, b)

            tiles(act, step, extra)


def expert_phase(nc, a_in, x_in, g_in, v_stream, final_gain, out):
    with Phase(nc, "expert") as m:
        E = 4
        NG = KEYS // E
        NQ = 4
        QC = NC // NQ
        QG = 2 * QC
        SG = NQ * QG
        acc = m.sb("acc", [P, NC, T])
        g_sb = m.sb("gain", [P, NC])
        ones = m.sb("ones", [P, P])
        vraw = m.sb("vraw", [P, NQ, E, QC * P])
        vhi = m.sb("vhi", [P, NQ, E, QC * P], F32R)
        vlo = m.sb("vlo", [P, NQ, E, QC * P], F32R)
        graw = m.sb("graw", [P, E, T])
        act = m.sb("act", [P, E, T])
        ahi = m.sb("ahi", [P, 2, E, T], F32R)
        alo = m.sb("alo", [P, 2, E, T], F32R)
        ops = m.ps("o", [P, QC, 2, H])
        sums = m.ps("sums", [P, 2, H])

        x_loaded, c_loaded = m.sem("x_loaded"), m.sem("c_loaded")
        ones_made = m.sem("ones_made")
        a_loaded = [m.sem(f"a_loaded{e}") for e in range(E)]
        g_loaded = [m.sem(f"g_loaded{e}") for e in range(E)]
        v_loaded = [m.sem(f"v_loaded{q}") for q in range(NQ)]
        vhi_made, vlo_made = m.sem("vhi_made"), m.sem("vlo_made")
        gated = m.sem("gated")
        ahi_made, alo_made = m.sem("ahi_made"), m.sem("alo_made")
        o_done = m.sem("o_done", start=2 * SG)
        added = m.sem("added", start=QG)
        sq_made, sq_used, sum_read = m.sem("sq_made"), m.sem("sq_used"), [m.sem(f"sum_read{h}") for h in range(2)]
        step, rooted = m.sem("step"), m.sem("rooted")
        y_made, stored = m.sem("y_made"), m.sem("stored")
        block = m.block()

        def groups(eng, body):
            with eng.Fori(0, NG // 2) as gg:
                for par in range(2):
                    body(gg * 2 + par, par)

        @block.sync
        def _(sync):
            def load_tile(e, i, j):
                if j is not None:
                    sync.wait_ge(alo_made, j)
                sync.dma_start(act[:, e], a_in[i].rearrange("a p t -> (a p) t")).then_inc(a_loaded[e], 16)
                sync.dma_start(graw[:, e], g_in[i].rearrange("a p t -> (a p) t")).then_inc(g_loaded[e], 16)

            def load_values(q, i, j):
                if j is not None:
                    sync.wait_ge(vlo_made, j)
                sync.dma_start(vraw[:, q], v_stream[i, q].rearrange("a p e n -> (a p) e n")).then_inc(v_loaded[q], 16)

            for e in range(E):
                load_tile(e, ds(e, 1), None)
            for q in range(NQ):
                load_values(q, ds(0, 1), None)
                if q == 0:
                    sync.dma_start(acc[:], x_in).then_inc(x_loaded, 16)
            sync.dma_start(g_sb[:], final_gain).then_inc(c_loaded, 16)
            with sync.Fori(0, NG - 1) as g:
                for e in range(E):
                    load_tile(e, ds(g * E + (E + e), 1), g * E + (e + 1))
                for q in range(NQ):
                    load_values(q, ds(g + 1, 1), g * NQ + (q + 1))
            for k in range(NC):
                sync.wait_ge(y_made, k + 1)
                sync.dma_start(out[:, k], acc[:, k]).then_inc(stored, 16)
            sync.wait_ge(stored, 16 * NC)

        def split_low(eng, low, raw, high):
            return eng.tensor_tensor(low, raw, high.bitcast(F32), ALU.subtract)

        @block.gpsimd
        def _(pool):
            nc.gpsimd.memset(ones[:], 1.0).then_inc(ones_made, 1)

            def body(g, par):
                for q in range(NQ):
                    pool.wait_ge(vhi_made, g * NQ + (q + 1))
                    split_low(nc.gpsimd, vlo[:, q], vraw[:, q], vhi[:, q]).then_inc(vlo_made, 1)

            groups(pool, body)

        @block.scalar
        def _(act_eng):
            def body(g, par):
                for e in range(E):
                    act_eng.wait_ge(gated, g * E + (e + 1))
                    act_eng.wait_ge(o_done, g * SG + SG)
                    nc.scalar.activation(ahi[:, par, e], act[:, e], ACT.Copy).then_inc(ahi_made, 1)
                    q = e
                    act_eng.wait_ge(v_loaded[q], g * 16 + 16)
                    act_eng.wait_ge(o_done, g * SG + (SG + (q + 1) * QG))
                    nc.scalar.activation(vhi[:, q], vraw[:, q], ACT.Copy).then_inc(vhi_made, 1)

            groups(act_eng, body)
            for k in range(NC):
                act_eng.wait_ge(added, QG + (NG - 1) * SG + (k + 1) * 2)
                if k >= 2:
                    act_eng.wait_ge(sq_used, k - 1)
                nc.scalar.activation(act[:, k % 2], acc[:, k], ACT.Square).then_inc(sq_made, 1)
            act_eng.wait_ge(step, 1)
            nc.scalar.activation(graw[:, 1], act[:, 2], ACT.Sqrt).then_inc(rooted, 1)

        @block.vector
        def _(dve):
            def gate(g, par, e):
                dve.wait_ge(a_loaded[e], g * 16 + 16)
                dve.wait_ge(g_loaded[e], g * 16 + 16)
                nc.vector.tensor_tensor(act[:, e], act[:, e], graw[:, e], ALU.mult).then_inc(gated, 1)

            def split(g, par, e):
                dve.wait_ge(ahi_made, g * E + (e + 1))
                split_low(nc.vector, alo[:, par, e], act[:, e], ahi[:, par, e]).then_inc(alo_made, 1)

            def add(g, w):
                q, d, h = w // QG, w // 2 % QC, w % 2
                k = q * QC + d
                dve.wait_ge(o_done, g * SG + (2 * SG + w + 1))
                nc.vector.tensor_tensor(acc[:, k, h * H:h * H + H], acc[:, k, h * H:h * H + H], ops[:, d, h], ALU.add
                                        ).then_inc(added, 1)

            for e in range(E):
                gate(0, 0, e)
                split(0, 0, e)
            dve.wait_ge(x_loaded, 16)

            def body(g, par, last=False):
                for w in range(SG):
                    add(g, w)
                    if not last and w % 4 == 1:
                        gate(g + 1, 1 - par, w // 4)
                    if not last and w % 4 == 3:
                        split(g + 1, 1 - par, w // 4)

            with dve.Fori(0, NG // 2 - 1) as gg:
                for par in range(2):
                    body(gg * 2 + par, par)
            body(NG - 2, 0)
            body(NG - 1, 1, last=True)
            dve.wait_ge(sq_used, NC)
            mean, inv, rstd = graw[:, 0], act[:, 2], graw[:, 1]
            for h in range(2):
                nc.vector.tensor_scalar(mean[:, h * H:h * H + H], sums[:, h], 1.0 / D, EPS, ALU.mult, ALU.add
                                        ).then_inc(sum_read[h], 1)
                dve.wait_ge(sum_read[h], 1)
            nc.vector.reciprocal(inv, mean).then_inc(step, 1)
            dve.wait_ge(rooted, 1)
            nc.vector.tensor_tensor(inv, mean, rstd, ALU.mult).then_inc(step, 1)
            dve.wait_ge(step, 2)
            nc.vector.tensor_tensor(inv, inv, rstd, ALU.mult).then_inc(step, 1)
            dve.wait_ge(step, 3)
            nc.vector.tensor_scalar(inv, inv, -0.5, 1.5, ALU.mult, ALU.add).then_inc(step, 1)
            dve.wait_ge(step, 4)
            nc.vector.tensor_tensor(rstd, rstd, inv, ALU.mult).then_inc(step, 1)
            dve.wait_ge(step, 5)
            dve.wait_ge(c_loaded, 16)
            for k in range(NC):
                nc.vector.scalar_tensor_tensor(out=acc[:, k], in0=acc[:, k], scalar=g_sb[:, k:k + 1], in1=rstd,
                                               op0=ALU.mult, op1=ALU.mult).then_inc(y_made, 1)

        @block.tensor
        def _(pe):
            def body(g, par):
                pe.wait_ge(ahi_made, g * E + E)
                pe.wait_ge(alo_made, g * E + E)
                for w in range(SG):
                    q, d, h = w // QG, w // 2 % QC, w % 2
                    if w % QG == 0:
                        pe.wait_ge(vhi_made, g * NQ + (q + 1))
                        pe.wait_ge(vlo_made, g * NQ + (q + 1))
                    pe.wait_ge(added, g * SG + (w + 1))
                    hs, dp = slice(h * H, h * H + H), slice(d * P, d * P + P)
                    three_pass(nc, ops[:, d, h], [(vhi[:, q, e, dp], vlo[:, q, e, dp], ahi[:, par, e, hs], alo[:, par, e, hs])
                                                  for e in range(E)]).then_inc(o_done, 1)

            groups(pe, body)
            pe.wait_ge(ones_made, 1)
            for k in range(NC):
                pe.wait_ge(sq_made, k + 1)
                for h in range(2):
                    mm = nc.tensor.matmul(sums[:, h], ones[:], act[:, k % 2, h * H:h * H + H], start=(k == 0), stop=(k == NC - 1))
                mm.then_inc(sq_used, 1)


def build(nc, a, out):
    def scratch(name, shape):
        return nc.dram_tensor(name, shape, F32).ap()

    full = [P, NC, T]
    h1, conv, attn = scratch("h1", full), scratch("conv", full), scratch("attn", full)
    x1, x2, sel = scratch("x1", full), scratch("x2", full), scratch("sel", [P, 3, T])
    gelu_u, gates = scratch("gelu_u", [KEYS, P, T]), scratch("gates", [KEYS, P, T])
    mixer_phase(nc, a["x"], a["mix_gain"], a["w_mix"], a["conv_w"], h1, conv, attn)
    merge_phase(nc, a["x"], h1, conv, attn, a["w_merge"], a["ln_g"], a["ln_b"], a["gate_b"], x1)
    cross_attention_phase(nc, x1, a["x_gain"], a["mem"], a["mem_gain"], a["w_cross"], x2)
    with ExitStack() as tensors:
        experts = Experts1(nc, tensors)
        select_phase(nc, experts, x2, a["ffn_gain"], a["keys"], a["w_query"], a["peer_u"], gelu_u, sel)
        spread_phase(nc, experts, sel, a["peer_u"], gelu_u, gates)
    expert_phase(nc, gelu_u, x2, gates, a["peer_v"], a["final_gain"], out)


def kernel(x, mem, norm_mix_g, w_in, b_gate, conv_dw_w, conv_dw_b, conv_ln_g, conv_ln_b,
           w_conv_out, w_attn_out, w_out, norm_xattn_g, norm_mem_g, w_xq, w_xkv, w_xo,
           norm_ffn_g, w_peer_q, peer_sub_keys, peer_u, peer_v, norm_final_g):
    import concourse.bacc as bacc
    from concourse.bass_utils import run_bass_kernel_spmd

    def channels(t):
        return t.T.reshape(NC, P, -1).transpose(1, 0, 2)

    def vector(t):
        return t.reshape(-1, P).T

    def chunks(w):
        return w.reshape(NC, P, -1, P).transpose(2, 1, 0, 3)

    w = np.asarray(w_in)[0]
    val, gate, q, k, v, g_conv, g_attn = [chunks(w[:, i * D:(i + 1) * D]) for i in range(7)]
    xq, xo = chunks(np.asarray(w_xq)[0]), chunks(np.asarray(w_xo)[0])
    xk, xv = [chunks(np.asarray(w_xkv)[0][:, i * D:(i + 1) * D]) for i in range(2)]
    per_head = [t.reshape(XH, 2, P, NC, P) for t in (xq, xk, xv)]
    flat = (-1, P, NC, P)
    arrays = {
        "x": channels(np.asarray(x)[0]),
        "mem": channels(np.asarray(mem)[0]),
        "mix_gain": vector(np.asarray(norm_mix_g)[0]),
        "w_mix": np.stack([gate, val, q, k, v], 1).reshape(flat),
        "conv_w": np.concatenate([np.asarray(conv_dw_w)[0], np.asarray(conv_dw_b)]).T.reshape(NC, P, TAPS + 1).transpose(1, 0, 2),
        "w_merge": np.concatenate([np.stack([g_conv, chunks(np.asarray(w_conv_out)[0]), g_attn,
                                             chunks(np.asarray(w_attn_out)[0])], 1).reshape(flat),
                                   chunks(np.asarray(w_out)[0])]),
        "ln_g": vector(np.asarray(conv_ln_g)[0]),
        "ln_b": vector(np.asarray(conv_ln_b)[0]),
        "gate_b": np.asarray(b_gate)[0].reshape(2, NC, P).transpose(2, 0, 1),
        "x_gain": vector(np.asarray(norm_xattn_g)[0]),
        "mem_gain": vector(np.asarray(norm_mem_g)[0]),
        "w_cross": np.concatenate([np.stack(per_head, 1).reshape(flat), xo]),
        "ffn_gain": vector(np.asarray(norm_ffn_g)[0]),
        "w_query": chunks(np.asarray(w_peer_q)[0]),
        "keys": np.asarray(peer_sub_keys)[0].transpose(2, 0, 1),
        "peer_u": np.asarray(peer_u)[0].reshape(P, KEYS, NC, P).transpose(1, 3, 2, 0),
        "peer_v": np.asarray(peer_v)[0].reshape(P, KEYS // 4, 4, 4, D // 4).transpose(1, 3, 0, 2, 4),
        "final_gain": vector(np.asarray(norm_final_g)),
    }
    arrays = {f"in_{n}": np.ascontiguousarray(t) for n, t in arrays.items()}
    nc = bacc.Bacc("TRN2", target_bir_lowering=False, num_devices=1)
    aps = {n: nc.dram_tensor(n, list(t.shape), F32, kind="ExternalInput").ap() for n, t in arrays.items()}
    out = nc.dram_tensor("out", [P, NC, T], F32, kind="ExternalOutput").ap()
    build(nc, {n[3:]: ap for n, ap in aps.items()}, out)
    r = run_bass_kernel_spmd(nc, [arrays], core_ids=[0])
    got = r.results[0]["out"]
    return np.ascontiguousarray(got.transpose(1, 0, 2).reshape(D, T).T)[None]
```

```python
from contextlib import ExitStack

import numpy as np
import concourse.bass as bass
from concourse import mybir

P = 128
D = 1024
T = 1024
M = 256
NC = D // P
NT = T // P
H = 512
TAPS = 31
PAD = TAPS - 1
SELECT_TILES = 48
SB_HD = 64
XH = 4
PH = 8
KEYS = 128
TOPK = 16
EPS = 1e-6
LOWEST = -3.4028235e38

F32 = mybir.dt.float32
F32R = mybir.dt.float32r
BF16 = mybir.dt.bfloat16
U32 = mybir.dt.uint32
ALU = mybir.AluOpType
ACT = mybir.ActivationFunctionType
AX = mybir.AxisListType
ds = bass.ds


class Phase:

    def __init__(self, nc, tag):
        self.nc, self.tag, self.tensors, self.sems = nc, tag, ExitStack(), []

    def __enter__(self):
        return self

    def sb(self, name, shape, dt=F32):
        return self.tensors.enter_context(self.nc.sbuf_tensor(f"{self.tag}_{name}", shape, dt))

    def ps(self, name, shape):
        return self.tensors.enter_context(self.nc.psum_tensor(f"{self.tag}_{name}", shape, F32))

    def sem(self, name, start=0):
        self.sems.append(self.nc.alloc_semaphore(name=f"{self.tag}_{name}"))
        if start:
            self.nc.gpsimd.sem_inc(self.sems[-1], start)
        return self.sems[-1]

    def block(self):
        self.nc.all_engine_barrier()
        return self.tensors.enter_context(self.nc.Block())

    def __exit__(self, *error):
        self.tensors.close()
        if not any(error):
            self.nc.clear_and_free_semaphores(self.sems)
            self.nc.all_engine_barrier()


class Rsqrt:

    def __init__(self, m, name, n, room=None):
        self.mean, self.inv, self.rstd = room or [m.sb(f"{name}_{what}", [P, n])[:] for what in ("mean", "inv", "rstd")]
        self.step = m.sem(f"{name}_step")
        self.logged = m.sem(f"{name}_logged")
        self.rooted = m.sem(f"{name}_rooted")
        self.made = m.sem(f"{name}_made")

    def start(self, nc, dve, sums, psum_free):
        for i, (cols, src) in enumerate(sums):
            nc.vector.tensor_scalar(self.mean[:, cols], src, 1.0 / D, EPS, ALU.mult, ALU.add).then_inc(psum_free(i), 1)
        for i in range(len(sums)):
            dve.wait_ge(psum_free(i), 1)
        dve.sem_inc(self.step, 1)

    def root(self, nc, act):
        act.wait_ge(self.step, 1)
        nc.scalar.activation(self.rstd, self.mean, ACT.Ln).then_inc(self.logged, 1)
        act.wait_ge(self.logged, 1)
        nc.scalar.activation(self.rstd, self.rstd, ACT.Exp, scale=-0.5).then_inc(self.rooted, 1)

    def finish(self, nc, dve):
        dve.wait_ge(self.rooted, 1)
        nc.vector.scalar_tensor_tensor(out=self.inv, in0=self.rstd, scalar=-0.5, in1=self.rstd,
                                       op0=ALU.mult, op1=ALU.mult).then_inc(self.step, 1)
        dve.wait_ge(self.step, 2)
        nc.vector.tensor_tensor(self.inv, self.inv, self.mean, ALU.mult).then_inc(self.step, 1)
        dve.wait_ge(self.step, 3)
        nc.vector.scalar_tensor_tensor(out=self.rstd, in0=self.inv, scalar=1.5, in1=self.rstd,
                                       op0=ALU.add, op1=ALU.mult).then_inc(self.made, 1)


class SumSquares:

    def __init__(self, m, sq, total, out):
        self.sq, self.total, self.out = sq, total, out
        self.made, self.added, self.done = m.sem("sq_made"), m.sem("sq_added"), m.sem("sq_summed")

    def square(self, nc, act, k, x):
        if k >= 3:
            act.wait_ge(self.added, k - 1)
        dst = self.sq[:, k % 2] if k else self.total
        nc.scalar.activation(dst, x, ACT.Square).then_inc(self.made, 1)

    def add(self, nc, dve, k):
        dve.wait_ge(self.made, k + 1)
        if k == 0:
            dve.sem_inc(self.added, 1)
            return
        dve.wait_ge(self.added, k)
        nc.vector.tensor_tensor(self.total, self.total, self.sq[:, k % 2], ALU.add).then_inc(self.added, 1)

    def sum(self, nc, pe, ones):
        pe.wait_ge(self.added, NC)
        for h in range(2):
            mm = nc.tensor.matmul(self.out[:, h], ones, self.total[:, h * H:h * H + H], start=True, stop=True)
        mm.then_inc(self.done, 1)


def three_pass(nc, out, terms, first=True, last=True):
    for i, (whi, wlo, xhi, xlo) in enumerate(terms):
        nc.tensor.matmul(out, whi, xhi, start=(first and i == 0), stop=False)
        nc.tensor.matmul(out, whi, xlo, start=False, stop=False)
        mm = nc.tensor.matmul(out, wlo, xhi, start=False, stop=(last and i == len(terms) - 1))
    return mm


class WeightStream:

    def __init__(self, nc, m):
        self.nc = nc
        self.raw = m.sb("w_raw", [P, 2, NC, P])
        self.hi, self.lo = m.sb("w_hi", [P, 2, NC, P], F32R), m.sb("w_lo", [P, 2, NC, P], F32R)
        self.loaded = [m.sem(f"w_loaded{s}") for s in range(2)]
        self.hi_made, self.lo_made = m.sem("whi_made"), m.sem("wlo_made")

    def load(self, sync, stream, n, slot, first=False):
        if not first:
            sync.wait_ge(self.lo_made, n - 1)
        sync.dma_start(self.raw[:, slot], stream[ds(n, 1)].rearrange("a p c n -> (a p) c n")).then_inc(self.loaded[slot], 16)

    def split_high(self, act, n, half, slot):
        act.wait_ge(self.loaded[slot], half * 16 + 16)
        self.nc.scalar.activation(self.hi[:, slot], self.raw[:, slot], ACT.Copy).then_inc(self.hi_made, 1)

    def split_low(self, pool, n, slot):
        pool.wait_ge(self.hi_made, n + 1)
        self.nc.gpsimd.tensor_tensor(self.lo[:, slot], self.raw[:, slot], self.hi[:, slot].bitcast(F32), ALU.subtract
                                     ).then_inc(self.lo_made, 1)

    def ready(self, pe, n):
        pe.wait_ge(self.hi_made, n + 1)
        pe.wait_ge(self.lo_made, n + 1)


def mixer_phase(nc, xT, gain, wstream, conv_w, y_out, attn_out, gate_out):
    with Phase(nc, "mix") as m:
        NW = 7
        CHUNKS = NC * NW
        GROUPS = [(c, h) for c in (0, 1, 2, 3, 4, 5, "turn", 6) for h in range(2)]
        NG = len(GROUPS)
        NB = NG // 2
        hhi, hlo = m.sb("hhi", [P, NC, T], F32R), m.sb("hlo", [P, NC, T], F32R)
        room = m.sb("room", [P, NC, T])
        ybuf = room[:, 0:2]
        v = room[:, 2:4].rearrange("p b (t n) -> p b t n", n=P)
        logit = room[:, 4:6]
        vT = room[:, 6]
        cgate = room[:, 7]
        q_hi, q_lo = m.sb("q_hi", [P, 2, T], F32R), m.sb("q_lo", [P, 2, T], F32R)
        k_hi, k_lo = m.sb("k_hi", [P, 2, T], F32R), m.sb("k_lo", [P, 2, T], F32R)
        oT = m.sb("oT", [P, 2, T])
        sq = oT
        g_sb = m.sb("gain", [P, NC])
        ones = m.sb("ones", [P, P])
        ident = m.sb("ident", [P, P])
        tri_made, rest_made = m.sb("tri_made", [P, P]), m.sb("rest_made", [P, P])
        tri = m.sb("tri", [P, P], F32R)
        rest = m.sb("rest", [P, P], F32R)
        causal = m.sb("causal", [P, P])
        w = WeightStream(nc, m)
        u = m.sb("u", [P, 2, PAD + T])
        cw = m.sb("cw", [P, NC, TAPS + 1])
        cwj = m.sb("cwj", [P, TAPS + 1])
        expz = m.sb("expz", [P, 2, H])
        ln = m.sb("ln", [P, 2, H])
        sp = m.sb("softplus", [P, 2, H])
        sp_hi, sp_lo = m.sb("sp_hi", [P, 2, H], F32R), m.sb("sp_lo", [P, 2, H], F32R)
        ls = m.sb("logsig", [P, 2, H])
        lw = m.sb("logw", [P, 2, H])
        wt = m.sb("weight", [P, 2, H])
        norm = Rsqrt(m, "norm", T, [b[:].rearrange("p s h -> p (s h)") for b in (ls, lw, wt)])

        gemm = m.ps("gemm", [P, 2, H])
        zps = m.ps("z", [P, 2, H])
        cps = m.ps("c", [P, 2, H])
        ops = m.ps("o", [P, 2, H])

        x_loaded = [m.sem(f"x_loaded{i}") for i in range(4)]
        c_loaded = m.sem("c_loaded")
        const_made = m.sem("const_made")
        squares = SumSquares(m, sq, norm.inv, gemm)
        h_made = m.sem("h_made")
        hhi_made, hlo_made = m.sem("hhi_made"), m.sem("hlo_made")
        group_done = m.sem("group_done")
        evicted = [m.sem(f"evicted{b}") for b in range(2)]
        qk_high = m.sem("qk_high")
        cgate_step, cgate_made = m.sem("cgate_step"), m.sem("cgate_made")
        u_made = m.sem("u_made", start=1)
        cwj_made = m.sem("cwj_made")
        conv_step = m.sem("conv_step")
        logit_made = m.sem("logit_made")
        logit_stored = [m.sem(f"logit_stored{b}", start=1) for b in range(2)]
        y_stored = [m.sem(f"y_stored{b}", start=1) for b in range(2)]
        o_copied = m.sem("o_copied", start=1)
        o_stored = [m.sem(f"o_stored{b}", start=1) for b in range(2)]
        z_done = [m.sem(f"z_done{s}") for s in range(2)]
        act_step = [m.sem(f"act_step{s}") for s in range(2)]
        ln_done = [m.sem(f"ln_done{s}") for s in range(2)]
        sp_raw = [m.sem(f"sp_raw{s}") for s in range(2)]
        sp_done = [m.sem(f"sp_done{s}") for s in range(2)]
        sp_hi_made = [m.sem(f"sp_hi_made{s}") for s in range(2)]
        sp_lo_made = [m.sem(f"sp_lo_made{s}", start=1) for s in range(2)]
        ones_copied = m.sem("ones_copied")
        c_done = [m.sem(f"c_done{s}") for s in range(2)]
        ls_done = [m.sem(f"ls_done{s}", start=1) for s in range(2)]
        lw_done = [m.sem(f"lw_done{s}", start=1) for s in range(2)]
        wt_raw = [m.sem(f"wt_raw{s}") for s in range(2)]
        wt_done = [m.sem(f"wt_done{s}", start=1) for s in range(2)]
        sp_used = [m.sem(f"sp_used{s}", start=1) for s in range(2)]
        pv_done = [m.sem(f"pv_done{s}", start=1) for s in range(2)]

        cells = [(qh, kb) for qh in range(2) for kb in range(4 * qh + 3, -1, -1)]
        NCELL = len(cells)
        col0 = [max(0, kb - 4 * qh) * P for qh, kb in cells]
        masked = [kb >= 4 * qh for qh, kb in cells]
        NMASK = sum(masked)
        opens = [kb == 4 * qh + 3 for qh, kb in cells]
        closes = [kb == 0 for qh, kb in cells]

        def pairs(eng, body):
            with eng.Fori(0, NC // 2 - 1) as jj:
                for par in range(2):
                    body(jj * 2 + par, par, jj, NW + 2)
            for par in range(2):
                body(NC - 2 + par, par, NC // 2 - 1, NW * (1 - par))

        def following(j, par, jj):
            return j + 1, 1 - par, jj + par

        def chunk(j, par, jj, c):
            return j * NW + c, jj * NW + (NW * par + c) // 2, (par + c) % 2

        PLACES = 2 * (NCELL - 1)

        def halves(place):
            return range(place * 2 * NG // PLACES, (place + 1) * 2 * NG // PLACES) if place < PLACES else ()

        ends = [[u // 2 for p in (2 * i, 2 * i + 1) for u in halves(p) if u % 2] for i in range(NCELL)]

        def mask_count(j, i):
            return NMASK * j + sum(masked[:i])

        def bank_evicted(eng, j, g):
            eng.wait_ge(evicted[g % 2], NB * j + g // 2 + 2)

        TAPS_AT = [(0, 2)] + [(1, 2)] * 9 + [(1, 1), (0, 0)]

        def low_part(eng, of, j, s, i):
            a = col0[i]
            eng.wait_ge(sp_hi_made[s], NCELL * j + i + 1)
            of.tensor_tensor(sp_lo[:, s, a:H], sp[:, s, a:H], sp_hi[:, s, a:H].bitcast(F32), ALU.subtract
                             ).then_inc(sp_lo_made[s], 1)

        QK_SCALE = (float(SB_HD) ** -0.5, 1.0)
        block = m.block()

        @block.sync
        def _(sync):
            for i in range(4):
                sync.dma_start(room[:, 2 * i:2 * i + 2, :], xT[:, 2 * i:2 * i + 2, :]).then_inc(x_loaded[i], 16)
            sync.dma_start(g_sb[:], gain).then_inc(c_loaded, 16)
            sync.dma_start(cw[:], conv_w).then_inc(c_loaded, 16)
            for n in range(NW + 2):
                w.load(sync, wstream, n, n % 2, first=(n < 2))

            def store_logits(j):
                for b in range(2):
                    sync.wait_ge(logit_made, 4 * j + 2 * b + 2)
                    sync.dma_start(gate_out[:, b, ds(j, 1), :], logit[:, b:b + 1, :]).then_inc(logit_stored[b], 16)

            store_logits(0)

            def body(j, par, jj, more):
                nj, npar, njj = following(j, par, jj)
                for c in range(2, more):
                    n, _, slot = chunk(nj, npar, njj, c)
                    w.load(sync, wstream, n, slot)
                sync.wait_ge(conv_step, TAPS * j + TAPS)
                sync.dma_start(y_out[:, ds(j, 1), :], ybuf[:, par:par + 1, :]).then_inc(y_stored[par], 16)
                if more:
                    store_logits(nj)
                sync.wait_ge(o_copied, 4 * j + 4 + 1)
                sync.dma_start(attn_out[:, ds(j, 1), :], oT[:, par:par + 1, :]).then_inc(o_stored[par], 16)

            pairs(sync, body)
            for b in range(2):
                sync.wait_ge(logit_stored[b], 16 * NC + 1)
                sync.wait_ge(y_stored[b], 16 * (NC // 2) + 1)
                sync.wait_ge(o_stored[b], 16 * (NC // 2) + 1)

        @block.gpsimd
        def _(pool):
            nc.gpsimd.memset(ones[:], 1.0).then_inc(const_made, 1)
            nc.gpsimd.memset(u[:, :, 0:PAD], 0.0).then_inc(const_made, 1)
            pool.wait_ge(const_made, 2)
            nc.gpsimd.affine_select(out=tri_made[:], in_=ones[:], pattern=[[-1, P]], compare_op=ALU.is_gt, fill=0.0,
                                    base=0, channel_multiplier=1).then_inc(const_made, 1)
            nc.gpsimd.affine_select(out=rest_made[:], in_=ones[:], pattern=[[1, P]], compare_op=ALU.is_ge, fill=0.0,
                                    base=0, channel_multiplier=-1).then_inc(const_made, 1)
            nc.gpsimd.affine_select(out=causal[:], in_=ones[:], pattern=[[1, P]], compare_op=ALU.is_gt, fill=0.0,
                                    base=0, channel_multiplier=-1).then_inc(const_made, 1)
            nc.gpsimd.affine_select(out=ident[:], in_=ones[:], pattern=[[-1, P]], compare_op=ALU.is_equal, fill=0.0,
                                    base=0, channel_multiplier=1).then_inc(const_made, 1)
            pool.wait_ge(const_made, 6)
            for n in range(NW + 2):
                w.split_low(pool, n, n % 2)

            def mask(s, raw, buf, done, j, i):
                a = col0[i]
                pool.wait_ge(raw[s], mask_count(j, i) + 1)
                nc.gpsimd.tensor_tensor(buf[:, s, a:a + P], buf[:, s, a:a + P], causal[:], ALU.mult).then_inc(done[s], 1)

            def body(j, par, jj, more):
                for i in range(NCELL):
                    if masked[i]:
                        for s in range(2):
                            mask(s, sp_raw, sp, sp_done, j, i)
                    low_part(pool, nc.gpsimd, j, 0, i)
                    for g in ends[i - 1] if i else ():
                        c, h = GROUPS[g]
                        if c != "turn" and h == 1 and c + 2 < more:
                            n, _, slot = chunk(*following(j, par, jj), c + 2)
                            w.split_low(pool, n, slot)
                    if masked[i]:
                        for s in range(2):
                            mask(s, wt_raw, wt, wt_done, j, i)

            pairs(pool, body)

        @block.scalar
        def _(act):
            nc.scalar.preload_act_table_set("natural_log_exp_and_others")
            for k in range(NC):
                act.wait_ge(x_loaded[k // 2], 16)
                squares.square(nc, act, k, room[:, k])
            norm.root(nc, act)
            for k in range(NC):
                act.wait_ge(h_made, k + 1)
                nc.scalar.activation(hhi[:, k], room[:, k], ACT.Copy).then_inc(hhi_made, 1)
                if k < 2:
                    w.split_high(act, k, k // 2, k % 2)
            act.wait_ge(const_made, 6)
            nc.scalar.activation(tri[:], tri_made[:], ACT.Copy).then_inc(ones_copied, 1)
            nc.scalar.activation(rest[:], rest_made[:], ACT.Copy).then_inc(ones_copied, 1)

            def evict(j, par, jj, g, more):
                c, h = GROUPS[g]
                hs = slice(h * H, h * H + H)
                act.wait_ge(group_done, NG * j + g + 1)
                if c == 0:
                    act.wait_ge(u_made, 2 * j + 1)
                    nc.scalar.activation(cgate[:, hs], gemm[:, h], ACT.Exp, scale=-1.0).then_inc(evicted[h], 1)
                    bank_evicted(act, j, g)
                    nc.scalar.activation(cgate[:, hs], cgate[:, hs], ACT.Ln, bias=1.0).then_inc(cgate_step, 1)
                    act.wait_ge(cgate_step, 2 * j + h + 1)
                    nc.scalar.activation(cgate[:, hs], cgate[:, hs], ACT.Exp, scale=-1.0).then_inc(cgate_made, 1)
                elif c in (2, 3):
                    nc.scalar.activation((q_hi, k_hi)[c - 2][:, par, hs], gemm[:, h], ACT.Copy, scale=QK_SCALE[c - 2]
                                         ).then_inc(qk_high, 1)
                elif c == 4:
                    nc.scalar.activation(vT[:, hs], gemm[:, h], ACT.Copy).then_inc(evicted[h], 1)
                elif c == "turn":
                    nc.scalar.activation(v[:, par, 4 * h:4 * h + 4, :],
                                         gemm[:, h].rearrange("p (t n) -> p t n", n=P), ACT.Copy).then_inc(evicted[h], 1)
                elif c in (5, 6):
                    act.wait_ge(logit_stored[c - 5], 16 * j + 1)
                    nc.scalar.activation(logit[:, c - 5, hs], gemm[:, h], ACT.Copy).then_inc(evicted[h], 1)
                    bank_evicted(act, j, g)
                    act.sem_inc(logit_made, 1)
                if c != "turn" and h == 1 and c + 2 < more:
                    n, half, slot = chunk(j, par, jj, c + 2)
                    w.split_high(act, n, half, slot)

            for g in range(NG):
                evict(0, 0, 0, g, NW + 2)

            def body(j, par, jj, more):
                for i in range(NCELL):
                    a, n = col0[i], NCELL * j + i
                    for s in range(2):
                        act.wait_ge(z_done[s], n + 1)
                        nc.scalar.activation(expz[:, s, a:H], zps[:, s, a:H], ACT.Abs).then_inc(act_step[s], 1)
                    for s in range(2):
                        act.wait_ge(act_step[s], n * 2 + 1)
                        act.wait_ge(ls_done[s], n + 1)
                        nc.scalar.activation(expz[:, s, a:H], expz[:, s, a:H], ACT.Exp, scale=-1.0).then_inc(act_step[s], 1)
                    for s in range(2):
                        act.wait_ge(act_step[s], n * 2 + 2)
                        nc.scalar.activation(ln[:, s, a:H], expz[:, s, a:H], ACT.Ln, bias=1.0).then_inc(ln_done[s], 1)
                    for s in range(2):
                        act.wait_ge(sp_done[s], n + 1)
                        act.wait_ge(sp_used[s], n + 1)
                        nc.scalar.activation(sp_hi[:, s, a:H], sp[:, s, a:H], ACT.Copy).then_inc(sp_hi_made[s], 1)
                    if more and i:
                        for g in ends[i - 1]:
                            evict(*following(j, par, jj), g, more)
                    for s in range(2):
                        act.wait_ge(lw_done[s], n + 1 + 1)
                        act.wait_ge(pv_done[s], n + 1)
                        ins = nc.scalar.activation(wt[:, s, a:H], lw[:, s, a:H], ACT.Exp)
                        ins.then_inc(wt_raw[s] if masked[i] else wt_done[s], 1)
                    if i and closes[i - 1]:
                        outputs(j, par, jj, cells[i - 1][0], NCELL * j + i)
                outputs(j, par, jj, 1, NCELL * j + NCELL)

            def outputs(j, par, jj, qh, n):
                act.wait_ge(o_stored[par], 16 * jj + 1)
                for s in range(2):
                    act.wait_ge(pv_done[s], n + 1)
                    rows = slice(64 * s, 64 * s + 64)
                    nc.scalar.activation(oT[rows, par, qh * H:qh * H + H], ops[rows, s, :], ACT.Copy
                                         ).then_inc(o_copied, 1)

            pairs(act, body)

        @block.vector
        def _(dve):
            def h_low(k):
                dve.wait_ge(hhi_made, k + 1)
                nc.vector.tensor_tensor(hlo[:, k], room[:, k], hhi[:, k].bitcast(F32), ALU.subtract).then_inc(hlo_made, 1)

            for k in range(NC):
                squares.add(nc, dve, k)
            dve.wait_ge(squares.done, 1)
            norm.start(nc, dve, [(slice(h * H, h * H + H), gemm[:, h]) for h in range(2)], lambda h: evicted[h])
            norm.finish(nc, dve)
            dve.wait_ge(c_loaded, 32)
            dve.wait_ge(norm.made, 1)
            for c in range(NC):
                nc.vector.scalar_tensor_tensor(out=room[:, c], in0=room[:, c], scalar=g_sb[:, c:c + 1], in1=norm.rstd[:],
                                               op0=ALU.mult, op1=ALU.mult).then_inc(h_made, 1)
                if c:
                    h_low(c - 1)
            h_low(NC - 1)

            def value(j, par, h):
                dve.wait_ge(group_done, NG * j + 2 + h + 1)
                dve.wait_ge(cgate_made, 2 * j + h + 1)
                nc.vector.tensor_tensor(u[:, par, PAD + h * H:PAD + h * H + H], gemm[:, h], cgate[:, h * H:h * H + H],
                                        ALU.mult).then_inc(evicted[h], 1)
                bank_evicted(dve, j, 2 + h)
                dve.sem_inc(u_made, 1)

            def qk_low(j, par, g):
                c, h = GROUPS[g]
                if c not in (2, 3):
                    return
                high, low = ((q_hi, q_lo), (k_hi, k_lo))[c - 2]
                hs = slice(h * H, h * H + H)
                dve.wait_ge(qk_high, 4 * j + (g - 3))
                nc.vector.scalar_tensor_tensor(out=low[:, par, hs], in0=gemm[:, h], scalar=QK_SCALE[c - 2],
                                               in1=high[:, par, hs].bitcast(F32), op0=ALU.mult, op1=ALU.subtract
                                               ).then_inc(evicted[h], 1)

            def conv(j, par, jj, t):
                if t == 0:
                    nc.vector.tensor_copy(cwj[:], cw[:, ds(j, 1), :].rearrange("p a t -> p (a t)")).then_inc(cwj_made, 1)
                    dve.wait_ge(cwj_made, j + 1)
                    dve.wait_ge(y_stored[par], 16 * jj + 1)
                    dve.wait_ge(u_made, 2 * j + 2 + 1)
                    nc.vector.tensor_scalar(ybuf[:, par], u[:, par, 0:T], cwj[:, 0:1], cwj[:, TAPS:TAPS + 1],
                                            ALU.mult, ALU.add).then_inc(conv_step, 1)
                else:
                    dve.wait_ge(conv_step, TAPS * j + t)
                    nc.vector.scalar_tensor_tensor(out=ybuf[:, par], in0=u[:, par, t:t + T], scalar=cwj[:, t:t + 1],
                                                   in1=ybuf[:, par], op0=ALU.mult, op1=ALU.add).then_inc(conv_step, 1)

            for h in range(2):
                value(0, 0, h)
            for g in range(NG):
                qk_low(0, 0, g)

            def body(j, par, jj, more):
                for i in range(NCELL):
                    a, n = col0[i], NCELL * j + i
                    for s in range(2):
                        dve.wait_ge(ln_done[s], n + 1)
                        dve.wait_ge(sp_lo_made[s], n + 1)
                        ins = nc.vector.scalar_tensor_tensor(out=sp[:, s, a:H], in0=zps[:, s, a:H], scalar=0.0,
                                                             in1=ln[:, s, a:H], op0=ALU.max, op1=ALU.add)
                        ins.then_inc(sp_raw[s] if masked[i] else sp_done[s], 1)
                    for s in range(2):
                        nc.vector.scalar_tensor_tensor(out=ls[:, s, a:H], in0=zps[:, s, a:H], scalar=0.0,
                                                       in1=ln[:, s, a:H], op0=ALU.min, op1=ALU.subtract
                                                       ).then_inc(ls_done[s], 1)
                        if s == 0:
                            low_part(dve, nc.vector, j, 1, i)
                    before = sum(map(sum, TAPS_AT[:i]))
                    for t in range(before, before + TAPS_AT[i][0]):
                        conv(j, par, jj, t)
                    if more and i:
                        for g in ends[i - 1]:
                            qk_low(j + 1, 1 - par, g)
                    for s in range(2):
                        dve.wait_ge(c_done[s], n + 1)
                        dve.wait_ge(wt_raw[s], mask_count(j, i)) if i and masked[i - 1] else dve.wait_ge(wt_done[s], n + 1)
                        dve.wait_ge(ls_done[s], n + 1 + 1)
                        nc.vector.tensor_tensor(lw[:, s, a:H], ls[:, s, a:H], cps[:, s, a:H], ALU.subtract
                                                ).then_inc(lw_done[s], 1)
                    if more and i in (2, 3):
                        value(j + 1, 1 - par, i - 2)
                    for t in range(before + TAPS_AT[i][0], before + sum(TAPS_AT[i])):
                        conv(j, par, jj, t)

            pairs(dve, body)

        @block.tensor
        def _(pe):
            pe.wait_ge(const_made, 6)
            squares.sum(nc, pe, ones[:])

            def project(j, par, jj, u, first=False):
                g, k0 = u // 2, u % 2 * (NC // 2)
                c, h = GROUPS[g]
                if k0 == 0:
                    pe.wait_ge(evicted[h], NB * j + g // 2 + 1)
                if c == "turn":
                    if k0 == 0:
                        bank_evicted(pe, j, 8 + h)
                        for x in range(4):
                            mm = nc.tensor.transpose(gemm[:, h, x * P:x * P + P], vT[:, (4 * h + x) * P:(4 * h + x + 1) * P],
                                                     ident[:])
                        mm.then_inc(group_done, 1)
                    return
                n, _, slot = chunk(j, par, jj, c)
                if k0 == 0 and h == 0:
                    w.ready(pe, n)
                hs = slice(h * H, h * H + H)
                for k in range(k0, k0 + NC // 2):
                    if first:
                        pe.wait_ge(hlo_made, k + 1)
                    mm = three_pass(nc, gemm[:, h], [(w.hi[:, slot, k], w.lo[:, slot, k], hhi[:, k, hs], hlo[:, k, hs])],
                                    first=(k == 0), last=(k == NC - 1))
                if k0:
                    mm.then_inc(group_done, 1)

            def z_cell(j, par, s, i):
                (qh, kb), a = cells[i], col0[i]
                if i == 0:
                    bank_evicted(pe, j, 6)
                    bank_evicted(pe, j, 7)
                pe.wait_ge(ls_done[s], NCELL * j + i + 1)
                rows = slice(64 * s, 64 * s + 64)
                keys, queries = slice(kb * P, kb * P + P), slice(qh * H + a, qh * H + H)
                three_pass(nc, zps[:, s, a:H], [(k_hi[rows, par, keys], k_lo[rows, par, keys],
                                                 q_hi[rows, par, queries], q_lo[rows, par, queries])]).then_inc(z_done[s], 1)

            def add_own(j, s, i):
                a = col0[i]
                pe.wait_ge(sp_hi_made[s], NCELL * j + i + 1)
                pe.wait_ge(sp_lo_made[s], NCELL * j + i + 2)
                if opens[i]:
                    pe.wait_ge(lw_done[s], NCELL * j + i + 1)
                nc.tensor.matmul(cps[:, s, a:H], tri[:], sp_hi[:, s, a:H], start=opens[i], stop=False, skip_group_check=True)
                nc.tensor.matmul(cps[:, s, a:H], tri[:], sp_lo[:, s, a:H], start=False, stop=True, skip_group_check=True
                                 ).then_inc(c_done[s], 1)
                if closes[i]:
                    pe.wait_ge(c_done[s], NCELL * j + i + 1)
                    pe.sem_inc(sp_used[s], 1)

            def add_rest(j, s, i):
                a = col0[i]
                if not closes[i]:
                    pe.wait_ge(lw_done[s], NCELL * j + i + 1 + 1)
                    nc.tensor.matmul(cps[:, s, a:H], rest[:], sp_hi[:, s, a:H], start=False, stop=False, skip_group_check=True)
                    nc.tensor.matmul(cps[:, s, a:H], rest[:], sp_lo[:, s, a:H], start=False, stop=True, skip_group_check=True
                                     ).then_inc(sp_used[s], 1)

            def weigh(j, par, s, i):
                (qh, kb), a = cells[i], col0[i]
                if i == 0:
                    bank_evicted(pe, j, 12)
                    bank_evicted(pe, j, 13)
                if opens[i]:
                    pe.wait_ge(o_copied, 4 * j + 2 * qh + 1)
                pe.wait_ge(wt_done[s], NCELL * j + i + 1 + 1)
                nc.tensor.matmul(ops[64 * s:64 * s + 64, s, a:H], v[:, par, kb, 64 * s:64 * s + 64], wt[:, s, a:H],
                                 start=opens[i], stop=closes[i], skip_group_check=True).then_inc(pv_done[s], 1)

            for u in range(2 * NG):
                project(0, 0, 0, u, first=(u < 2))
            pe.wait_ge(ones_copied, 2)
            for s in range(2):
                z_cell(0, 0, s, 0)

            def body(j, par, jj, more):
                for i in range(NCELL):
                    for s in range(2):
                        add_own(j, s, i)
                    for s in range(2):
                        if i < NCELL - 1:
                            z_cell(j, par, s, i + 1)
                        elif more:
                            z_cell(j + 1, 1 - par, s, 0)
                    if more:
                        for u in halves(2 * i):
                            project(*following(j, par, jj), u)
                    for s in range(2):
                        add_rest(j, s, i)
                    if more:
                        for u in halves(2 * i + 1):
                            project(*following(j, par, jj), u)
                    for s in range(2):
                        weigh(j, par, s, i)

            pairs(pe, body)


def merge_phase(nc, xT, y_in, attn_in, gate_in, wstream, ln_g, ln_b, gate_b, half_out, x_out):
    with Phase(nc, "merge") as m:
        xy = m.sb("xy", [P, NC, T])
        ahi, alo = m.sb("ahi", [P, NC, T], F32R), m.sb("alo", [P, NC, T], F32R)
        zhi, zlo = m.sb("zhi", [P, NC, T], F32R), m.sb("zlo", [P, NC, T], F32R)
        w = WeightStream(nc, m)
        gate = m.sb("gate", [P, 2, T])
        part = m.sb("part", [P, 2, T])
        mean = m.sb("mean", [P, T])
        norm = Rsqrt(m, "norm", T, (mean[:], part[:, 0], part[:, 1]))
        sq = m.sb("sq", [P, H])
        ones = m.sb("ones", [P, P])
        lng, lnb = m.sb("lng", [P, NC]), m.sb("lnb", [P, NC])
        gb = m.sb("gb", [P, 2 * NC])
        gbn = m.sb("gbn", [P, 2])
        banks = m.ps("banks", [P, 4, H])
        sums = m.ps("sums", [P, 4, H])

        y_loaded, c_loaded = m.sem("y_loaded"), m.sem("c_loaded")
        a_loaded = [m.sem(f"a_loaded{b}") for b in range(2)]
        ahi_made, alo_made = m.sem("ahi_made"), m.sem("alo_made")
        ones_made = m.sem("ones_made")
        y_summed, mean_sum, mean_made, centred = m.sem("y_summed"), m.sem("mean_sum"), m.sem("mean_made"), m.sem("centred")
        sq_made, sq_added, var_sum = m.sem("sq_made"), m.sem("sq_added"), m.sem("var_sum")
        sums_read = [m.sem(f"sums_read{h}") for h in range(2)]
        scaled, z_made, zhi_made, zlo_made = m.sem("scaled"), m.sem("z_made"), m.sem("zhi_made"), m.sem("zlo_made")
        group_done = m.sem("group_done")
        bank_read = m.sem("bank_read", start=4)
        g_loaded = [m.sem(f"g_loaded{s}") for s in range(2)]
        gbn_made, opened = m.sem("gbn_made"), m.sem("opened")
        product = m.sem("product")
        half_stored = [m.sem(f"half_stored{s}") for s in range(2)]
        part_loaded = [m.sem(f"part_loaded{s}") for s in range(2)]
        merged, mhi_made, mlo_made = m.sem("merged"), m.sem("mhi_made"), m.sem("mlo_made")
        x_loaded, x_stored = m.sem("x_loaded"), m.sem("x_stored")
        block = m.block()

        def pairs(eng, body, i0, i1):
            with eng.Fori(i0, i1) as i:
                for s in range(2):
                    body(i * 2 + s, i, s)

        flat = lambda ap: ap.rearrange("p a t -> p (a t)")

        @block.sync
        def _(sync):
            sync.dma_start(part[:, 0], attn_in[:, 0]).then_inc(a_loaded[0], 16)
            w.load(sync, wstream, 0, 0, first=True)
            sync.dma_start(part[:, 1], attn_in[:, 1]).then_inc(a_loaded[1], 16)
            w.load(sync, wstream, 1, 1, first=True)
            for k in range(2, NC):
                sync.wait_ge(alo_made, k - 1)
                sync.dma_start(part[:, k % 2], attn_in[:, k]).then_inc(a_loaded[k % 2], 16)
                if k == 3:
                    for s in range(2):
                        sync.dma_start(gate[:, s], gate_in[:, s]).then_inc(g_loaded[s], 16)
            sync.dma_start(xy[:], y_in).then_inc(y_loaded, 16)
            for dst, src in ((gb, gate_b), (lng, ln_g), (lnb, ln_b)):
                sync.dma_start(dst[:], src).then_inc(c_loaded, 16)

            def attention(n, i, s):
                w.load(sync, wstream, n + 2, s)
                sync.wait_ge(product, n * 2 + 2)
                sync.dma_start(flat(half_out[:, ds(n, 1)]), gate[:, s]).then_inc(half_stored[s], 16)
                sync.wait_ge(half_stored[s], i * 16 + 16)
                sync.dma_start(gate[:, s], flat(gate_in[:, ds(n + 2, 1)])).then_inc(g_loaded[s], 16)

            pairs(sync, attention, 0, NC // 2)
            sync.wait_ge(zlo_made, NC)
            for s in range(2):
                sync.dma_start(part[:, s], half_out[:, s]).then_inc(part_loaded[s], 16)
            sync.dma_start(xy[:], xT).then_inc(x_loaded, 16)

            def convolution(n, i, s, more):
                w.load(sync, wstream, n + 2, s)
                sync.wait_ge(mlo_made, n - (NC - 1))
                if more:
                    sync.dma_start(gate[:, s], flat(gate_in[:, ds(n + 2, 1)])).then_inc(g_loaded[s], 16)
                    sync.dma_start(part[:, s], flat(half_out[:, ds(n + (2 - NC), 1)])).then_inc(part_loaded[s], 16)

            pairs(sync, lambda n, i, s: convolution(n, i, s, True), NC // 2, NC - 1)
            for s in range(2):
                convolution(2 * NC - 2 + s, NC - 1, s, False)

            def output(n, i, s, more):
                if more:
                    w.load(sync, wstream, n + 2, s)
                sync.wait_ge(bank_read, n * 2 + 6)
                sync.dma_start(flat(x_out[:, ds(n - 2 * NC, 1)]), flat(xy[:, ds(n - 2 * NC, 1)])).then_inc(x_stored, 16)

            pairs(sync, lambda n, i, s: output(n, i, s, True), NC, 3 * NC // 2 - 1)
            for s in range(2):
                output(3 * NC - 2 + s, 0, s, False)
            sync.wait_ge(x_stored, 16 * NC)

        @block.gpsimd
        def _(pool):
            nc.gpsimd.memset(ones[:], 1.0).then_inc(ones_made, 1)
            pairs(pool, lambda n, i, s: w.split_low(pool, n, s), 0, 3 * NC // 2)

        @block.tensor
        def _(pe):
            def chunk(n, s, xhi, xlo, made=None):
                w.ready(pe, n)
                for h in range(2):
                    pe.wait_ge(bank_read, n * 2 + (h + 1))
                    hs = slice(h * H, h * H + H)
                    for k in range(NC):
                        if made and h == 0:
                            pe.wait_ge(made, k + 1)
                        mm = three_pass(nc, banks[:, 2 * s + h], [(w.hi[:, s, k], w.lo[:, s, k], xhi[:, k, hs], xlo[:, k, hs])],
                                        first=(k == 0), last=(k == NC - 1))
                    mm.then_inc(group_done, 1)

            def total(src, first_bank, done):
                for h in range(2):
                    mm = nc.tensor.matmul(sums[:, first_bank + h], ones[:], src[:, h * H:h * H + H], start=True, stop=True)
                mm.then_inc(done, 1)

            pe.wait_ge(ones_made, 1)
            for n in range(NC):
                chunk(n, n % 2, ahi, alo, alo_made if n == 0 else None)
                if n == 1:
                    pe.wait_ge(y_summed, 1)
                    total(mean, 0, mean_sum)
                if n == 4:
                    pe.wait_ge(sq_added, 2 * NC)
                    total(norm.inv, 2, var_sum)
            for s in range(2):
                chunk(NC + s, s, zhi, zlo, zlo_made if s == 0 else None)
            pairs(pe, lambda n, i, s: chunk(n, s, zhi, zlo), NC // 2 + 1, NC)
            for s in range(2):
                chunk(2 * NC + s, s, ahi, alo, mlo_made if s == 0 else None)
            pairs(pe, lambda n, i, s: chunk(n, s, ahi, alo), NC + 1, 3 * NC // 2)

        @block.scalar
        def _(act):
            for s in range(2):
                w.split_high(act, s, 0, s)
            for k in range(NC):
                act.wait_ge(a_loaded[k % 2], 16 * (k // 2 + 1))
                nc.scalar.activation(ahi[:, k], part[:, k % 2], ACT.Copy).then_inc(ahi_made, 1)
            act.wait_ge(c_loaded, 48)

            def open_gate(n, i, s):
                act.wait_ge(g_loaded[s], i * 16 + 16)
                if not isinstance(n, int) or n > 1:
                    act.wait_ge(product, n * 2 - 2)
                nc.scalar.activation(gbn[:, s:s + 1], gb[:, ds(n, 1)], ACT.Copy).then_inc(gbn_made, 1)
                act.wait_ge(gbn_made, n + 1)
                nc.scalar.activation(gate[:, s], gate[:, s], ACT.Sigmoid, bias=gbn[:, s:s + 1]).then_inc(opened, 1)

            def next_weights(n, i, s):
                act.wait_ge(group_done, n * 2 + 2)
                w.split_high(act, n + 2, i + 1, s)

            def squares(g0, g1):
                for g in range(g0, g1):
                    k, h = g // 2, g % 2
                    act.wait_ge(centred, k + 1)
                    if g:
                        act.wait_ge(sq_added, g)
                    nc.scalar.activation(sq[:], xy[:, k, h * H:h * H + H], ACT.Square).then_inc(sq_made, 1)

            def silu(k0, k1):
                for k in range(k0, k1):
                    act.wait_ge(scaled, k + 1)
                    nc.scalar.activation(xy[:, k], xy[:, k], ACT.Silu, bias=lnb[:, k:k + 1]).then_inc(z_made, 1)
                for k in range(k0, k1):
                    act.wait_ge(z_made, k + 1)
                    nc.scalar.activation(zhi[:, k], xy[:, k], ACT.Copy).then_inc(zhi_made, 1)

            for n in range(NC):
                open_gate(n, n // 2, n % 2)
                if n in (2, 3, 4):
                    squares(*((0, 6), (6, 12), (12, 16))[n - 2])
                if n == 5:
                    norm.root(nc, act)
                if n in (6, 7):
                    silu(4 * (n - 6), 4 * (n - 5))
                next_weights(n, n // 2, n % 2)

            def convolution(n, i, s):
                open_gate(n, i, s)
                next_weights(n, i, s)
                act.wait_ge(merged, n - (NC - 1))
                nc.scalar.activation(flat(ahi[:, ds(n - NC, 1)]), part[:, s], ACT.Copy).then_inc(mhi_made, 1)

            pairs(act, convolution, NC // 2, NC)
            pairs(act, next_weights, NC, 3 * NC // 2 - 1)

        @block.vector
        def _(dve):
            for k in range(NC):
                dve.wait_ge(ahi_made, k + 1)
                nc.vector.tensor_tensor(alo[:, k], part[:, k % 2], ahi[:, k].bitcast(F32), ALU.subtract).then_inc(alo_made, 1)
            dve.wait_ge(y_loaded, 16)
            nc.vector.tensor_reduce(mean[:], xy[:].rearrange("p c t -> p t c"), AX.X, ALU.add).then_inc(y_summed, 1)

            def gated(n, s):
                for h in range(2):
                    dve.wait_ge(group_done, n * 2 + (h + 1))
                    dve.wait_ge(opened, n + 1)
                    nc.vector.tensor_tensor(gate[:, s, h * H:h * H + H], gate[:, s, h * H:h * H + H], banks[:, 2 * s + h], ALU.mult
                                            ).then_inc(product, 1)
                dve.wait_ge(product, n * 2 + 2)
                dve.sem_inc(bank_read, 2)

            def centre():
                dve.wait_ge(mean_sum, 1)
                for h in range(2):
                    nc.vector.tensor_scalar(mean[:, h * H:h * H + H], sums[:, h], 1.0 / D, None, ALU.mult).then_inc(mean_made, 1)
                dve.wait_ge(mean_made, 2)
                for k in range(NC):
                    nc.vector.tensor_tensor(xy[:, k], xy[:, k], mean[:], ALU.subtract).then_inc(centred, 1)

            def add_squares(g0, g1):
                for g in range(g0, g1):
                    hs = slice((g % 2) * H, (g % 2) * H + H)
                    dve.wait_ge(sq_made, g + 1)
                    if g < 2:
                        nc.vector.tensor_copy(norm.inv[:, hs], sq[:]).then_inc(sq_added, 1)
                    else:
                        dve.wait_ge(sq_added, g - 1)
                        nc.vector.tensor_tensor(norm.inv[:, hs], norm.inv[:, hs], sq[:], ALU.add).then_inc(sq_added, 1)

            def scale(k0, k1):
                for k in range(k0, k1):
                    nc.vector.scalar_tensor_tensor(out=xy[:, k], in0=xy[:, k], scalar=lng[:, k:k + 1], in1=norm.rstd,
                                                   op0=ALU.mult, op1=ALU.mult).then_inc(scaled, 1)

            def low(k0, k1):
                for k in range(k0, k1):
                    dve.wait_ge(zhi_made, k + 1)
                    nc.vector.tensor_tensor(zlo[:, k], xy[:, k], zhi[:, k].bitcast(F32), ALU.subtract).then_inc(zlo_made, 1)

            for n in range(NC):
                gated(n, n % 2)
                if n == 1:
                    centre()
                if n in (2, 3, 4):
                    add_squares(*((0, 6), (6, 12), (12, 16))[n - 2])
                if n == 4:
                    dve.wait_ge(var_sum, 1)
                    dve.wait_ge(centred, NC)
                    norm.start(nc, dve, [(slice(h * H, h * H + H), sums[:, 2 + h]) for h in range(2)], lambda h: sums_read[h])
                if n == 5:
                    norm.finish(nc, dve)
                    dve.wait_ge(norm.made, 1)
                    dve.wait_ge(c_loaded, 48)
                    scale(0, NC)
                if n in (6, 7):
                    low(4 * (n - 6), 4 * (n - 5))

            def convolution(n, i, s):
                gated(n, s)
                dve.wait_ge(part_loaded[s], i * 16 + (16 - 16 * (NC // 2)))
                nc.vector.tensor_tensor(part[:, s], part[:, s], gate[:, s], ALU.add).then_inc(merged, 1)
                dve.wait_ge(mhi_made, n - (NC - 1))
                nc.vector.tensor_tensor(flat(alo[:, ds(n - NC, 1)]), part[:, s], flat(ahi[:, ds(n - NC, 1)]).bitcast(F32),
                                        ALU.subtract).then_inc(mlo_made, 1)

            pairs(dve, convolution, NC // 2, NC)
            dve.wait_ge(x_loaded, 16)

            def output(n, i, s):
                for h in range(2):
                    x = flat(xy[:, ds(n - 2 * NC, 1), h * H:h * H + H])
                    dve.wait_ge(group_done, n * 2 + (h + 1))
                    nc.vector.tensor_tensor(x, x, banks[:, 2 * s + h], ALU.add).then_inc(bank_read, 1)

            pairs(dve, output, NC, 3 * NC // 2)


def cross_attention_phase(nc, x_in, gain, memT, mem_gain, wstream, x_out):
    with Phase(nc, "xattn") as m:
        HC = NC // XH
        MT = M // P
        S = NT // 2
        STEPS = XH * S
        xq = m.sb("xq", [P, NC, T])
        hhi, hlo = m.sb("hhi", [P, NC, T], F32R), m.sb("hlo", [P, NC, T], F32R)
        mem = m.sb("mem", [P, NC, M])
        mhi, mlo = m.sb("mhi", [P, NC, M], F32R), m.sb("mlo", [P, NC, M], F32R)
        w = WeightStream(nc, m)
        msq = m.sb("msq", [P, NC, M])
        sq = msq[:].rearrange("p c t -> p (c t)").rearrange("p (b t) -> p b t", b=2)
        norm = Rsqrt(m, "norm", T)
        mnorm = Rsqrt(m, "mnorm", M)
        total_sq = norm.inv
        g_sb, mg_sb = m.sb("gain", [P, NC]), m.sb("mgain", [P, NC])
        ones = m.sb("ones", [P, P])
        ident = m.sb("ident", [P, P])
        kT = m.sb("kT", [P, NC, M])
        vT = m.sb("vT", [P, 2, M])
        v = m.sb("v", [P, MT, D])
        top = m.sb("top", [P, 2, NT])
        total = m.sb("total", [P, 2, NT])
        inv = m.sb("inv", [P, 2, NT])
        prob = m.sb("prob", [P, 2, 2, M])
        pT = m.sb("pT", [P, MT, T])

        gemm = m.ps("gemm", [P, 2, H])
        score = m.ps("score", [P, 2, 2, M])
        turned = m.ps("turned", [P, 2, MT, 2 * P])
        out = m.ps("out", [P, 2, H])

        x_loaded = [m.sem(f"x_loaded{i}") for i in range(2)]
        m_loaded, c_loaded, made = m.sem("m_loaded"), m.sem("c_loaded"), m.sem("made")
        msq_made, msum_done, msum_read = m.sem("msq_made"), m.sem("msum_done"), m.sem("msum_read")
        mh_made, mhi_made, mlo_made = m.sem("mh_made"), m.sem("mhi_made"), m.sem("mlo_made")
        sq_made, sq_added, sum_done = m.sem("sq_made"), m.sem("sq_added"), m.sem("sum_done")
        sum_read = [m.sem(f"sum_read{h}") for h in range(2)]
        h_made, hhi_made, hlo_made = m.sem("h_made"), m.sem("hhi_made"), m.sem("hlo_made")
        group_done = m.sem("group_done")
        bank_read = m.sem("bank_read", start=2)
        v_turned, v_made = m.sem("v_turned"), m.sem("v_made")
        score_done, top_made, exp_made = m.sem("score_done"), m.sem("top_made"), m.sem("exp_made")
        inv_made, prob_made = m.sem("inv_made"), m.sem("prob_made")
        turned_done, pT_made = m.sem("turned_done"), m.sem("pT_made")
        out_done, ohi_made, olo_made = m.sem("out_done"), m.sem("ohi_made"), m.sem("olo_made")
        x_back, x_stored = m.sem("x_back"), m.sem("x_stored")
        block = m.block()

        KV = 2 * NC

        def group(n, h=0):
            return n if n < KV else KV + 2 * (n - KV) + h

        @block.sync
        def _(sync):
            sync.dma_start(mem[:], memT).then_inc(m_loaded, 16)
            for s in range(2):
                w.load(sync, wstream, s, s, first=True)
            sync.dma_start(g_sb[:], gain).then_inc(c_loaded, 16)
            sync.dma_start(mg_sb[:], mem_gain).then_inc(c_loaded, 16)
            for i in range(2):
                sync.dma_start(xq[:, 4 * i:4 * i + 4], x_in[:, 4 * i:4 * i + 4]).then_inc(x_loaded[i], 16)

            def weights(i0, i1):
                with sync.Fori(i0, i1) as i:
                    for s in range(2):
                        w.load(sync, wstream, i * 2 + s, s)

            weights(1, 3 * NC // 2 + 2)
            sync.wait_ge(score_done, STEPS)
            sync.dma_start(xq[:], x_in).then_inc(x_back, 16)
            weights(3 * NC // 2 + 2, 2 * NC)
            for k in range(NC):
                sync.wait_ge(bank_read, group(3 * NC + k, 1) + 3)
                sync.dma_start(x_out[:, k], xq[:, k]).then_inc(x_stored, 16)
            sync.wait_ge(x_stored, 16 * NC)

        @block.gpsimd
        def _(pool):
            nc.gpsimd.memset(ones[:], 1.0).then_inc(made, 1)
            pool.wait_ge(made, 1)
            nc.gpsimd.affine_select(out=ident[:], in_=ones[:], pattern=[[-1, P]], compare_op=ALU.is_equal, fill=0.0,
                                    base=0, channel_multiplier=1).then_inc(made, 1)
            with pool.Fori(0, 2 * NC) as i:
                for s in range(2):
                    w.split_low(pool, i * 2 + s, s)

        @block.tensor
        def _(pe):
            pe.wait_ge(made, 2)
            pe.wait_ge(msq_made, 1)
            for k in range(NC):
                mm = nc.tensor.matmul(out[:, 0, 0:M], ones[:], msq[:, k], start=(k == 0), stop=(k == NC - 1))
            mm.then_inc(msum_done, 1)

            def turn_v(i):
                pe.wait_ge(bank_read, group(NC + i) + 3)
                if i >= 2:
                    pe.wait_ge(v_made, i - 1)
                for t in range(MT):
                    mm = nc.tensor.transpose(turned[:, i % 2, t, 0:P], vT[:, i % 2, t * P:t * P + P], ident[:])
                mm.then_inc(v_turned, 1)

            for n in range(KV):
                w.ready(pe, n)
                pe.wait_ge(bank_read, n + 1)
                for k in range(NC):
                    if n == 0:
                        pe.wait_ge(mlo_made, k + 1)
                    mm = three_pass(nc, gemm[:, n % 2, 0:M], [(w.hi[:, n % 2, k], w.lo[:, n % 2, k], mhi[:, k], mlo[:, k])],
                                    first=(k == 0), last=(k == NC - 1))
                mm.then_inc(group_done, 1)
                if n == 4:
                    pe.wait_ge(sq_added, NC)
                    for h in range(2):
                        mm = nc.tensor.matmul(out[:, h], ones[:], total_sq[:, h * H:h * H + H], start=True, stop=True)
                    mm.then_inc(sum_done, 1)
                if n > NC:
                    turn_v(n - NC - 1)
            turn_v(NC - 1)

            def project(n, slot, made=None):
                w.ready(pe, n)
                for h in range(2):
                    pe.wait_ge(bank_read, n * 2 + (h + 1 - KV))
                    hs = slice(h * H, h * H + H)
                    for k in range(NC):
                        if made and h == 0:
                            pe.wait_ge(made[0], made[1](k))
                        mm = three_pass(nc, gemm[:, h], [(w.hi[:, slot, k], w.lo[:, slot, k], hhi[:, k, hs], hlo[:, k, hs])],
                                        first=(k == 0), last=(k == NC - 1))
                    mm.then_inc(group_done, 1)

            for s in range(2):
                project(KV + s, s, (hlo_made, lambda k: k + 1) if s == 0 else None)
            with pe.Fori(NC + 1, 3 * NC // 2) as i:
                for s in range(2):
                    project(i * 2 + s, s)
            pe.wait_ge(bank_read, group(3 * NC) + 2)
            pe.wait_ge(v_made, NC)

            def turn(u):
                pe.wait_ge(prob_made, 2 * u + 2)
                if u >= 2:
                    pe.wait_ge(pT_made, u - 1)
                for x in range(2):
                    for t in range(MT):
                        mm = nc.tensor.transpose(turned[:, u % 2, t, x * P:x * P + P], prob[:, u % 2, x, t * P:t * P + P],
                                                 ident[:])
                mm.then_inc(turned_done, 1)

            def weigh(hd):
                pe.wait_ge(pT_made, S * hd + S)
                for g in range(2 * HC):
                    c, h = g // 2, g % 2
                    if hd or g >= 2:
                        pe.wait_ge(olo_made, 2 * HC * hd + g - 1)
                    for t in range(MT):
                        col = (hd * HC + c) * P
                        mm = nc.tensor.matmul(out[:, h], v[:, t, col:col + P], pT[:, t, h * H:h * H + H],
                                              start=(t == 0), stop=(t == MT - 1))
                    mm.then_inc(out_done, 1)

            for u in range(STEPS + 2):
                if u < STEPS:
                    hd, s = u // S, u % S
                    if u >= 2:
                        pe.wait_ge(exp_made, 2 * u - 2)
                    for x in range(2):
                        t = 2 * s + x
                        for c in range(HC):
                            mm = nc.tensor.matmul(score[:, s % 2, x], xq[:, hd * HC + c, t * P:t * P + P], kT[:, hd * HC + c],
                                                  start=(c == 0), stop=(c == HC - 1))
                    mm.then_inc(score_done, 1)
                if u >= S + 2 and u % S == 2:
                    weigh((u - 2) // S - 1)
                if u >= 2:
                    turn(u - 2)
            weigh(XH - 1)
            for s in range(2):
                project(3 * NC + s, s, (olo_made, lambda k: 2 * k + 2) if s == 0 else None)
            with pe.Fori(3 * NC // 2 + 1, 2 * NC) as i:
                for s in range(2):
                    project(i * 2 + s, s)

        @block.scalar
        def _(act):
            nc.scalar.preload_act_table_set("natural_log_exp_and_others")
            act.wait_ge(m_loaded, 16)
            nc.scalar.activation(msq[:], mem[:], ACT.Square).then_inc(msq_made, 1)
            for s in range(2):
                w.split_high(act, s, 0, s)
            mnorm.root(nc, act)
            for k in range(NC):
                act.wait_ge(mh_made, k + 1)
                nc.scalar.activation(mhi[:, k], mem[:, k], ACT.Copy).then_inc(mhi_made, 1)

            def square(k):
                act.wait_ge(x_loaded[k // 4], 16)
                if k == 0:
                    nc.scalar.activation(total_sq[:], xq[:, k], ACT.Square).then_inc(sq_made, 1)
                    return
                if k >= 3:
                    act.wait_ge(sq_added, k - 1)
                nc.scalar.activation(sq[:, k % 2], xq[:, k], ACT.Square).then_inc(sq_made, 1)

            for n in range(KV):
                act.wait_ge(group_done, n + 1)
                if n < NC:
                    nc.scalar.activation(kT[:, n], gemm[:, n % 2, 0:M], ACT.Copy).then_inc(bank_read, 1)
                else:
                    if n >= NC + 2:
                        act.wait_ge(v_turned, n - NC - 1)
                    nc.scalar.activation(vT[:, n % 2], gemm[:, n % 2, 0:M], ACT.Copy).then_inc(bank_read, 1)
                w.split_high(act, n + 2, n // 2 + 1, n % 2)
                if n < 4:
                    square(2 * n)
                    square(2 * n + 1)
                if n == 5:
                    norm.root(nc, act)
                if n >= NC:
                    act.wait_ge(h_made, n - NC + 1)
                    nc.scalar.activation(hhi[:, n - NC], xq[:, n - NC], ACT.Copy).then_inc(hhi_made, 1)

            act.wait_ge(hlo_made, NC)
            with act.Fori(NC, 3 * NC // 2) as i:
                for s in range(2):
                    n = i * 2 + s
                    for h in range(2):
                        act.wait_ge(group_done, n * 2 + (h + 1 - KV))
                        nc.scalar.activation(xq[:, ds(n - KV, 1), h * H:h * H + H].rearrange("p a t -> p (a t)"), gemm[:, h],
                                             ACT.Copy, scale=1.0 / 16).then_inc(bank_read, 1)
                    w.split_high(act, n + 2, i + 1, s)

            def copy_turned(u):
                act.wait_ge(turned_done, u + 1)
                if u >= S and u % S == 0:
                    act.wait_ge(out_done, 2 * HC * (u // S))
                s = u % S
                nc.scalar.activation(pT[:, :, 2 * s * P:2 * s * P + 2 * P], turned[:, u % 2], ACT.Copy).then_inc(pT_made, 1)

            def outputs_high(hd):
                for g in range(2 * HC):
                    act.wait_ge(out_done, 2 * HC * hd + g + 1)
                    nc.scalar.activation(hhi[:, hd * HC + g // 2, g % 2 * H:g % 2 * H + H], out[:, g % 2], ACT.Copy
                                         ).then_inc(ohi_made, 1)

            for u in range(STEPS + 2):
                if u >= S + 2 and u % S == 2 and u < STEPS:
                    outputs_high((u - 2) // S - 1)
                if u < STEPS:
                    hd, s = u // S, u % S
                    act.wait_ge(top_made, u + 1)
                    if u >= 2:
                        act.wait_ge(turned_done, u - 1)
                    for x in range(2):
                        t = 2 * s + x
                        nc.scalar.activation(prob[:, s % 2, x], score[:, s % 2, x], ACT.Exp, bias=top[:, hd % 2, t:t + 1],
                                             accum_out=total[:, hd % 2, t:t + 1]).then_inc(exp_made, 1)
                if u >= 2:
                    copy_turned(u - 2)
            outputs_high(XH - 1)
            with act.Fori(3 * NC // 2, 2 * NC - 1) as i:
                for s in range(2):
                    act.wait_ge(group_done, (i * 2 + s) * 2 + (2 - KV))
                    w.split_high(act, i * 2 + (s + 2), i + 1, s)

        @block.vector
        def _(dve):
            dve.wait_ge(msum_done, 1)
            mnorm.start(nc, dve, [(slice(0, M), out[:, 0, 0:M])], lambda h: msum_read)
            mnorm.finish(nc, dve)
            dve.wait_ge(mnorm.made, 1)
            dve.wait_ge(c_loaded, 32)
            for k in range(NC):
                nc.vector.scalar_tensor_tensor(out=mem[:, k], in0=mem[:, k], scalar=mg_sb[:, k:k + 1], in1=mnorm.rstd[:],
                                               op0=ALU.mult, op1=ALU.mult).then_inc(mh_made, 1)
            for k in range(NC):
                dve.wait_ge(mhi_made, k + 1)
                nc.vector.tensor_tensor(mlo[:, k], mem[:, k], mhi[:, k].bitcast(F32), ALU.subtract).then_inc(mlo_made, 1)
            dve.wait_ge(sq_made, 1)
            dve.sem_inc(sq_added, 1)
            for k in range(1, NC):
                dve.wait_ge(sq_made, k + 1)
                dve.wait_ge(sq_added, k)
                nc.vector.tensor_tensor(total_sq[:], total_sq[:], sq[:, k % 2], ALU.add).then_inc(sq_added, 1)
            dve.wait_ge(sum_done, 1)
            norm.start(nc, dve, [(slice(h * H, h * H + H), out[:, h]) for h in range(2)], lambda h: sum_read[h])
            norm.finish(nc, dve)
            dve.wait_ge(norm.made, 1)

            def values(k):
                dve.wait_ge(v_turned, k + 1)
                nc.vector.tensor_copy(v[:, :, k * P:k * P + P], turned[:, k % 2, :, 0:P]).then_inc(v_made, 1)

            for k in range(NC):
                nc.vector.scalar_tensor_tensor(out=xq[:, k], in0=xq[:, k], scalar=g_sb[:, k:k + 1], in1=norm.rstd[:],
                                               op0=ALU.mult, op1=ALU.mult).then_inc(h_made, 1)
            for k in range(NC):
                if k < NC - 1:
                    values(k)
                dve.wait_ge(hhi_made, k + 1)
                nc.vector.tensor_tensor(hlo[:, k], xq[:, k], hhi[:, k].bitcast(F32), ALU.subtract).then_inc(hlo_made, 1)
            values(NC - 1)

            def normalise(u):
                hd, s = u // S, u % S
                cols = slice(2 * s, 2 * s + 2)
                dve.wait_ge(exp_made, 2 * u + 2)
                nc.vector.reciprocal(inv[:, hd % 2, cols], total[:, hd % 2, cols]).then_inc(inv_made, 1)
                dve.wait_ge(inv_made, u + 1)
                for x in range(2):
                    t = 2 * s + x
                    nc.vector.tensor_scalar(prob[:, s % 2, x], prob[:, s % 2, x], inv[:, hd % 2, t:t + 1], None, ALU.mult
                                            ).then_inc(prob_made, 1)

            def outputs_low(hd):
                for g in range(2 * HC):
                    dve.wait_ge(ohi_made, 2 * HC * hd + g + 1)
                    k, hs = hd * HC + g // 2, slice(g % 2 * H, g % 2 * H + H)
                    nc.vector.tensor_tensor(hlo[:, k, hs], out[:, g % 2], hhi[:, k, hs].bitcast(F32), ALU.subtract
                                            ).then_inc(olo_made, 1)

            for u in range(STEPS + 1):
                if u < STEPS:
                    hd, s = u // S, u % S
                    dve.wait_ge(score_done, u + 1)
                    nc.vector.tensor_reduce(top[:, hd % 2, 2 * s:2 * s + 2], score[:, s % 2], AX.X, ALU.max, negate=True
                                            ).then_inc(top_made, 1)
                if u:
                    normalise(u - 1)
                if u >= S + 2 and u % S == 2:
                    outputs_low((u - 2) // S - 1)
            outputs_low(XH - 1)
            dve.wait_ge(x_back, 16)
            with dve.Fori(3 * NC // 2, 2 * NC) as i:
                for s in range(2):
                    n = i * 2 + s
                    for h in range(2):
                        x = xq[:, ds(n - 3 * NC, 1), h * H:h * H + H].rearrange("p a t -> p (a t)")
                        dve.wait_ge(group_done, n * 2 + (h + 1 - KV))
                        nc.vector.tensor_tensor(x, x, gemm[:, h], ALU.add).then_inc(bank_read, 1)


class Experts1:

    def __init__(self, nc, tensors):
        sb = lambda name, shape, dt=F32: tensors.enter_context(nc.sbuf_tensor(name, shape, dt))
        self.nc = nc
        self.hhi, self.hlo = sb("hhi", [P, NC, T], F32R), sb("hlo", [P, NC, T], F32R)
        self.raw = sb("uraw", [P, 2, NC, P])
        self.hi, self.lo = sb("uhi", [P, 2, NC, P], F32R), sb("ulo", [P, 2, NC, P], F32R)
        self.out = sb("ugelu", [P, 2, T])

    def begin(self, m, u_stream, a_out):
        self.u_stream, self.a_out = u_stream, a_out
        self.ps = m.ps("a", [P, 2, H])
        self.loaded = [m.sem(f"u_loaded{s}") for s in range(2)]
        self.hi_made, self.lo_made = m.sem("uhi_made"), m.sem("ulo_made")
        self.done = m.sem("a_done")
        self.gelu = m.sem("a_gelu", start=2)
        self.stored = [m.sem(f"a_stored{s}", start=1) for s in range(2)]


    def load(self, sync, tile0, n, slot, first=False):
        if not first:
            sync.wait_ge(self.lo_made, n - 1)
        sync.dma_start(self.raw[:, slot], self.u_stream[ds(n + tile0, 1)].rearrange("a p c n -> (a p) c n")
                       ).then_inc(self.loaded[slot], 16)

    def store(self, sync, tile0, n, slot):
        sync.wait_ge(self.gelu, n * 2 + 4)
        sync.dma_start(self.a_out[ds(n + tile0, 1)].rearrange("a p t -> (a p) t"), self.out[:, slot]
                       ).then_inc(self.stored[slot], 16)

    def split_high(self, act, n, m, slot, first=False):
        act.wait_ge(self.loaded[slot], m * 16 + 16)
        if not first:
            act.wait_ge(self.done, n * 2 - 2)
        self.nc.scalar.activation(self.hi[:, slot], self.raw[:, slot], ACT.Copy).then_inc(self.hi_made, 1)

    def split_low(self, pool, n, slot):
        pool.wait_ge(self.hi_made, n + 1)
        self.nc.gpsimd.tensor_tensor(self.lo[:, slot], self.raw[:, slot], self.hi[:, slot].bitcast(F32), ALU.subtract
                                     ).then_inc(self.lo_made, 1)

    def product(self, pe, n, slot):
        pe.wait_ge(self.hi_made, n + 1)
        pe.wait_ge(self.lo_made, n + 1)
        for h in range(2):
            pe.wait_ge(self.gelu, n * 2 + (h + 1))
            mm = three_pass(self.nc, self.ps[:, h], [(self.hi[:, slot, k], self.lo[:, slot, k],
                                                      self.hhi[:, k, h * H:h * H + H], self.hlo[:, k, h * H:h * H + H])
                                                     for k in range(NC)])
            mm.then_inc(self.done, 1)

    def activate(self, act, n, m, slot):
        act.wait_ge(self.stored[slot], m * 16 + 1)
        for h in range(2):
            act.wait_ge(self.done, n * 2 + (h + 1))
            self.nc.scalar.activation(self.out[:, slot, h * H:h * H + H], self.ps[:, h], ACT.Gelu_apprx_tanh
                                      ).then_inc(self.gelu, 1)

    def finish(self, sync, n):
        for s in range(2):
            sync.wait_ge(self.stored[s], n // 2 * 16 + 1)


def select_phase(nc, ex, x_in, gain, keysT, wstream, u_stream, a_out, sel_out):
    with Phase(nc, "select") as m:
        K = TOPK
        xT = m.sb("xT", [P, NC, T])
        room = xT[:].rearrange("p c t -> p (c t)")
        sc = room[:, 0:2048].rearrange("p (c t n) -> p c t n", c=2, t=NT)
        sc2 = room[:, 2048:4096].rearrange("p (c t n) -> p c t n", c=2, t=NT)
        cand = room[:, 4096:6144].rearrange("p (t n) -> p t n", t=NT)
        cand2 = room[:, 6144:8192].rearrange("p (t n) -> p t n", t=NT)
        sq = ex.out
        norm = Rsqrt(m, "norm", T)
        g_sb = m.sb("gain", [P, NC])
        ones, ident = m.sb("ones", [P, P]), m.sb("ident", [P, P])
        keys = m.sb("keys", [P, 2, KEYS])
        w_raw = m.sb("wraw", [P, 2, NC, P])
        w_hi, w_lo = m.sb("whi", [P, 2, NC, P], F32R), m.sb("wlo", [P, 2, NC, P], F32R)
        qT = m.sb("qT", [P, 2, T])
        top = m.sb("top", [P, 2, NT, K])
        idx = m.sb("idx", [P, 2, NT, K], U32)
        idxf = m.sb("idxf", [P, 2, NT, K])
        best = m.sb("best", [P, NT, K])
        bidx = m.sb("bidx", [P, NT, K], U32)
        part = m.sb("part", [P, 2, NT, K], U32)
        partf = m.sb("partf", [P, 2, NT, K])
        iota16 = m.sb("iota16", [P, K])
        hit = m.sb("hit", [P, NT, K, K])
        shifted = m.sb("shifted", [P, NT, K])
        expv = m.sb("expv", [P, NT, K])
        total, inv = m.sb("total", [P, NT]), m.sb("inv", [P, NT])
        res = m.sb("res", [P, 3, NT, PH, K])
        resT = room[:, 0:3 * T].rearrange("p (r t) -> p r t", r=3)

        gemm = m.ps("gemm", [P, 2, H])
        scps = m.ps("scps", [P, 2, NT, KEYS])

        x_loaded = [m.sem(f"x_loaded{i}") for i in range(4)]
        c_loaded = m.sem("c_loaded")
        made = m.sem("made")
        squares = SumSquares(m, sq, norm.inv, gemm)
        h_made, hhi_made, hlo_made = m.sem("h_made"), m.sem("hhi_made"), m.sem("hlo_made")
        w_loaded = [m.sem(f"w_loaded{c}") for c in range(2)]
        whi_made, wlo_made = m.sem("whi_made"), m.sem("wlo_made")
        group_done = m.sem("group_done")
        evicted = [m.sem(f"evicted{b}") for b in range(2)]
        scored = m.sem("scored", start=1)
        sc_made = m.sem("sc_made", start=1)
        first8, index8, cut8, last8 = [m.sem(n) for n in ("first8", "index8", "cut8", "last8")]
        index16 = m.sem("index16", start=1)
        idxf_made = m.sem("idxf_made")
        cand_made = m.sem("cand_made")
        cfirst8, cindex8, ccut8, clast8, cindex16 = [m.sem(n) for n in ("cfirst8", "cindex8", "ccut8", "clast8", "cindex16")]
        part_made, partf_made = m.sem("part_made"), m.sem("partf_made")
        hit_step = m.sem("hit_step")
        shift_made, exp_made, gate_step = m.sem("shift_made"), m.sem("exp_made"), m.sem("gate_step")
        hit_summed = m.sem("hit_summed", start=1)
        gate_made = m.sem("gate_made", start=1)
        turn_done, turn_read = m.sem("turn_done"), m.sem("turn_read")
        held = m.sem("held")
        stored = m.sem("stored")
        ex.begin(m, u_stream, a_out)
        NX = SELECT_TILES // PH
        block = m.block()

        def heads(eng, body):
            body(0, True, False)
            with eng.Fori(1, PH - 1) as hd:
                body(hd, False, False)
            body(PH - 1, False, True)

        @block.sync
        def _(sync):
            for i in range(4):
                sync.dma_start(xT[:, 2 * i:2 * i + 2, :], x_in[:, 2 * i:2 * i + 2, :]).then_inc(x_loaded[i], 16)
            sync.dma_start(g_sb[:], gain).then_inc(c_loaded, 16)
            sync.dma_start(keys[:], keysT).then_inc(c_loaded, 16)
            for c in range(2):
                sync.dma_start(w_raw[:, c], wstream[c]).then_inc(w_loaded[c], 16)
            for s in range(2):
                ex.load(sync, 0, s, s, first=True)

            def body(hd, first, last):
                for i in range(NX):
                    if i in (0, 1) and not last:
                        sync.wait_ge(wlo_made, hd * 2 + (i + 1))
                        sync.dma_start(w_raw[:, i], wstream[ds(hd * 2 + (2 + i), 1)].rearrange("a p c n -> (a p) c n")
                                       ).then_inc(w_loaded[i], 16)
                    if not (last and i >= NX - 2):
                        ex.load(sync, 0, hd * NX + (i + 2), i % 2)
                    ex.store(sync, 0, hd * NX + i, i % 2)

            heads(sync, body)
            sync.wait_ge(turn_read, 6)
            sync.dma_start(sel_out, resT).then_inc(stored, 16)
            ex.finish(sync, SELECT_TILES)
            sync.wait_ge(stored, 16)

        @block.gpsimd
        def _(pool):
            nc.gpsimd.memset(ones[:], 1.0).then_inc(made, 1)
            nc.gpsimd.iota(iota16[:], pattern=[[1, K]], base=0, channel_multiplier=0,
                           allow_small_or_imprecise_dtypes=True).then_inc(made, 1)
            pool.wait_ge(made, 2)
            nc.gpsimd.affine_select(out=ident[:], in_=ones[:], pattern=[[-1, P]], compare_op=ALU.is_equal, fill=0.0,
                                    base=0, channel_multiplier=1).then_inc(made, 1)

            def weights(n, c):
                pool.wait_ge(whi_made, n + 1)
                nc.gpsimd.tensor_tensor(w_lo[:, c], w_raw[:, c], w_hi[:, c].bitcast(F32), ALU.subtract).then_inc(wlo_made, 1)

            for c in range(2):
                weights(c, c)
            for s in range(2):
                ex.split_low(pool, s, s)

            def body(hd, first, last):
                for i in range(NX):
                    if i in (2, 3) and not last:
                        weights(hd * 2 + i, i - 2)
                    if not (last and i >= NX - 2):
                        ex.split_low(pool, hd * NX + (i + 2), i % 2)

            heads(pool, body)

        @block.tensor
        def _(pe):
            pe.wait_ge(made, 3)
            squares.sum(nc, pe, ones[:])
            pe.wait_ge(c_loaded, 32)

            def queries(hd, c, first):
                pe.wait_ge(wlo_made, hd * 2 + (c + 1))
                for h in range(2):
                    pe.wait_ge(evicted[h], hd * 2 + (c + 1))
                    hs = slice(h * H, h * H + H)
                    for k in range(NC):
                        if first and h == 0:
                            pe.wait_ge(hlo_made, k + 1)
                        mm = three_pass(nc, gemm[:, h], [(w_hi[:, c, k], w_lo[:, c, k], ex.hhi[:, k, hs], ex.hlo[:, k, hs])],
                                        first=(k == 0), last=(k == NC - 1))
                    mm.then_inc(group_done, 1)

            def scores(hd, c):
                pe.wait_ge(evicted[1], hd * 2 + (c + 2))
                pe.wait_ge(evicted[0], hd * 2 + (c + 2))
                pe.wait_ge(sc_made, hd * 2 + 1)
                for t in range(NT):
                    mm = nc.tensor.matmul(scps[:, c, t], qT[:, c, t * P:t * P + P], keys[:, c], start=True, stop=True)
                mm.then_inc(scored, 1)

            def body(hd, first, last):
                for i in range(NX):
                    if i == 0:
                        queries(hd, 0, first)
                        queries(hd, 1, False)
                    if i == 1:
                        scores(hd, 0)
                        scores(hd, 1)
                    ex.product(pe, hd * NX + i, i % 2)

            heads(pe, body)
            pe.wait_ge(gate_made, PH + 1)
            pe.wait_ge(hit_summed, 2 * PH + 1)
            for g in range(6):
                r, b = g // 2, g % 2
                if g >= 2:
                    pe.wait_ge(turn_read, g - 1)
                for x in range(4):
                    mm = nc.tensor.transpose(gemm[:, b, x * P:x * P + P],
                                             res[:, r, 4 * (g % 2) + x].rearrange("p h k -> p (h k)"), ident[:])
                mm.then_inc(turn_done, 1)

        @block.scalar
        def _(act):
            nc.scalar.preload_act_table_set("natural_log_exp_and_others")
            for k in range(NC):
                act.wait_ge(x_loaded[k // 2], 16)
                squares.square(nc, act, k, xT[:, k])
            for c in range(2):
                act.wait_ge(w_loaded[c], 16)
                nc.scalar.activation(w_hi[:, c], w_raw[:, c], ACT.Copy).then_inc(whi_made, 1)
            norm.root(nc, act)
            for k in range(NC):
                act.wait_ge(h_made, k + 1)
                nc.scalar.activation(ex.hhi[:, k], xT[:, k], ACT.Copy).then_inc(hhi_made, 1)
            for s in range(2):
                ex.split_high(act, s, 0, s, first=True)

            def body(hd, first, last):
                for i in range(NX):
                    if i == 0:
                        for g in range(4):
                            c, h = g // 2, g % 2
                            act.wait_ge(group_done, hd * 4 + (g + 1))
                            act.wait_ge(scored, hd * 2 + 1)
                            nc.scalar.activation(qT[:, c, h * H:h * H + H], gemm[:, h], ACT.Copy).then_inc(evicted[h], 1)
                    if i == 1:
                        if not first:
                            act.wait_ge(shift_made, hd)
                            nc.scalar.activation(expv[:], shifted[:], ACT.Exp).then_inc(exp_made, 1)
                        for c in range(2):
                            act.wait_ge(scored, hd * 2 + (c + 2))
                            act.wait_ge(index16, hd * 16 + 1)
                            nc.scalar.activation(sc[:, c], scps[:, c], ACT.Copy).then_inc(sc_made, 1)
                        if not last:
                            for c in range(2):
                                act.wait_ge(w_loaded[c], hd * 16 + 32)
                                nc.scalar.activation(w_hi[:, c], w_raw[:, c], ACT.Copy).then_inc(whi_made, 1)
                    ex.activate(act, hd * NX + i, hd * (NX // 2) + i // 2, i % 2)
                    if not (last and i >= NX - 2):
                        ex.split_high(act, hd * NX + (i + 2), hd * (NX // 2) + (i // 2 + 1), i % 2)

            act.wait_ge(hlo_made, NC)
            heads(act, body)
            act.wait_ge(shift_made, PH)
            nc.scalar.activation(expv[:], shifted[:], ACT.Exp).then_inc(exp_made, 1)
            act.wait_ge(index16, PH * 16 + 1)
            for g in range(6):
                act.wait_ge(turn_done, g + 1)
                nc.scalar.activation(resT[:, g // 2, (g % 2) * H:(g % 2) * H + H], gemm[:, g % 2], ACT.Copy).then_inc(turn_read, 1)

        def alone(dve, sem, value):
            dve.wait_ge(sem, value)
            dve.sem_inc(held, 1)

        @block.vector
        def _(dve):
            for k in range(NC):
                squares.add(nc, dve, k)
            dve.wait_ge(squares.done, 1)
            norm.start(nc, dve, [(slice(h * H, h * H + H), gemm[:, h]) for h in range(2)], lambda h: evicted[h])
            norm.finish(nc, dve)
            dve.wait_ge(norm.made, 1)
            dve.wait_ge(c_loaded, 32)

            def h_low(k):
                dve.wait_ge(hhi_made, k + 1)
                nc.vector.tensor_tensor(ex.hlo[:, k], xT[:, k], ex.hhi[:, k].bitcast(F32), ALU.subtract).then_inc(hlo_made, 1)

            for k in range(NC):
                nc.vector.scalar_tensor_tensor(out=xT[:, k], in0=xT[:, k], scalar=g_sb[:, k:k + 1], in1=norm.rstd[:],
                                               op0=ALU.mult, op1=ALU.mult).then_inc(h_made, 1)
                if k:
                    h_low(k - 1)
            h_low(NC - 1)
            units = [(c, t) for c in range(2) for t in range(NT)]
            NU = len(units)

            def gates(hd):
                dve.wait_ge(exp_made, hd + 1)
                nc.vector.tensor_reduce(total[:], expv[:], AX.X, ALU.add).then_inc(gate_step, 1)
                dve.wait_ge(gate_step, hd * 2 + 1)
                nc.vector.reciprocal(inv[:], total[:]).then_inc(gate_step, 1)
                dve.wait_ge(gate_step, hd * 2 + 2)
                nc.vector.tensor_tensor(res[:, 2, :, ds(hd, 1), :].rearrange("p t a k -> p t (a k)"), expv[:],
                                        inv[:].unsqueeze(2).to_broadcast([P, NT, K]), ALU.mult).then_inc(gate_made, 1)

            def body(hd, first, last):
                if not first:
                    gates(hd - 1)
                alone(dve, sc_made, hd * 2 + 3)
                for c, t in units:
                    nc.vector.max(top[:, c, t, 0:8], sc[:, c, t]).then_inc(first8, 1)
                alone(dve, first8, hd * NU + NU)
                for c, t in units:
                    nc.vector.max_index(idx[:, c, t, 0:8], top[:, c, t, 0:8], sc[:, c, t]).then_inc(index8, 1)
                    nc.vector.match_replace(sc2[:, c, t], top[:, c, t, 0:8], sc[:, c, t], LOWEST).then_inc(cut8, 1)
                alone(dve, cut8, hd * NU + NU)
                for c, t in units:
                    nc.vector.max(top[:, c, t, 8:16], sc2[:, c, t]).then_inc(last8, 1)
                alone(dve, last8, hd * NU + NU)
                for c, t in units:
                    nc.vector.max_index(idx[:, c, t, 8:16], top[:, c, t, 8:16], sc2[:, c, t]).then_inc(index16, 1)
                for t in range(NT):
                    nc.vector.tensor_tensor(cand[:, t].rearrange("p (a b) -> p a b", b=K),
                                            top[:, 0, t].unsqueeze(2).to_broadcast([P, K, K]),
                                            top[:, 1, t].unsqueeze(1).to_broadcast([P, K, K]), ALU.add).then_inc(cand_made, 1)
                dve.wait_ge(index8, hd * NU + NU)
                dve.wait_ge(index16, hd * NU + NU + 1)
                nc.vector.tensor_copy(idxf[:], idx[:]).then_inc(idxf_made, 1)
                alone(dve, cand_made, hd * NT + NT)
                for t in range(NT):
                    nc.vector.max(best[:, t, 0:8], cand[:, t]).then_inc(cfirst8, 1)
                alone(dve, cfirst8, hd * NT + NT)
                for t in range(NT):
                    nc.vector.max_index(bidx[:, t, 0:8], best[:, t, 0:8], cand[:, t]).then_inc(cindex8, 1)
                    nc.vector.match_replace(cand2[:, t], best[:, t, 0:8], cand[:, t], LOWEST).then_inc(ccut8, 1)
                alone(dve, ccut8, hd * NT + NT)
                for t in range(NT):
                    nc.vector.max(best[:, t, 8:16], cand2[:, t]).then_inc(clast8, 1)
                alone(dve, clast8, hd * NT + NT)
                for t in range(NT):
                    nc.vector.max_index(bidx[:, t, 8:16], best[:, t, 8:16], cand2[:, t]).then_inc(cindex16, 1)
                nc.vector.tensor_tensor(shifted[:], best[:], best[:, :, 0:1].to_broadcast([P, NT, K]), ALU.subtract
                                        ).then_inc(shift_made, 1)
                dve.wait_ge(cindex8, hd * NT + NT)
                dve.wait_ge(cindex16, hd * NT + NT)
                nc.vector.tensor_single_scalar(part[:, 0], bidx[:], 4, ALU.logical_shift_right).then_inc(part_made, 1)
                nc.vector.tensor_single_scalar(part[:, 1], bidx[:], K - 1, ALU.bitwise_and).then_inc(part_made, 1)
                dve.wait_ge(part_made, hd * 2 + 2)
                nc.vector.tensor_copy(partf[:], part[:]).then_inc(partf_made, 1)
                dve.wait_ge(partf_made, hd + 1)
                dve.wait_ge(idxf_made, hd + 1)
                for c in range(2):
                    dve.wait_ge(hit_summed, hd * 2 + c + 1)
                    nc.vector.tensor_tensor(hit[:], partf[:, c].unsqueeze(3).to_broadcast([P, NT, K, K]),
                                            iota16[:].unsqueeze(1).unsqueeze(1).to_broadcast([P, NT, K, K]), ALU.is_equal
                                            ).then_inc(hit_step, 1)
                    dve.wait_ge(hit_step, hd * 4 + (2 * c + 1))
                    nc.vector.tensor_tensor(hit[:], hit[:], idxf[:, c].unsqueeze(2).to_broadcast([P, NT, K, K]), ALU.mult
                                            ).then_inc(hit_step, 1)
                    dve.wait_ge(hit_step, hd * 4 + (2 * c + 2))
                    nc.vector.tensor_reduce(res[:, c, :, ds(hd, 1), :].rearrange("p t a k -> p t (a k)"), hit[:], AX.X, ALU.add
                                            ).then_inc(hit_summed, 1)

            dve.wait_ge(made, 3)
            heads(dve, body)
            gates(PH - 1)


def spread_phase(nc, ex, sel_in, u_stream, a_out, g_out):
    with Phase(nc, "spread") as m:
        B = 16
        NB = B // 4
        STEPS = P // B
        PER = (KEYS - SELECT_TILES) // NT
        EXTRA = PER - STEPS
        NS = EXTRA
        parts = m.sb("parts", [P, 5, T], BF16)
        iota = m.sb("iota", [P, KEYS], BF16)
        eq = m.sb("eq", [P, B, KEYS], BF16)
        one1 = m.sb("one1", [P, 2, B, KEYS], BF16)
        gate = m.sb("gate", [P, 3, 2, B, KEYS], BF16)
        stage = m.sb("stage", [P, KEYS, P])
        sel = stage[:, 0:3 * NT, :].rearrange("p (r t) n -> p r (t n)", r=3)
        ps = m.ps("g", [P, NB, 4, KEYS])

        loaded = m.sem("loaded")
        iota_made = m.sem("iota_made")
        part_made, rest_made = m.sem("part_made"), m.sem("rest_made")
        eq_made = m.sem("eq_made")
        one1_made = m.sem("one1_made")
        dve_gated, pool_gated = m.sem("dve_gated", start=4), m.sem("pool_gated", start=2)
        g_done = m.sem("g_done", start=2 * NB)
        staged = m.sem("staged", start=NB)
        stored = m.sem("stored", start=1)
        ex.begin(m, u_stream, a_out)
        block = m.block()

        def tiles(eng, step, extra):
            def tile(tt, last):
                with eng.Fori(0, STEPS // 2) as ss:
                    for b in range(2):
                        step(tt * STEPS + (ss * 2 + b), tt * PER + (ss * 2 + b), tt * (PER // 2) + ss, b, tt, ss * 2 + b)
                for i in range(EXTRA):
                    extra(i, tt, tt * PER + (STEPS + i), tt * (PER // 2) + (STEPS + i) // 2, i % 2,
                          EXTRA - 1 - i if last else EXTRA)

            with eng.Fori(0, NT - 1) as tt:
                tile(tt, False)
            tile(NT - 1, True)

        @block.sync
        def _(sync):
            for s in range(2):
                ex.load(sync, SELECT_TILES, s, s, first=True)
            sync.dma_start(sel, sel_in).then_inc(loaded, 16)

            def step(n, tile, half, b, tt, st):
                ex.load(sync, SELECT_TILES, tile + 2, b)
                ex.store(sync, SELECT_TILES, tile, b)

            def extra(i, tt, tile, half, b, left):
                if left >= 2:
                    ex.load(sync, SELECT_TILES, tile + 2, b)
                sync.wait_ge(staged, tt * (STEPS * NB) + (STEPS * NB + NB))
                part = slice(i * KEYS // NS, (i + 1) * KEYS // NS)
                sync.dma_start(g_out[part].rearrange("a p t -> p a t")[:, :, ds(tt * P, P)], stage[:, part, :]
                               ).then_inc(stored, 16)
                ex.store(sync, SELECT_TILES, tile, b)

            tiles(sync, step, extra)
            ex.finish(sync, KEYS - SELECT_TILES)
            sync.wait_ge(stored, 16 * NS * NT + 1)

        @block.gpsimd
        def _(pool):
            nc.gpsimd.iota(iota[:], pattern=[[1, KEYS]], base=0, channel_multiplier=0,
                           allow_small_or_imprecise_dtypes=True).then_inc(iota_made, 1)
            ex.split_low(pool, 0, 0)
            pool.wait_ge(part_made, 5)

            def step(n, tile, half, b, tt, st):
                pool.wait_ge(eq_made, n + 1)
                pool.wait_ge(g_done, n * NB + NB)
                nc.gpsimd.tensor_tensor(gate[:, 2, b], eq[:], parts[:, 4, ds(n * B, B)].unsqueeze(2).to_broadcast([P, B, KEYS]),
                                        ALU.mult).then_inc(pool_gated, 1)
                ex.split_low(pool, tile + 1, 1 - b)

            def extra(i, tt, tile, half, b, left):
                if left >= 1:
                    ex.split_low(pool, tile + 1, 1 - b)

            tiles(pool, step, extra)

        @block.vector
        def _(dve):
            for i in range(2):
                dve.wait_ge(part_made, 3 + i)
                nc.vector.tensor_tensor(sel[:, 2], sel[:, 2], parts[:, 2 + i], ALU.subtract).then_inc(rest_made, 1)
            dve.wait_ge(part_made, 5)
            dve.wait_ge(iota_made, 1)

            def one_hot(dst, row, n):
                return nc.vector.tensor_tensor(dst, iota[:].unsqueeze(1).to_broadcast([P, B, KEYS]),
                                               parts[:, row, ds(n * B, B)].unsqueeze(2).to_broadcast([P, B, KEYS]),
                                               ALU.is_equal)

            def step(n, tile, half, b, tt, st):
                dve.wait_ge(g_done, n * NB + NB)
                one_hot(one1[:, b], 0, n).then_inc(one1_made, 1)
                dve.wait_ge(pool_gated, n + 2)
                dve.wait_ge(dve_gated, n * 2 + 4)
                one_hot(eq[:], 1, n).then_inc(eq_made, 1)
                dve.wait_ge(eq_made, n + 1)
                for i in range(2):
                    nc.vector.tensor_tensor(gate[:, i, b], eq[:],
                                            parts[:, 2 + i, ds(n * B, B)].unsqueeze(2).to_broadcast([P, B, KEYS]),
                                            ALU.mult).then_inc(dve_gated, 1)

            tiles(dve, step, lambda *a: None)

        @block.tensor
        def _(pe):
            def step(n, tile, half, b, tt, st):
                ex.product(pe, tile, b)
                pe.wait_ge(one1_made, n + 1)
                pe.wait_ge(dve_gated, n * 2 + 6)
                pe.wait_ge(pool_gated, n + 3)
                for bank in range(NB):
                    pe.wait_ge(staged, n * NB + (bank + 1))
                    for x in range(4):
                        t = 4 * bank + x
                        for i in range(3):
                            mm = nc.tensor.matmul(ps[:, bank, x], one1[:, b, t], gate[:, i, b, t], start=(i == 0), stop=(i == 2))
                    mm.then_inc(g_done, 1)

            tiles(pe, step, lambda i, tt, tile, half, b, left: ex.product(pe, tile, b))

        @block.scalar
        def _(act):
            for s in range(2):
                ex.split_high(act, s, 0, s, first=True)
            act.wait_ge(loaded, 16)
            for i in range(5):
                if i >= 3:
                    act.wait_ge(rest_made, i - 2)
                nc.scalar.activation(parts[:, i], sel[:, min(i, 2)], ACT.Copy).then_inc(part_made, 1)

            def step(n, tile, half, b, tt, st):
                ex.activate(act, tile, half, b)
                ex.split_high(act, tile + 2, half + 1, b)
                act.wait_ge(stored, tt * (16 * NS) + 1)
                for bank in range(NB):
                    act.wait_ge(g_done, n * NB + (2 * NB + bank + 1))
                    nc.scalar.activation(stage[:, :, ds(st * B + 4 * bank, 4)], ps[:, bank].rearrange("p t i -> p i t"), ACT.Copy
                                         ).then_inc(staged, 1)

            def extra(i, tt, tile, half, b, left):
                ex.activate(act, tile, half, b)
                if left >= 2:
                    ex.split_high(act, tile + 2, half + 1, b)

            tiles(act, step, extra)


def expert_phase(nc, a_in, x_in, g_in, v_stream, final_gain, out):
    with Phase(nc, "expert") as m:
        E = 4
        NG = KEYS // E
        NQ = 4
        QC = NC // NQ
        QG = 2 * QC
        SG = NQ * QG
        acc = m.sb("acc", [P, NC, T])
        g_sb = m.sb("gain", [P, NC])
        ones = m.sb("ones", [P, P])
        vraw = m.sb("vraw", [P, NQ, E, QC * P])
        vhi = m.sb("vhi", [P, NQ, E, QC * P], F32R)
        vlo = m.sb("vlo", [P, NQ, E, QC * P], F32R)
        graw = m.sb("graw", [P, E, T])
        act = m.sb("act", [P, E, T])
        ahi = m.sb("ahi", [P, 2, E, T], F32R)
        alo = m.sb("alo", [P, 2, E, T], F32R)
        ops = m.ps("o", [P, QC, 2, H])
        sums = m.ps("sums", [P, 2, H])

        x_loaded, c_loaded = m.sem("x_loaded"), m.sem("c_loaded")
        ones_made = m.sem("ones_made")
        a_loaded = [m.sem(f"a_loaded{e}") for e in range(E)]
        g_loaded = [m.sem(f"g_loaded{e}") for e in range(E)]
        v_loaded = [m.sem(f"v_loaded{q}") for q in range(NQ)]
        vhi_made, vlo_made = m.sem("vhi_made"), m.sem("vlo_made")
        gated = m.sem("gated")
        ahi_made, alo_made = m.sem("ahi_made"), m.sem("alo_made")
        o_done = m.sem("o_done", start=2 * SG)
        added = m.sem("added", start=QG)
        norm = Rsqrt(m, "norm", T, (graw[:, 0], act[:, 2], graw[:, 1]))
        squares = SumSquares(m, act[:, 0:2], act[:, 3], sums)
        sum_read = [m.sem(f"sum_read{h}") for h in range(2)]
        y_made, stored = m.sem("y_made"), m.sem("stored")
        block = m.block()

        def groups(eng, body):
            with eng.Fori(0, NG // 2) as gg:
                for par in range(2):
                    body(gg * 2 + par, par)

        @block.sync
        def _(sync):
            def load_tile(e, i, j):
                if j is not None:
                    sync.wait_ge(alo_made, j)
                sync.dma_start(act[:, e], a_in[i].rearrange("a p t -> (a p) t")).then_inc(a_loaded[e], 16)
                sync.dma_start(graw[:, e], g_in[i].rearrange("a p t -> (a p) t")).then_inc(g_loaded[e], 16)

            def load_values(q, i, j):
                if j is not None:
                    sync.wait_ge(vlo_made, j)
                sync.dma_start(vraw[:, q], v_stream[i, q].rearrange("a p e n -> (a p) e n")).then_inc(v_loaded[q], 16)

            for i in range(E):
                load_tile(i, ds(i, 1), None)
                load_values(i, ds(0, 1), None)
            sync.dma_start(acc[:], x_in).then_inc(x_loaded, 16)
            sync.dma_start(g_sb[:], final_gain).then_inc(c_loaded, 16)
            with sync.Fori(0, NG - 1) as g:
                for e in range(E):
                    load_tile(e, ds(g * E + (E + e), 1), g * E + (e + 1))
                for q in range(NQ):
                    load_values(q, ds(g + 1, 1), g * NQ + (q + 1))
            for k in range(NC):
                sync.wait_ge(y_made, k + 1)
                sync.dma_start(out[:, k], acc[:, k]).then_inc(stored, 16)
            sync.wait_ge(stored, 16 * NC)

        def split_low(eng, low, raw, high):
            return eng.tensor_tensor(low, raw, high.bitcast(F32), ALU.subtract)

        @block.gpsimd
        def _(pool):
            nc.gpsimd.memset(ones[:], 1.0).then_inc(ones_made, 1)

            def body(g, par):
                for q in range(NQ):
                    pool.wait_ge(vhi_made, g * NQ + (q + 1))
                    split_low(nc.gpsimd, vlo[:, q], vraw[:, q], vhi[:, q]).then_inc(vlo_made, 1)

            groups(pool, body)

        @block.scalar
        def _(act_eng):
            def values(g, q):
                act_eng.wait_ge(v_loaded[q], g * 16 + 16)
                act_eng.wait_ge(o_done, g * SG + (SG + (q + 1) * QG))
                nc.scalar.activation(vhi[:, q], vraw[:, q], ACT.Copy).then_inc(vhi_made, 1)

            def body(g, par):
                for e in range(E):
                    act_eng.wait_ge(gated, g * E + (e + 1))
                    act_eng.wait_ge(o_done, g * SG + SG)
                    nc.scalar.activation(ahi[:, par, e], act[:, e], ACT.Copy).then_inc(ahi_made, 1)
                    if e > 0:
                        values(g, e - 1)
                values(g, NQ - 1)

            groups(act_eng, body)
            nc.scalar.preload_act_table_set("natural_log_exp_and_others")
            act_eng.wait_ge(alo_made, NG * E)
            for k in range(NC):
                act_eng.wait_ge(added, QG + (NG - 1) * SG + (k + 1) * 2)
                squares.square(nc, act_eng, k, acc[:, k])
            norm.root(nc, act_eng)

        @block.vector
        def _(dve):
            def gate(g, par, e):
                dve.wait_ge(a_loaded[e], g * 16 + 16)
                dve.wait_ge(g_loaded[e], g * 16 + 16)
                nc.vector.tensor_tensor(act[:, e], act[:, e], graw[:, e], ALU.mult).then_inc(gated, 1)

            def split(g, par, e):
                dve.wait_ge(ahi_made, g * E + (e + 1))
                split_low(nc.vector, alo[:, par, e], act[:, e], ahi[:, par, e]).then_inc(alo_made, 1)

            def add(g, w):
                q, d, h = w // QG, w // 2 % QC, w % 2
                k = q * QC + d
                dve.wait_ge(o_done, g * SG + (2 * SG + w + 1))
                nc.vector.tensor_tensor(acc[:, k, h * H:h * H + H], acc[:, k, h * H:h * H + H], ops[:, d, h], ALU.add
                                        ).then_inc(added, 1)

            for e in range(E):
                gate(0, 0, e)
                split(0, 0, e)
            dve.wait_ge(x_loaded, 16)

            def body(g, par, last=False):
                for w in range(SG):
                    add(g, w)
                    if last and w % 2 and w > 1:
                        squares.add(nc, dve, w // 2 - 1)
                    if not last and w % 3 == 0 and w // 3 < E:
                        gate(g + 1, 1 - par, w // 3)
                    if not last and w % 3 == 2 and w // 3 < E:
                        split(g + 1, 1 - par, w // 3)

            with dve.Fori(0, NG // 2 - 1) as gg:
                for par in range(2):
                    body(gg * 2 + par, par)
            body(NG - 2, 0)
            body(NG - 1, 1, last=True)
            squares.add(nc, dve, NC - 1)
            dve.wait_ge(squares.done, 1)
            norm.start(nc, dve, [(slice(h * H, h * H + H), sums[:, h]) for h in range(2)], lambda h: sum_read[h])
            norm.finish(nc, dve)
            dve.wait_ge(norm.made, 1)
            dve.wait_ge(c_loaded, 16)
            for k in range(NC):
                nc.vector.scalar_tensor_tensor(out=acc[:, k], in0=acc[:, k], scalar=g_sb[:, k:k + 1], in1=norm.rstd,
                                               op0=ALU.mult, op1=ALU.mult).then_inc(y_made, 1)

        @block.tensor
        def _(pe):
            def body(g, par):
                for w in range(SG):
                    q, d, h = w // QG, w // 2 % QC, w % 2
                    if w % QG == 0:
                        pe.wait_ge(vhi_made, g * NQ + (q + 1))
                        pe.wait_ge(vlo_made, g * NQ + (q + 1))
                    pe.wait_ge(added, g * SG + (w + 1))
                    hs, dp = slice(h * H, h * H + H), slice(d * P, d * P + P)
                    for e in range(E):
                        if w == 0:
                            pe.wait_ge(ahi_made, g * E + (e + 1))
                            pe.wait_ge(alo_made, g * E + (e + 1))
                        mm = three_pass(nc, ops[:, d, h], [(vhi[:, q, e, dp], vlo[:, q, e, dp], ahi[:, par, e, hs], alo[:, par, e, hs])],
                                        first=(e == 0), last=(e == E - 1))
                    mm.then_inc(o_done, 1)

            groups(pe, body)
            pe.wait_ge(ones_made, 1)
            squares.sum(nc, pe, ones[:])


def build(nc, a, out):
    def scratch(name, shape):
        return nc.dram_tensor(name, shape, F32).ap()

    full = [P, NC, T]
    conv, attn, half, logits = scratch("conv", full), scratch("attn", full), scratch("half", full), scratch("logits", [P, 2, NC, T])
    x1, x2, sel = scratch("x1", full), scratch("x2", full), scratch("sel", [P, 3, T])
    gelu_u, gates = scratch("gelu_u", [KEYS, P, T]), scratch("gates", [KEYS, P, T])
    mixer_phase(nc, a["x"], a["mix_gain"], a["w_mix"], a["conv_w"], conv, attn, logits)
    merge_phase(nc, a["x"], conv, attn, logits.rearrange("p b c t -> p (b c) t"), a["w_merge"], a["ln_g"], a["ln_b"],
                a["gate_b"], half, x1)
    cross_attention_phase(nc, x1, a["x_gain"], a["mem"], a["mem_gain"], a["w_cross"], x2)
    with ExitStack() as tensors:
        experts = Experts1(nc, tensors)
        select_phase(nc, experts, x2, a["ffn_gain"], a["keys"], a["w_query"], a["peer_u"], gelu_u, sel)
        spread_phase(nc, experts, sel, a["peer_u"], gelu_u, gates)
    expert_phase(nc, gelu_u, x2, gates, a["peer_v"], a["final_gain"], out)


def kernel(x, mem, norm_mix_g, w_in, b_gate, conv_dw_w, conv_dw_b, conv_ln_g, conv_ln_b,
           w_conv_out, w_attn_out, w_out, norm_xattn_g, norm_mem_g, w_xq, w_xkv, w_xo,
           norm_ffn_g, w_peer_q, peer_sub_keys, peer_u, peer_v, norm_final_g):
    import concourse.bacc as bacc
    from concourse.bass_utils import run_bass_kernel_spmd

    def channels(t):
        return t.T.reshape(NC, P, -1).transpose(1, 0, 2)

    def vector(t):
        return t.reshape(-1, P).T

    def chunks(w):
        return w.reshape(NC, P, -1, P).transpose(2, 1, 0, 3)

    w = np.asarray(w_in)[0]
    val, gate, q, k, v, g_conv, g_attn = [chunks(w[:, i * D:(i + 1) * D]) for i in range(7)]
    arrays = {
        "x": channels(np.asarray(x)[0]),
        "mem": channels(np.asarray(mem)[0]),
        "mix_gain": vector(np.asarray(norm_mix_g)[0]),
        "w_mix": np.stack([gate, val, q, k, v, g_attn, g_conv], 1).reshape(-1, P, NC, P),
        "conv_w": np.concatenate([np.asarray(conv_dw_w)[0], np.asarray(conv_dw_b)]).T.reshape(NC, P, TAPS + 1).transpose(1, 0, 2),
        "w_merge": np.concatenate([chunks(np.asarray(t)[0]) for t in (w_attn_out, w_conv_out, w_out)]),
        "ln_g": vector(np.asarray(conv_ln_g)[0]),
        "ln_b": vector(np.asarray(conv_ln_b)[0]),
        "gate_b": np.asarray(b_gate)[0].reshape(2, NC * P)[::-1].reshape(2 * NC, P).T,
        "x_gain": vector(np.asarray(norm_xattn_g)[0]),
        "mem_gain": vector(np.asarray(norm_mem_g)[0]),
        "w_cross": np.concatenate([chunks(np.asarray(t)[0]) for t in (w_xkv, w_xq, w_xo)]),
        "ffn_gain": vector(np.asarray(norm_ffn_g)[0]),
        "w_query": chunks(np.asarray(w_peer_q)[0]),
        "keys": np.asarray(peer_sub_keys)[0].transpose(2, 0, 1),
        "peer_u": np.asarray(peer_u)[0].reshape(P, KEYS, NC, P).transpose(1, 3, 2, 0),
        "peer_v": np.asarray(peer_v)[0].reshape(P, KEYS // 4, 4, 4, D // 4).transpose(1, 3, 0, 2, 4),
        "final_gain": vector(np.asarray(norm_final_g)),
    }
    arrays = {f"in_{n}": np.ascontiguousarray(t) for n, t in arrays.items()}
    nc = bacc.Bacc("TRN2", target_bir_lowering=False, num_devices=1)
    aps = {n: nc.dram_tensor(n, list(t.shape), F32, kind="ExternalInput").ap() for n, t in arrays.items()}
    out = nc.dram_tensor("out", [P, NC, T], F32, kind="ExternalOutput").ap()
    build(nc, {n[3:]: ap for n, ap in aps.items()}, out)
    r = run_bass_kernel_spmd(nc, [arrays], core_ids=[0])
    got = r.results[0]["out"]
    return np.ascontiguousarray(got.transpose(1, 0, 2).reshape(D, T).T)[None]
```
